# Optimizing a Trainium2 kernel written in Bass

```python
import jax, jax.numpy as jnp
from jax import lax
import numpy as np

D_MODEL = 1024
BATCH = 1
SEQ = 256
DEPTH = 1

MIX_WIDTH = D_MODEL
HEAD_DIM = 64
ATTN_WIDTH = MIX_WIDTH // 2
N_Q_HEADS = ATTN_WIDTH // HEAD_DIM
N_KV_HEADS = 2
KV_GROUP = N_Q_HEADS // N_KV_HEADS
KV_WIDTH = N_KV_HEADS * HEAD_DIM
WINDOW = 128
ATTN_BLOCK = 128
LRU_WIDTH = MIX_WIDTH - ATTN_WIDTH
LRU_BLOCKS = 8
LRU_BLOCK_W = LRU_WIDTH // LRU_BLOCKS
CONV_WIDTH = 4
LRU_C = 8.0
IN_SPLITS = [ATTN_WIDTH, ATTN_WIDTH + KV_WIDTH, ATTN_WIDTH + 2 * KV_WIDTH, ATTN_WIDTH + 2 * KV_WIDTH + LRU_WIDTH]
IN_COLS = ATTN_WIDTH + 2 * KV_WIDTH + 2 * LRU_WIDTH
N_EXPERTS = 32
TOP_K = 4
D_EXPERT = D_MODEL
SWIGLU_LIMIT = 7.0
SWIGLU_ALPHA = 1.702
MOE_BLOCK = 256
EPS = 1e-6


def rms_norm(x, g):
    xf = x.astype(jnp.float32)
    y = xf * lax.rsqrt(jnp.mean(xf * xf, axis=-1, keepdims=True) + EPS)
    return (y * g.astype(jnp.float32)).astype(x.dtype)

def causal_depthwise_conv(x, w, b):
    y = lax.conv_general_dilated(
        x, w[:, None, :].astype(x.dtype), window_strides=(1,),
        padding=[(CONV_WIDTH - 1, 0)], dimension_numbers=("NWC", "WIO", "NWC"),
        feature_group_count=x.shape[-1])
    return y + b

def rg_lru(x, w_a, b_a, w_x, b_x, lam):
    B, S, C = x.shape
    xf = x.astype(jnp.float32)
    xh = xf.reshape(B, S, LRU_BLOCKS, LRU_BLOCK_W)
    r = jax.nn.sigmoid(jnp.einsum("bshi,hij->bshj", xh, w_a.astype(jnp.float32)) + b_a).reshape(B, S, C)
    i = jax.nn.sigmoid(jnp.einsum("bshi,hij->bshj", xh, w_x.astype(jnp.float32)) + b_x).reshape(B, S, C)
    log_a = LRU_C * r * jax.nn.log_sigmoid(lam.astype(jnp.float32))
    a = jnp.exp(log_a)
    mult = jnp.sqrt(jnp.maximum(-jnp.expm1(2.0 * log_a), 0.0))
    u = mult * (i * xf)

    def combine(left, right):
        a1, b1 = left
        a2, b2 = right
        return a1 * a2, a2 * b1 + b2

    _, h = lax.associative_scan(combine, (a, u), axis=1)
    return h.astype(x.dtype)

def sliding_window_sink_attention(q, k, v, sinks):
    B, S = q.shape[0], q.shape[1]
    nblk = S // ATTN_BLOCK
    qb = q.reshape(B, nblk, ATTN_BLOCK, N_KV_HEADS, KV_GROUP, HEAD_DIM)

    def band(t):
        tp = jnp.pad(t, ((0, 0), (ATTN_BLOCK, 0), (0, 0), (0, 0)))
        prev = tp[:, :S].reshape(B, nblk, ATTN_BLOCK, N_KV_HEADS, HEAD_DIM)
        cur = t.reshape(B, nblk, ATTN_BLOCK, N_KV_HEADS, HEAD_DIM)
        return jnp.concatenate([prev, cur], axis=2)

    kw, vw = band(k), band(v)
    scores = jnp.einsum("bnqkgd,bnskd->bnkgqs", qb, kw).astype(jnp.float32) * (HEAD_DIM ** -0.5)
    qi = jnp.arange(ATTN_BLOCK)[:, None]
    sj = jnp.arange(2 * ATTN_BLOCK)[None, :]
    rel = qi + ATTN_BLOCK - sj
    key_pos = jnp.arange(nblk)[:, None, None] * ATTN_BLOCK - ATTN_BLOCK + sj[None]
    mask = ((rel >= 0) & (rel < WINDOW))[None] & (key_pos >= 0)
    scores = jnp.where(mask[None, :, None, None], scores, jnp.finfo(jnp.float32).min)
    sink = jnp.broadcast_to(sinks.astype(jnp.float32).reshape(1, 1, N_KV_HEADS, KV_GROUP, 1, 1),
                            scores.shape[:-1] + (1,))
    probs = jax.nn.softmax(jnp.concatenate([scores, sink], axis=-1), axis=-1)[..., :-1]
    out = jnp.einsum("bnkgqs,bnskd->bnqkgd", probs.astype(v.dtype), vw)
    return out.reshape(B, S, N_Q_HEADS * HEAD_DIM)

def parallel_mixer(h, w_in, conv_w, conv_b, w_rg_a, b_rg_a, w_rg_x, b_rg_x, lru_lambda,
                   sinks, g_attn_out, g_lru_out, w_out):
    B, S, _ = h.shape
    p = h @ w_in
    q, k, v, xr, xg = jnp.split(p, IN_SPLITS, axis=-1)
    attn = sliding_window_sink_attention(
        q.reshape(B, S, N_Q_HEADS, HEAD_DIM), k.reshape(B, S, N_KV_HEADS, HEAD_DIM),
        v.reshape(B, S, N_KV_HEADS, HEAD_DIM), sinks)
    xc = causal_depthwise_conv(xr, conv_w, conv_b)
    lru = rg_lru(xc, w_rg_a, b_rg_a, w_rg_x, b_rg_x, lru_lambda) * jax.nn.gelu(xg)
    merged = jnp.concatenate([rms_norm(attn, g_attn_out), rms_norm(lru, g_lru_out)], axis=-1)
    return merged @ w_out

def moe_ffn(h, w_router, b_router, w_gu, b_gu, w_down, b_down):
    B, S, D = h.shape
    T = B * S
    A = T * TOP_K
    R = ((A + N_EXPERTS * (MOE_BLOCK - 1) + MOE_BLOCK - 1) // MOE_BLOCK) * MOE_BLOCK
    nb = R // MOE_BLOCK
    hf = h.reshape(T, D)
    logits = (hf @ w_router + b_router).astype(jnp.float32)
    top_vals, top_idx = lax.top_k(logits, TOP_K)
    gates = jax.nn.softmax(top_vals, axis=-1)
    flat_e = top_idx.reshape(A).astype(jnp.int32)
    flat_tok = jnp.repeat(jnp.arange(T, dtype=jnp.int32), TOP_K)
    flat_w = gates.reshape(A)
    order = jnp.argsort(flat_e)
    se = flat_e[order]
    sizes = jnp.bincount(flat_e, length=N_EXPERTS)
    padded = ((sizes + MOE_BLOCK - 1) // MOE_BLOCK) * MOE_BLOCK
    pad_end = jnp.cumsum(padded)
    pad_start = pad_end - padded
    start = jnp.cumsum(sizes) - sizes
    dest = pad_start[se] + (jnp.arange(A, dtype=jnp.int32) - start[se])
    row_tok = jnp.zeros((R,), jnp.int32).at[dest].set(flat_tok[order])
    row_w = jnp.zeros((R,), jnp.float32).at[dest].set(flat_w[order])
    blk_e = jnp.minimum(jnp.searchsorted(pad_end, jnp.arange(nb) * MOE_BLOCK, side="right"),
                        N_EXPERTS - 1).astype(jnp.int32)
    xs = hf[row_tok].reshape(nb, MOE_BLOCK, D)

    def expert_block(args):
        xb, e = args
        gu = xb @ w_gu[e] + b_gu[e]
        gate = jnp.minimum(gu[:, :D_EXPERT], SWIGLU_LIMIT)
        up = jnp.clip(gu[:, D_EXPERT:], -SWIGLU_LIMIT, SWIGLU_LIMIT)
        glu = gate * jax.nn.sigmoid(SWIGLU_ALPHA * gate)
        return ((up + 1.0) * glu) @ w_down[e] + b_down[e]

    ys = lax.map(expert_block, (xs, blk_e)).reshape(R, D)
    ys = ys.astype(jnp.float32) * row_w[:, None]
    out = jax.ops.segment_sum(ys, row_tok, num_segments=T)
    return out.reshape(B, S, D).astype(h.dtype)

def first_inputs(seed: int = 0) -> dict:
    key = jax.random.key(seed)
    ks = jax.random.split(key, 26)
    L, D, E, F = DEPTH, D_MODEL, N_EXPERTS, D_EXPERT
    nrm = lambda k, shape, s: jax.random.normal(k, shape, jnp.float32) * s
    a0 = jax.random.uniform(ks[13], (L, LRU_WIDTH), jnp.float32, minval=0.9, maxval=0.999)
    root = a0 ** (1.0 / LRU_C)
    return {
        "x": nrm(ks[0], (BATCH, SEQ, D), 1.0),
        "c": nrm(ks[1], (BATCH, D), 1.0),
        "w_ada": nrm(ks[2], (L, D, 6 * D), 0.5 * D ** -0.5),
        "b_ada": nrm(ks[3], (L, 6 * D), 0.02),
        "g_mix": 1.0 + nrm(ks[4], (L, D), 0.05),
        "w_in": nrm(ks[5], (L, D, IN_COLS), D ** -0.5),
        "conv_w": nrm(ks[6], (L, CONV_WIDTH, LRU_WIDTH), CONV_WIDTH ** -0.5),
        "conv_b": nrm(ks[7], (L, LRU_WIDTH), 0.02),
        "w_rg_a": nrm(ks[8], (L, LRU_BLOCKS, LRU_BLOCK_W, LRU_BLOCK_W), LRU_BLOCK_W ** -0.5),
        "b_rg_a": nrm(ks[9], (L, LRU_BLOCKS, LRU_BLOCK_W), 0.02),
        "w_rg_x": nrm(ks[10], (L, LRU_BLOCKS, LRU_BLOCK_W, LRU_BLOCK_W), LRU_BLOCK_W ** -0.5),
        "b_rg_x": nrm(ks[11], (L, LRU_BLOCKS, LRU_BLOCK_W), 0.02),
        "lru_lambda": jnp.log(root) - jnp.log1p(-root),
        "sinks": nrm(ks[12], (L, N_Q_HEADS), 0.5),
        "g_attn_out": 1.0 + nrm(ks[14], (L, ATTN_WIDTH), 0.05),
        "g_lru_out": 1.0 + nrm(ks[15], (L, LRU_WIDTH), 0.05),
        "w_out": nrm(ks[16], (L, MIX_WIDTH, D), MIX_WIDTH ** -0.5),
        "g_ffn": 1.0 + nrm(ks[17], (L, D), 0.05),
        "w_router": nrm(ks[18], (L, D, E), D ** -0.5),
        "b_router": nrm(ks[19], (L, E), 0.01),
        "w_gu": nrm(ks[20], (L, E, D, 2 * F), D ** -0.5),
        "b_gu": nrm(ks[21], (L, E, 2 * F), 0.02),
        "w_down": nrm(ks[22], (L, E, F, D), F ** -0.5),
        "b_down": nrm(ks[23], (L, E, D), 0.02),
        "g_final": 1.0 + nrm(ks[24], (D,), 0.05),
    }

def first_block(x, c, w_ada, b_ada, g_mix, w_in, conv_w, conv_b, w_rg_a, b_rg_a, w_rg_x, b_rg_x,
              lru_lambda, sinks, g_attn_out, g_lru_out, w_out, g_ffn, w_router, b_router,
              w_gu, b_gu, w_down, b_down, g_final):
    for l in range(DEPTH):
        mod = (c @ w_ada[l] + b_ada[l])[:, None, :]
        sh1, sc1, gt1, sh2, sc2, gt2 = jnp.split(mod, 6, axis=-1)
        h = rms_norm(x, g_mix[l]) * (1.0 + sc1) + sh1
        x = x + gt1 * parallel_mixer(h, w_in[l], conv_w[l], conv_b[l], w_rg_a[l], b_rg_a[l],
                                     w_rg_x[l], b_rg_x[l], lru_lambda[l], sinks[l],
                                     g_attn_out[l], g_lru_out[l], w_out[l])
        h = rms_norm(x, g_ffn[l]) * (1.0 + sc2) + sh2
        x = x + gt2 * moe_ffn(h, w_router[l], b_router[l], w_gu[l], b_gu[l], w_down[l], b_down[l])
    return rms_norm(x, g_final)


DEPTH_2 = 2

GRID_W = 64
ROPE_THETA = 10000.0
Q_BLOCK = 128

MLA_HEADS = 8
MLA_Q_LORA = 256
MLA_KV_LORA = 128
MLA_NOPE = 64
MLA_ROPE = 32
MLA_V = 64
MLA_QK = MLA_NOPE + MLA_ROPE

GQA_HEADS = 8
GQA_KV_HEADS = 2
GQA_HEAD_DIM = 64

POOL_WINDOWS = (2, 4, 8, 16)
POOL_GROUPS = 4
POOL_GROUP = 128
POOL_WIDTH = POOL_GROUPS * POOL_GROUP

N_BRANCH = 3
MLA_OUT = MLA_HEADS * MLA_V
GQA_OUT = GQA_HEADS * GQA_HEAD_DIM

D_FF = 2816
CONV_W = 3

IN_SIZES = (MLA_Q_LORA, MLA_KV_LORA, MLA_ROPE,
            GQA_HEADS * GQA_HEAD_DIM, GQA_KV_HEADS * GQA_HEAD_DIM, GQA_KV_HEADS * GQA_HEAD_DIM,
            POOL_WIDTH, N_BRANCH * D_MODEL)
IN_WIDTH = (MLA_Q_LORA + MLA_KV_LORA + MLA_ROPE
            + (GQA_HEADS + 2 * GQA_KV_HEADS) * GQA_HEAD_DIM
            + POOL_WIDTH + N_BRANCH * D_MODEL)


def rms_norm_2(x, g):
    xf = x.astype(jnp.float32)
    y = xf * lax.rsqrt(jnp.mean(xf * xf, axis=-1, keepdims=True) + EPS)
    return (y * g.astype(jnp.float32)).astype(x.dtype)

def split_columns(y, sizes):
    out, start = [], 0
    for n in sizes:
        out.append(y[..., start:start + n])
        start += n
    return out

def axial_rope_tables(seq_len, rot_dim):
    rows = seq_len // GRID_W
    row_idx = jnp.repeat(jnp.arange(rows, dtype=jnp.float32), GRID_W)
    col_idx = jnp.tile(jnp.arange(GRID_W, dtype=jnp.float32), rows)
    n_axis = rot_dim // 4
    inv_freq = ROPE_THETA ** (-jnp.arange(n_axis, dtype=jnp.float32) / n_axis)
    ang = jnp.concatenate([row_idx[:, None] * inv_freq, col_idx[:, None] * inv_freq], axis=-1)
    return jnp.cos(ang), jnp.sin(ang)

def apply_rope(x, cos, sin):
    half = x.shape[-1] // 2
    x1, x2 = x[..., :half], x[..., half:]
    c = cos[None, :, None, :].astype(x.dtype)
    s = sin[None, :, None, :].astype(x.dtype)
    return jnp.concatenate([x1 * c - x2 * s, x1 * s + x2 * c], axis=-1)

def block_attention(q, k, v):
    b, s, h, dk = q.shape
    g = k.shape[2]
    rep = h // g
    dv = v.shape[-1]
    scale = dk ** -0.5
    nb = s // Q_BLOCK
    qb = q.reshape(b, nb, Q_BLOCK, g, rep, dk).transpose(1, 0, 2, 3, 4, 5)

    def one_block(qi):
        sc = jnp.einsum('bqgrd,bkgd->bgrqk', qi, k, preferred_element_type=jnp.float32) * scale
        p = jax.nn.softmax(sc, axis=-1).astype(v.dtype)
        return jnp.einsum('bgrqk,bkgv->bqgrv', p, v)

    out = lax.map(one_block, qb)
    return out.transpose(1, 0, 2, 3, 4, 5).reshape(b, s, h, dv)

def mla_branch(c_q, c_kv, k_rope_raw, q_norm_g, w_uq, kv_norm_g, w_ukv, qh_g, kh_g, cos, sin):
    b, s, _ = c_q.shape
    q = (rms_norm_2(c_q, q_norm_g) @ w_uq).reshape(b, s, MLA_HEADS, MLA_QK)
    kv = (rms_norm_2(c_kv, kv_norm_g) @ w_ukv).reshape(b, s, MLA_HEADS, MLA_NOPE + MLA_V)
    k_nope, v = kv[..., :MLA_NOPE], kv[..., MLA_NOPE:]
    k_rope = jnp.broadcast_to(k_rope_raw[:, :, None, :], (b, s, MLA_HEADS, MLA_ROPE))
    k = jnp.concatenate([k_nope, k_rope], axis=-1)
    q = rms_norm_2(q, qh_g)
    k = rms_norm_2(k, kh_g)
    q = jnp.concatenate([q[..., :MLA_NOPE], apply_rope(q[..., MLA_NOPE:], cos, sin)], axis=-1)
    k = jnp.concatenate([k[..., :MLA_NOPE], apply_rope(k[..., MLA_NOPE:], cos, sin)], axis=-1)
    o = block_attention(q, k, v)
    return o.reshape(b, s, MLA_OUT)

def gqa_branch(q_raw, k_raw, v_raw, qn_g, kn_g, cos, sin):
    b, s, _ = q_raw.shape
    q = q_raw.reshape(b, s, GQA_HEADS, GQA_HEAD_DIM)
    k = k_raw.reshape(b, s, GQA_KV_HEADS, GQA_HEAD_DIM)
    v = v_raw.reshape(b, s, GQA_KV_HEADS, GQA_HEAD_DIM)
    q = apply_rope(rms_norm_2(q, qn_g), cos, sin)
    k = apply_rope(rms_norm_2(k, kn_g), cos, sin)
    o = block_attention(q, k, v)
    return o.reshape(b, s, GQA_OUT)

def pool_branch(p, w_pool, pool_scale):
    b, s, _ = p.shape
    pg = p.reshape(b, s, POOL_GROUPS, POOL_GROUP)
    pf = pg.astype(jnp.float32)
    csum = jnp.concatenate([jnp.zeros((b, 1, POOL_GROUPS, POOL_GROUP), jnp.float32),
                            jnp.cumsum(pf, axis=1)], axis=1)
    t = jnp.arange(s)
    means = []
    for gi, w in enumerate(POOL_WINDOWS):
        lo = jnp.clip(t - w // 2, 0, s)
        hi = jnp.clip(t + w - w // 2, 0, s)
        cg = csum[:, :, gi]
        total = jnp.take(cg, hi, axis=1) - jnp.take(cg, lo, axis=1)
        means.append(total / (hi - lo).astype(jnp.float32)[None, :, None])
    pooled = jnp.stack(means, axis=2)
    mixed = (pooled - pf).astype(p.dtype)
    y = jnp.einsum('bsgc,gcd->bsgd', mixed, w_pool).reshape(b, s, POOL_WIDTH)
    return y * pool_scale

def depthwise_conv(u, w, bias):
    c = u.shape[-1]
    y = lax.conv_general_dilated(u, w[:, None, :], window_strides=(1,),
                                 padding=[(CONV_W // 2, CONV_W // 2)],
                                 dimension_numbers=('NWC', 'WIO', 'NWC'),
                                 feature_group_count=c)
    return y + bias

def second_inputs(seed: int = 0) -> dict:
    key = jax.random.key(seed)
    ks = jax.random.split(key, 24)
    f32 = jnp.float32

    def dense(k, shape, fan_in):
        return jax.random.normal(k, shape, f32) * (fan_in ** -0.5)

    def gain(k, shape):
        return 1.0 + 0.1 * jax.random.normal(k, shape, f32)

    L = DEPTH_2
    conv_center = jnp.zeros((CONV_W, 1), f32).at[CONV_W // 2].set(1.0)
    return {
        'x': jax.random.normal(ks[0], (BATCH, SEQ, D_MODEL), f32),
        'attn_norm_g': gain(ks[1], (L, D_MODEL)),
        'w_in': dense(ks[2], (L, D_MODEL, IN_WIDTH), D_MODEL),
        'mla_q_norm_g': gain(ks[3], (L, MLA_Q_LORA)),
        'mla_w_uq': dense(ks[4], (L, MLA_Q_LORA, MLA_HEADS * MLA_QK), MLA_Q_LORA),
        'mla_kv_norm_g': gain(ks[5], (L, MLA_KV_LORA)),
        'mla_w_ukv': dense(ks[6], (L, MLA_KV_LORA, MLA_HEADS * (MLA_NOPE + MLA_V)), MLA_KV_LORA),
        'mla_q_head_g': gain(ks[7], (L, MLA_QK)),
        'mla_k_head_g': gain(ks[8], (L, MLA_QK)),
        'gqa_q_head_g': gain(ks[9], (L, GQA_HEAD_DIM)),
        'gqa_k_head_g': gain(ks[10], (L, GQA_HEAD_DIM)),
        'pool_w': dense(ks[11], (L, POOL_GROUPS, POOL_GROUP, POOL_GROUP), POOL_GROUP),
        'pool_scale': gain(ks[12], (L, POOL_WIDTH)),
        'w_branch_mla': dense(ks[13], (L, MLA_OUT, D_MODEL), MLA_OUT),
        'w_branch_gqa': dense(ks[14], (L, GQA_OUT, D_MODEL), GQA_OUT),
        'w_branch_pool': dense(ks[15], (L, POOL_WIDTH, D_MODEL), POOL_WIDTH),
        'w_out': dense(ks[16], (L, D_MODEL, D_MODEL), D_MODEL),
        'ffn_norm_g': gain(ks[17], (L, D_MODEL)),
        'ffn_w_up': dense(ks[18], (L, D_MODEL, 2 * D_FF), D_MODEL),
        'ffn_conv_w': conv_center[None] + 0.3 * jax.random.normal(ks[19], (L, CONV_W, 2 * D_FF), f32),
        'ffn_conv_b': 0.01 * jax.random.normal(ks[20], (L, 2 * D_FF), f32),
        'ffn_w_down': dense(ks[21], (L, D_FF, D_MODEL), D_FF),
    }

def second_block(x, attn_norm_g, w_in, mla_q_norm_g, mla_w_uq, mla_kv_norm_g, mla_w_ukv,
              mla_q_head_g, mla_k_head_g, gqa_q_head_g, gqa_k_head_g, pool_w, pool_scale,
              w_branch_mla, w_branch_gqa, w_branch_pool, w_out, ffn_norm_g, ffn_w_up,
              ffn_conv_w, ffn_conv_b, ffn_w_down):
    b, s, d = x.shape
    cos_m, sin_m = axial_rope_tables(s, MLA_ROPE)
    cos_g, sin_g = axial_rope_tables(s, GQA_HEAD_DIM)
    for l in range(DEPTH_2):
        h = rms_norm_2(x, attn_norm_g[l])
        proj = h @ w_in[l]
        c_q, c_kv, k_rope, gq, gk, gv, pool_in, gate_logits = split_columns(proj, IN_SIZES)
        o_mla = mla_branch(c_q, c_kv, k_rope, mla_q_norm_g[l], mla_w_uq[l], mla_kv_norm_g[l],
                           mla_w_ukv[l], mla_q_head_g[l], mla_k_head_g[l], cos_m, sin_m)
        o_gqa = gqa_branch(gq, gk, gv, gqa_q_head_g[l], gqa_k_head_g[l], cos_g, sin_g)
        o_pool = pool_branch(pool_in, pool_w[l], pool_scale[l])
        gates = jax.nn.sigmoid(gate_logits.astype(jnp.float32)).astype(x.dtype).reshape(b, s, N_BRANCH, d)
        merged = (gates[:, :, 0] * (o_mla @ w_branch_mla[l])
                  + gates[:, :, 1] * (o_gqa @ w_branch_gqa[l])
                  + gates[:, :, 2] * (o_pool @ w_branch_pool[l]))
        x = x + merged @ w_out[l]
        hf = rms_norm_2(x, ffn_norm_g[l])
        u = depthwise_conv(hf @ ffn_w_up[l], ffn_conv_w[l], ffn_conv_b[l])
        u_gate, u_val = u[..., :D_FF], u[..., D_FF:]
        x = x + (jax.nn.silu(u_gate) * u_val) @ ffn_w_down[l]
    return x


def setup_inputs(seed=0):
    out = dict(first_inputs(seed))
    for name, value in second_inputs(seed + 1).items():
        if name != "x":
            out[name + "_2"] = value
    return out


def reference(
    x, c, w_ada, b_ada, g_mix, w_in, conv_w, conv_b, w_rg_a, b_rg_a, w_rg_x, b_rg_x, lru_lambda,
    sinks, g_attn_out, g_lru_out, w_out, g_ffn, w_router, b_router, w_gu, b_gu, w_down, b_down,
    g_final, attn_norm_g_2, w_in_2, mla_q_norm_g_2, mla_w_uq_2, mla_kv_norm_g_2, mla_w_ukv_2,
    mla_q_head_g_2, mla_k_head_g_2, gqa_q_head_g_2, gqa_k_head_g_2, pool_w_2, pool_scale_2,
    w_branch_mla_2, w_branch_gqa_2, w_branch_pool_2, w_out_2, ffn_norm_g_2, ffn_w_up_2,
    ffn_conv_w_2, ffn_conv_b_2, ffn_w_down_2,
):
    x = first_block(
        x, c, w_ada, b_ada, g_mix, w_in, conv_w, conv_b, w_rg_a, b_rg_a, w_rg_x, b_rg_x,
        lru_lambda, sinks, g_attn_out, g_lru_out, w_out, g_ffn, w_router, b_router, w_gu, b_gu,
        w_down, b_down, g_final,
    )
    return second_block(
        x, attn_norm_g_2, w_in_2, mla_q_norm_g_2, mla_w_uq_2, mla_kv_norm_g_2, mla_w_ukv_2,
        mla_q_head_g_2, mla_k_head_g_2, gqa_q_head_g_2, gqa_k_head_g_2, pool_w_2, pool_scale_2,
        w_branch_mla_2, w_branch_gqa_2, w_branch_pool_2, w_out_2, ffn_norm_g_2, ffn_w_up_2,
        ffn_conv_w_2, ffn_conv_b_2, ffn_w_down_2,
    )


_drawn_inputs = setup_inputs


def setup_inputs(seed=0):
    import zlib

    import numpy as np

    out = dict(_drawn_inputs(seed))
    spreads = {}
    factors = {'b_rg_a': 8.0,
     'b_rg_x': 8.0,
     'sinks': 8.0,
     'b_router': 3.63,
     'b_gu': 6.686,
     'b_down': 8.0,
     'mla_q_norm_g_2': 6.686,
     'mla_q_head_g_2': 7.095,
     'mla_k_head_g_2': 6.75,
     'gqa_q_head_g_2': 8.0,
     'gqa_k_head_g_2': 8.0,
     'ffn_conv_b_2': 5.591}
    for name, (base, spread) in spreads.items():
        noise = np.random.default_rng([zlib.crc32(name.encode()), seed]).standard_normal(out[name].shape)
        drawn = base * np.exp(spread * noise) if base else spread * noise
        out[name] = __import__('jax').numpy.asarray(drawn.astype(out[name].dtype))
    for name, factor in factors.items():
        out[name] = (out[name] * factor).astype(out[name].dtype)
    return out
```

```python
from contextlib import ExitStack

import numpy as np

import concourse.bass as bass
from concourse import mybir

F32 = mybir.dt.float32
I32 = mybir.dt.int32
U32 = mybir.dt.uint32
ALU = mybir.AluOpType
ACT = mybir.ActivationFunctionType
AX = mybir.AxisListType

P = 128
T = 256
TT = T // P
D = 1024
DT = D // P
EPS = 1e-6
HD = 64
NH = 8
NE = 32
TOPK = 4
NL = 2
MQ = 96
FF = 2816
FT = FF // P
POOLS = (2, 4, 8, 16)
PAD = 8
NEG = -1.0e30
WIDTHS = (128, 256)
LIMIT, ALPHA = 7.0, 1.702

RING = 24576
LRING = 16384
HEAP = 21600
STOP = None
LCH = {"act": 1, "dve": 117, "pool": 17, "expert": 8}



class Signal:

    def __init__(self, sem, per=0):
        self.sem, self.per = sem, per

    def at(self, count, run=None):
        return count if run is None else run * self.per + count


class Chain:

    def __init__(self, eng, raised, run=None):
        self.eng, self.raised, self.run, self.n = eng, raised, run, 0

    def mark(self, ins):
        self.n += 1
        ins.then_inc(self.raised.sem, 1)

    def settle(self):
        self.eng.wait_ge(self.raised.sem, self.raised.at(self.n, self.run))

    def step(self, ins):
        self.mark(ins)
        self.settle()


class Fills:

    def __init__(self, order, nbanks, first=0):
        self.order, self.nbanks, self.first = order, nbanks, first
        self.index = {name: n for n, (name, _) in enumerate(order)}
        self.count = {"act": 0, "dve": 0}
        self.drain = []
        for _, who in order:
            self.count[who] += 1
            self.drain.append((who, self.count[who]))

    def bank(self, name):
        return self.first + self.index[name] % self.nbanks

    def full(self, name):
        return self.index[name] + 1

    def before(self, name):
        n = self.index[name] - self.nbanks
        return self.drain[n] if n >= 0 else None


class Stream:

    def __init__(self, pieces, words, again=False):
        self.names = [n for n, _ in pieces]
        self.at, self.over = {}, {}
        owners, self.size = [], dict(pieces)
        for run in range(2 if again else 1):
            pos = 0
            for n, (name, w) in enumerate(pieces):
                if pos + w > words:
                    pos = 0
                lo, hi = pos, pos + w
                before = [o for o in owners if o[0] < hi and o[1] > lo]
                rest = [o for o in owners if o not in before]
                for a, b, o in before:
                    rest += [(a, lo, o)] * (a < lo) + [(hi, b, o)] * (b > hi)
                owners = rest + [(lo, hi, run * len(pieces) + n)]
                self.at[name] = lo
                self.over[name] = [o[2] - run * len(pieces) for o in before]
                pos += w

    def here(self, name):
        return [self.names[i] for i in self.over[name] if i >= 0]


class Arrivals:

    def __init__(self, signals, dmas):
        self.where, count = {}, [0] * len(signals)
        for n, (name, k) in enumerate(dmas):
            i = n % len(signals)
            count[i] += 16 * k
            self.where[name] = (signals[i], count[i])
        for sig, c in zip(signals, count):
            sig.per = c

    def sem(self, name):
        return self.where[name][0].sem

    def here(self, name, run=None):
        sig, count = self.where[name]
        return sig.sem, sig.at(count, run)



def constants():
    i = np.arange(P)
    parts = {}
    parts["ident"] = np.eye(P)
    parts["ones"] = np.ones((P, P))
    parts["pair"] = (i[:, None] // HD == i[None, :] // HD).astype(float)
    parts["earlier"] = (i[:, None] < i[None, :]).astype(float)
    cur = np.where(i[None, :] <= i[:, None], 0.0, NEG)
    prev = np.where(i[None, :] > i[:, None], 0.0, NEG)
    parts["band"] = np.concatenate([cur, prev, cur], 1)
    parts["slots"] = np.tile(np.arange(T, dtype=float), (P, 1))
    parts["experts"] = np.tile(np.arange(NE, dtype=float), (P, 1))

    def rope(rot):
        rows = T // 64
        row = np.repeat(np.arange(rows, dtype=np.float32), 64)
        col = np.tile(np.arange(64, dtype=np.float32), rows)
        n = rot // 4
        inv = (np.float32(10000.0) ** (-np.arange(n, dtype=np.float32) / np.float32(n))).astype(np.float32)
        ang = np.concatenate([row[:, None] * inv, col[:, None] * inv], 1).astype(np.float32)
        return np.cos(ang).T, np.sin(ang).T

    def swap(n, base, half):
        m = np.zeros((P, P))
        for r in range(n):
            q = (r - base) % (2 * half) if r >= base else None
            partner = r if q is None else (r + half if q < half else r - half)
            m[partner, r] = 1.0
        return m

    c, s = rope(HD)
    parts["swap_g"] = swap(P, 0, HD // 2)
    parts["cos_g"] = np.concatenate([c, c, c, c], 0)
    parts["sin_g"] = np.concatenate([-s, s, -s, s], 0)
    c, s = rope(32)
    z = np.zeros((32, T))
    parts["swap_m"] = swap(MQ, 64, 16)
    parts["cos_m"] = np.concatenate([z + 1, z + 1, c, c, z], 0)
    parts["sin_m"] = np.concatenate([z, z, -s, s, z], 0)
    t = np.arange(T)
    inv = [1.0 / (np.clip(t + w - w // 2, 0, T) - np.clip(t - w // 2, 0, T)) for w in POOLS]
    parts["mean"] = np.tile(np.concatenate(inv), (P, 1))
    at, off = {}, 0
    for k, v in parts.items():
        at[k] = (off, v.shape[1])
        off += v.shape[1]
    return np.concatenate(list(parts.values()), 1).astype(np.float32), at


VEC1 = {"b_ada": 48, "c": 8, "g_mix": 8, "conv_w": 16, "conv_b": 4, "b_rg_a": 4, "b_rg_x": 4, "lam": 4,
        "g_attn": 4, "g_lru": 4, "g_ffn": 8, "g_final": 8, "sinks": 8, "b_router": 32, "b_gu": NE * 16}
VEC2 = {"attn_norm": 8, "q_norm": 2, "kv_norm": 1, "q_head": 1, "k_head": 1, "gq_head": 1, "gk_head": 1,
        "pool_scale": 4, "ffn_norm": 8, "conv_w": 3 * 2 * FT, "conv_b": 2 * FT}


def columns(table):
    at, off = {}, 0
    for k, n in table.items():
        at[k] = (off, n)
        off += n
    return at, off



def build(nc, dram, out, stop=None):
    ctx = ExitStack()
    CAT = dram["const_at"]
    V1, V1N = columns(VEC1)
    V2, V2N = columns(VEC2)
    CN = dram["consts"].shape[1]

    def sb(name, shape, dt=F32):
        return ctx.enter_context(nc.sbuf_tensor(name, shape, dt))

    def signal(name, per=0):
        return Signal(ctx.enter_context(nc.semaphore(name)), per)

    with ctx:
        ring = sb("ring", [P, RING])
        heap = sb("heap", [P, HEAP])
        xT = sb("xT", [P, DT, T])
        consts = sb("consts_sb", [P, CN])
        vec1 = sb("vec1", [P, V1N])
        vec2_all = sb("vec2_all", [P, NL, V2N])
        vec2 = sb("vec2", [P, V2N])
        counts_i = sb("counts_i", [1, NE + 1], I32)
        psum = [ctx.enter_context(nc.psum_tensor(f"bank{b}", [P, 512], F32))[:, :] for b in range(8)]

        def const(name, n=None):
            o, w = CAT[name]
            return consts[:, o:o + (n or w)]

        def v1(name, i=None):
            o, w = V1[name]
            return vec1[:, o:o + w] if i is None else vec1[:, o + i:o + i + 1]

        def v2(name, i=None):
            o, w = V2[name]
            return vec2[:, o:o + w] if i is None else vec2[:, o + i:o + i + 1]

        class Carve:

            def __init__(self, spare=False):
                self.areas = [[heap, 0, HEAP]] + ([[ring, LRING, RING]] if spare else [])

            def __call__(self, *shape):
                n = int(np.prod(shape))
                for a in self.areas:
                    if a[1] + n <= a[2]:
                        ap = a[0][:, a[1]:a[1] + n]
                        a[1] += n
                        break
                else:
                    raise ValueError(f"no room for {shape}")
                if len(shape) == 2:
                    return ap.rearrange("p (a b) -> p a b", a=shape[0])
                if len(shape) == 3:
                    return ap.rearrange("p (a b c) -> p a b c", a=shape[0], b=shape[1])
                return ap

        mixer = [(f"ada{j}", 8 * 512) for j in range(4)] + [("w_q", 8 * 512), ("w_kv", 8 * 384), ("w_xr", 8 * 512),
                 ("w_xg", 8 * 512), ("w_rg", 2 * 4 * 64)] + [(f"ada{j}", 8 * 512) for j in range(4, 12)] \
            + [("w_o0", 8 * 512), ("w_o1", 8 * 512), ("w_route", 8 * NE)]
        mix_stream = Stream(mixer, RING)
        MIX_LAST = {**{f"ada{j}": f"ada{j}" for j in range(12)}, "w_q": "q1", "w_kv": "v", "w_xr": "xr1", "w_xg": "xg1",
                    "w_rg": "rg3", "w_o0": "mo1", "w_o1": "mo3", "w_route": "rt"}
        EXPERT = [(f"gu{j}", 8 * 2 * 256) for j in range(4)] + [(f"dn{j}", 2 * D) for j in range(4)]
        exp_stream = Stream(EXPERT, RING)
        layer = [("w_lat", 8 * 416), ("w_gq", 8 * 512), ("w_gkv", 8 * 384), ("w_pool", 8 * 512), ("w_uq", 2 * 768),
                 ("w_ukv", 1024), ("pool_w", 4 * P)] + [(f"gate{j}", 8 * 3 * 256) for j in range(4)] \
            + [(f"br{b}", 4 * D) for b in range(3)] + [(f"wo{j}", 8 * 512) for j in range(2)] \
            + [(f"up{j}", 8 * 2 * 256) for j in range(FT // 2)] + [(f"down{j}", FT * 256) for j in range(4)]
        lay_stream = Stream(layer, LRING, again=True)
        LAY_LAST = {"w_lat": "ckv", "w_gq": "gq1", "w_gkv": "gv", "w_pool": "po1", "w_uq": "uq3", "w_ukv": "uv1",
                    "pool_w": "pl1", **{f"gate{j}": f"ga{3 * j + 2}" for j in range(4)},
                    **{f"br{b}": f"br3{b}" for b in range(3)}, **{f"wo{j}": f"wo{2 * j + 1}" for j in range(2)},
                    **{f"up{j}": f"up{2 * j + 1}" for j in range(FT // 2)}, **{f"down{j}": f"dn{j}" for j in range(4)}}

        def piece(stream, name, a, b=None):
            o = stream.at[name]
            ap = ring[:, o:o + stream.size[name]]
            return ap.rearrange("p (k n) -> p k n", k=a) if b is None else \
                ap.rearrange("p (k g n) -> p k g n", k=a, g=b)

        small_in = signal("small_in")
        mix_in = Arrivals([signal(f"mix_in{i}") for i in range(8)],
                          [(n, {"w_kv": 5, "w_rg": 2}.get(n, 1)) for n, _ in mixer])
        exp_in = {n: signal(f"in_{n}", 16) for n, _ in EXPERT}
        lay_in = Arrivals([signal(f"lay_in{i}") for i in range(11)],
                          [(n, {"w_gkv": 5}.get(n, 3 if n[:4] == "gate" else 2 if n[:2] == "up" else 1))
                           for n, _ in layer])
        out_stored = signal("out_stored")

        take = Carve()
        hT = take(DT, T)
        sq = take(DT, T)
        rstd = take(2, T)
        modT = take(48)
        scale1, scale2 = take(8), take(8)
        qT = take(4, T)
        kT = take(2, T)
        vtok = take(TT, P)
        xr = take(4, 3 + T)
        xg = take(4, T)
        xc = take(4, T)
        lru_a, lru_u = take(4, T), take(4, T)
        lru_t = take(4, T)
        decay = take(4)
        small_done = take(1)
        small = take(64)
        probs = take(NH, 384)
        pT = take(2, 384)
        stat = take(8, 2, NH)
        attnT = take(4, T)
        merged = sq
        gel, lru_h = hT[:, 0:4, :], hT[:, 4:8, :]
        sqm = hT
        lru_d = xr[:, :, 3:3 + T]
        b_down = heap[0:NE, 19800:19800 + D]
        assert take.areas[0][1] <= 19800, take.areas

        MIXFILLS = Fills([("ss1", "dve")] + [(f"ada{j}", "dve") for j in range(4)] + [ ("q0", "act"), ("q1", "act"), ("kd", "act"), ("v", "act"),
                          ("xr0", "act"), ("xr1", "act"), ("xg0", "act"), ("xg1", "act")]
                         + [(f"s{h}", "dve") for h in range(NH)]
                         + [(f"rg{i}", "act") for i in range(4)]
                         + [x for h in range(NH) for x in
                            ([(f"pt{h}", "act")] + ([(f"o{h // 2}", "act")] if h % 2 else []))]
                         + [(f"ada{j}", "dve") for j in range(4, 12)] + [("ssa", "dve"), ("ssl", "dve")]
                         + [(f"mo{i}", "dve") for i in range(4)]
                         + [("ss2", "dve"), ("rt", "dve"), ("rank", "dve"), ("ht0", "act"), ("ht1", "act"),
                            ("ht2", "act"), ("ht3", "act"), ("gT", "act")], 8)
        mix_full = signal("mix_full")
        mix_drained = {"act": signal("mix_drained_act"), "dve": signal("mix_drained_dve")}
        a_chain = signal("mixer_act_chain")
        d_chain = signal("mixer_dve_chain")
        zeroed = signal("zeroed")
        sq_ready, var_ready, std_ready = signal("sq_ready"), signal("var_ready"), signal("std_ready")
        h_ready = signal("h_ready")
        negmax_ready, exp_ready = signal("negmax_ready"), signal("exp_ready")
        probs_ready = signal("probs_ready")
        conv_base, conv_ready = signal("conv_base"), signal("conv_ready")
        decay_ready = signal("decay_ready")
        loga_ready, tanh_ready, sqrt_ready = signal("loga_ready"), signal("tanh_ready"), signal("sqrt_ready")
        gel_poly, gel_tanh, lru_ready = signal("gel_poly"), signal("gel_tanh"), signal("lru_ready")
        lam_exp_in, lam_exp = signal("lam_exp_in"), signal("lam_exp")
        sqm_ready, varm_ready, stdm_ready, merged_ready = (signal("sqm_ready"), signal("varm_ready"),
                                                           signal("stdm_ready"), signal("merged_ready"))
        x1_ready = signal("x1_ready")
        top_ready, gate_exp = signal("top_ready"), signal("gate_exp")
        chosen_ready, gate_ready, slots_ready = signal("chosen_ready"), signal("gate_ready"), signal("slots_ready")

        h2T = hT
        htok = sq.rearrange("p a b -> p (a b)").rearrange("p (a b) -> p a b", a=TT)
        take_e = Carve()
        take_e.areas[0][1] = 2 * DT * T + 2 * T + 64
        xgT = take_e(DT * T)
        hid = take_e(DT * T)
        act_g, act_u, act_s = take_e(1024), take_e(1024), take_e(1024)
        y_sb = take_e(2, D)
        sgT = take_e(2, T)
        pick, pickg = take_e(TT, T), take_e(TT, T)
        gateT = take_e(T)
        expert_end = take_e.areas[0][1]
        router_at = HEAP - TT * 320
        assert expert_end <= router_at, (expert_end, router_at)
        router = heap[:, router_at:HEAP].rearrange("p (a b) -> p a b", a=TT)
        lg, top8, place, gexp, gsum = (router[:, :, 0:32], router[:, :, 32:40], router[:, :, 40:48],
                                       router[:, :, 48:52], router[:, :, 52:54])
        ntop, chosen, gate, slot = (router[:, :, 54:55], router[:, :, 64:96], router[:, :, 96:128],
                                    router[:, :, 128:161])
        gate_of = router[:, :, 96:129]
        onehot, placef = router[:, :, 192:224], router[:, :, 56:64]

        sg_full, sg_drained = signal("sg_full", 1), signal("sg_drained", 1)
        xg_full, xg_drained = signal("xg_full", 1), signal("xg_drained", 1)
        gu_full, gu_drained = signal("gu_full", 4), signal("gu_drained", 4)
        y_full, y_drained = signal("y_full", 2), signal("y_drained", 2)
        dn_used = signal("dn_used", 3)
        pick_ready = signal("pick_ready", 1)
        pre_ready, sig_ready = signal("pre_ready", 4), signal("sig_ready", 4)
        hid_ready = signal("hid_ready", 4)
        combined = signal("combined", 1)
        e_chain = signal("expert_dve_chain", LCH["expert"])
        fin_chain = signal("final_dve_chain")
        x2_ready = signal("x2_ready")
        fin_full = signal("fin_full")
        xin_ready = signal("xin_ready")

        take = Carve(spare=True)
        L = {}
        L["h"] = take(DT, T)
        L["cq"], L["ckv"], L["krope"] = take(2, T), take(T), take(T)
        L["gq"], L["gk"], L["gv"] = take(4, T), take(2, T), take(TT, P)
        L["pool"] = take(4, T + 2 * PAD)
        L["sumA"], L["sumB"] = take(T + 2 * PAD), take(T + 2 * PAD)
        L["sq"], L["rs"] = take(NH, T), take(NH, T)
        L["mq"], L["mk"], L["mv"] = take(NH, T), take(NH, T), take(TT, 512)
        L["gates"] = take(24, T)
        L["o"] = take(3, 4, T)
        L["p"], L["pT"] = take(2, 512), take(4, 512)
        L["stat"] = take(2, 8)
        merged2 = L["mq"]
        ffact = L["gates"].rearrange("p a b -> p (a b)")[:, 0:FT * T].rearrange("p (a b) -> p a b", a=FT)
        conv_t = L["mk"]
        silu_t = L["sq"]

        heads = [f"m{h}" for h in range(NH)] + [f"g{h}" for h in range(NH)]
        order = [("ss1", "dve"), ("cq", "act"), ("ckv", "act"), ("gq0", "act"), ("gq1", "act"), ("gk", "act"),
                 ("gv", "act"), ("po0", "act"), ("po1", "act"), ("sslat", "dve"), ("ssg0", "dve"), ("ssg1", "dve"),
                 ("ssgk", "dve"), ("ga0", "act"), ("ga1", "act")]
        order += [(f"uq{i}", "act") for i in range(4)] + [(f"uk{i}", "act") for i in range(4)]
        order += [("uv0", "act"), ("uv1", "act")] + [("swg0", "dve"), ("swg1", "dve"), ("swgk", "dve")]
        order += [("pl0", "dve"), ("pl1", "dve"), ("ga2", "act")] + [(f"ssq{i}", "dve") for i in range(4)] + [("ga3", "act"), ("ga4", "act")]
        order += [(f"ssk{i}", "dve") for i in range(4)] + [("ga5", "act"), ("ga6", "act")]
        order += [(f"swq{i}", "dve") for i in range(4)] + [(f"swk{i}", "dve") for i in range(4)] + [("ga7", "act")]
        att = heads[NH:] + heads[:NH]
        for i in range(2 * NH + 2):
            if i < 2 * NH:
                order.append((f"s_{att[i]}", "act"))
            if 1 <= i <= 2 * NH:
                order.append((f"t_{att[i - 1]}", "act"))
            if i < 4:
                order.append((f"ga{i + 8}", "act"))
            if i >= 3 and i % 2:
                order.append((f"o_{att[i - 3]}", "act"))
        order += [(f"br{i}{b}", "dve") for i in range(4) for b in range(3)]
        order += [(f"wo{i}", "dve") for i in range(4)] + [("ss2", "dve")]
        order += [(f"up{f}", "dve") for f in range(FT)] + [(f"dn{i}", "dve") for i in range(4)]
        LF = Fills(order, 8)
        lay_full = signal("lay_full", len(order))
        lay_drained = {"act": signal("lay_drained_act", LF.count["act"]),
                       "dve": signal("lay_drained_dve", LF.count["dve"])}
        l_achain = signal("layer_act_chain", LCH["act"])
        l_dchain = signal("layer_dve_chain", LCH["dve"])
        l_pchain = signal("layer_pool_chain", LCH["pool"])
        S = {name: signal(f"l_{name}", per) for name, per in {
            "vecs": 1, "sq1": 1, "var1": 1, "std1": 1, "h1": 1, "lsq": 1, "lvar": 1, "lstd": 1, "lat": 1,
            "gsq": 1, "gvar": 1, "gstd": 1, "gn": 1, "rope_g": 1, "qsq": 1, "qvar": 1, "qstd": 1, "qn": 1,
            "ksq": 1, "kvar": 1, "kstd": 1, "kn": 1, "rope_m": 1, "krope": 1, "mixed": 1,
            "nmax": 2 * NH, "pexp": 2 * NH, "pnorm": 2 * NH, "merged": 4, "x3": 1, "sq2": 1, "var2": 1, "std2": 1,
            "h2": 1, "vals": FT, "conv": FT, "silu": FT, "ffact": FT, "x4": 1}.items()}
        pads_zero = signal("pads_zero")

        def gu_out(w, s, f):
            if w == 256:
                return psum[2 * (s % 2) + f].rearrange("p (g w) -> p g w", g=2)
            return psum[s][:, 2 * w * f:2 * w * (f + 1)].rearrange("p (g w) -> p g w", g=2)

        def tiles_of(bank, w, x, first, parts):
            for a in range(2):
                last = nc.tensor.matmul(bank[0:parts, T * a:T * (a + 1)], w, x[0:parts, first + a, :],
                                        start=True, stop=True)
            return last

        block = ctx.enter_context(nc.Block())

        @block.sync
        def _(sp):
            sp.dma_start(xT[:, :, :], dram["xT"].rearrange("(k p) t -> p k t", p=P)).then_inc(small_in.sem, 16)
            sp.dma_start(vec1[:, :], dram["vec1"]).then_inc(small_in.sem, 16)
            sp.dma_start(consts[:, :], dram["consts"]).then_inc(small_in.sem, 16)
            sp.dma_start(vec2_all[:, :, :], dram["vec2"]).then_inc(small_in.sem, 16)
            sp.dma_start(b_down, dram["b_down"]).then_inc(small_in.sem, 16)

            w_in = dram["w_in"].rearrange("(k p) n -> p k n", p=P)
            w_ada = dram["w_ada"].rearrange("(k p) n -> p k n", p=P)
            w_out = dram["w_out"].rearrange("(k p) n -> p k n", p=P)
            for name, _ in mixer:
                if mix_stream.here(name):
                    sp.wait_ge(mix_full.sem, max(MIXFILLS.full(MIX_LAST[m]) for m in mix_stream.here(name)))
                here = mix_in.sem(name)
                if name.startswith("ada"):
                    j = int(name[3:])
                    sp.dma_start(piece(mix_stream, name, 8), w_ada[:, :, 512 * j:512 * (j + 1)]).then_inc(here, 16)
                elif name == "w_q":
                    sp.dma_start(piece(mix_stream, name, 8), w_in[:, :, 0:512]).then_inc(here, 16)
                elif name == "w_kv":
                    dst = piece(mix_stream, name, 8)
                    for kv in range(2):
                        for twice in range(2):
                            c = 128 * kv + 64 * twice
                            sp.dma_start(dst[:, :, c:c + 64], w_in[:, :, 512 + 64 * kv:576 + 64 * kv]).then_inc(here, 16)
                    sp.dma_start(dst[:, :, 256:384], w_in[:, :, 640:768]).then_inc(here, 16)
                elif name in ("w_xr", "w_xg"):
                    c = 768 if name == "w_xr" else 1280
                    sp.dma_start(piece(mix_stream, name, 8), w_in[:, :, c:c + 512]).then_inc(here, 16)
                elif name == "w_rg":
                    dst = piece(mix_stream, name, 8)
                    for g, w in enumerate(("w_rg_a", "w_rg_x")):
                        sp.dma_start(dst[:, 4 * g:4 * g + 4, :],
                                     dram[w].rearrange("(t b) i j -> (b i) t j", b=2)).then_inc(here, 16)
                elif name in ("w_o0", "w_o1"):
                    c = 512 * int(name[3])
                    sp.dma_start(piece(mix_stream, name, 8), w_out[:, :, c:c + 512]).then_inc(here, 16)
                elif name == "w_route":
                    sp.dma_start(piece(mix_stream, name, 8),
                                 dram["w_router"].rearrange("(k p) n -> p k n", p=P)).then_inc(here, 16)
            if stop == "mix":
                sp.wait_ge(x1_ready.sem, 1)
                sp.dma_start(out.rearrange("(k p) t -> p k t", p=P), xT[:, :, :]).then_inc(out_stored.sem, 16)
                sp.wait_ge(out_stored.sem, 16)
                return

            def load_expert(e, free):
                gu = dram["w_gu"][e].rearrange("(k p) (g n) -> p k g n", p=P, g=2)
                dn = dram["w_down"][e].rearrange("(k p) n -> p k n", p=P)
                for n, (name, _) in enumerate(EXPERT):
                    sp.wait_ge(*free(name))
                    j = int(name[2])
                    if name.startswith("gu"):
                        dst = piece(exp_stream, name, 8, 2)
                        for g in range(2):
                            sp.dma_start(dst[:, :, g, :], gu[:, :, g, 256 * j:256 * (j + 1)]) \
                              .then_inc(exp_in[name].sem, 16)
                    else:
                        sp.dma_start(piece(exp_stream, name, 2), dn[:, 2 * j:2 * j + 2, :]).then_inc(exp_in[name].sem, 16)

            def after_mixer(name):
                lo = exp_stream.at[name]
                return mix_full.sem, max(MIXFILLS.full(MIX_LAST[m]) for m, w in mixer
                                         if mix_stream.at[m] < lo + exp_stream.size[name] and mix_stream.at[m] + w > lo)

            def after_expert(e):
                def free(name):
                    j = int(name[2])
                    if name.startswith("gu"):
                        return gu_full.sem, gu_full.at(j + 1, e)
                    return (dn_used.sem, dn_used.at(j + 1, e)) if j < 3 else (y_full.sem, y_full.at(2, e))
                return free

            load_expert(0, after_mixer)
            with sp.Fori(0, NE - 1) as e:
                load_expert(e + 1, after_expert(e))
            if stop == "moe":
                sp.wait_ge(xin_ready.sem, 8)
                sp.dma_start(out.rearrange("(k p) t -> p k t", p=P), xT[:, :, :]).then_inc(out_stored.sem, 16)
                sp.wait_ge(out_stored.sem, 16)
                return

            lay_names = [n for n, _ in layer]

            def load_layer(l, names, before):
                w_in2 = dram["w_in_2"][l].rearrange("(k p) n -> p k n", p=P)
                w_out2 = dram["w_out_2"][l].rearrange("(k p) n -> p k n", p=P)
                w_up = dram["ffn_w_up_2"][l].rearrange("(k p) (g n) -> p k g n", p=P, g=2)
                w_down = dram["ffn_w_down_2"][l].rearrange("(k p) n -> p k n", p=P)
                for name in names:
                    w = lay_stream.size[name]
                    if lay_stream.here(name):
                        sp.wait_ge(lay_full.sem, lay_full.at(max(LF.full(LAY_LAST[m]) for m in lay_stream.here(name)), l))
                    elif before is None:
                        j = (lay_stream.at[name] + w - 1) // exp_stream.size["gu0"]
                        sp.wait_ge(gu_full.sem, gu_full.at(j + 1, NE - 1))
                    else:
                        sp.wait_ge(lay_full.sem, lay_full.at(max(LF.full(LAY_LAST[lay_names[i]])
                                                                 for i in lay_stream.over[name]), before))
                    here = lay_in.sem(name)
                    if name == "w_lat":
                        sp.dma_start(piece(lay_stream, name, 8), w_in2[:, :, 0:416]).then_inc(here, 16)
                    elif name == "w_gq":
                        sp.dma_start(piece(lay_stream, name, 8), w_in2[:, :, 416:928]).then_inc(here, 16)
                    elif name == "w_gkv":
                        dst = piece(lay_stream, name, 8)
                        for kv in range(2):
                            for twice in range(2):
                                c = 128 * kv + 64 * twice
                                sp.dma_start(dst[:, :, c:c + 64], w_in2[:, :, 928 + 64 * kv:992 + 64 * kv]) \
                                  .then_inc(here, 16)
                        sp.dma_start(dst[:, :, 256:384], w_in2[:, :, 1056:1184]).then_inc(here, 16)
                    elif name == "w_pool":
                        sp.dma_start(piece(lay_stream, name, 8), w_in2[:, :, 1184:1696]).then_inc(here, 16)
                    elif name == "w_uq":
                        sp.dma_start(piece(lay_stream, name, 2), dram["mla_w_uq_2"][l].rearrange("(k p) n -> p k n", p=P)) \
                          .then_inc(here, 16)
                    elif name == "w_ukv":
                        o = lay_stream.at[name]
                        sp.dma_start(ring[:, o:o + 1024], dram["mla_w_ukv_2"][l]).then_inc(here, 16)
                    elif name == "pool_w":
                        sp.dma_start(piece(lay_stream, name, 4), dram["pool_w_2"][l].rearrange("g c d -> c g d")) \
                          .then_inc(here, 16)
                    elif name.startswith("gate"):
                        j = int(name[4])
                        dst = piece(lay_stream, name, 8, 3)
                        for b in range(3):
                            c = 1696 + b * D + 256 * j
                            sp.dma_start(dst[:, :, b, :], w_in2[:, :, c:c + 256]).then_inc(here, 16)
                    elif name.startswith("br"):
                        w_br = dram[("w_branch_mla_2", "w_branch_gqa_2", "w_branch_pool_2")[int(name[2])]][l]
                        sp.dma_start(piece(lay_stream, name, 4), w_br.rearrange("(k p) n -> p k n", p=P)) \
                          .then_inc(here, 16)
                    elif name.startswith("wo"):
                        j = int(name[2])
                        sp.dma_start(piece(lay_stream, name, 8), w_out2[:, :, 512 * j:512 * (j + 1)]).then_inc(here, 16)
                    elif name.startswith("up"):
                        j = int(name[2:])
                        dst = piece(lay_stream, name, 8, 2)
                        for g in range(2):
                            sp.dma_start(dst[:, :, g, :], w_up[:, :, g, 256 * j:256 * (j + 1)]).then_inc(here, 16)
                    elif name.startswith("down"):
                        j = int(name[4:])
                        sp.dma_start(piece(lay_stream, name, FT), w_down[:, :, 256 * j:256 * (j + 1)]).then_inc(here, 16)

            early = [n for n in lay_names if not lay_stream.here(n)]
            late = [n for n in lay_names if lay_stream.here(n)]
            assert lay_names[:len(early)] == early
            load_layer(0, early, None)
            with sp.Fori(0, NL - 1) as l:
                load_layer(l, late, None)
                load_layer(l + 1, early, l)
            load_layer(NL - 1, late, None)
            sp.wait_ge(S["x4"].sem, NL * S["x4"].per)
            sp.dma_start(out.rearrange("(k p) t -> p k t", p=P), xT[:, :, :]).then_inc(out_stored.sem, 16)
            sp.wait_ge(out_stored.sem, 16)

        @block.tensor
        def _(pe):
            mm = nc.tensor.matmul

            def product(outp, w, x, nk):
                for k in range(nk):
                    last = mm(outp, w(k), x(k), start=k == 0, stop=k == nk - 1)
                return last

            def opened(fills, drained, name, run=None):
                b = fills.before(name)
                if b:
                    pe.wait_ge(drained[b[0]].sem, drained[b[0]].at(b[1], run))
                return psum[fills.bank(name)]

            def halves(bank, parts=P):
                return bank[0:parts, :].rearrange("p (a b) -> p a b", a=2)

            ident = const("ident")
            pe.wait_ge(small_in.sem, 5 * 16)

            def mix(name):
                return opened(MIXFILLS, mix_drained, name)

            pe.wait_ge(sq_ready.sem, 1)
            b = mix("ss1")
            product(b[:, 0:T], lambda k: const("ones"), lambda k: sq[:, k, :], DT).then_inc(mix_full.sem, 1)

            def ada(j):
                pe.wait_ge(*mix_in.here(f"ada{j}"))
                b = mix(f"ada{j}")
                w = piece(mix_stream, f"ada{j}", 8)
                for i in range(4):
                    last = product(b[:, i:i + 1], lambda k: w[:, k, P * i:P * (i + 1)],
                                   lambda k: v1("c", k), DT)
                last.then_inc(mix_full.sem, 1)

            for j in range(4):
                ada(j)

            pe.wait_ge(h_ready.sem, 8)
            for name, w_name, i in (("q0", "w_q", 0), ("q1", "w_q", 1), ("kd", "w_kv", 0), ("v", "w_kv", 1),
                                    ("xr0", "w_xr", 0), ("xr1", "w_xr", 1), ("xg0", "w_xg", 0), ("xg1", "w_xg", 1)):
                pe.wait_ge(*mix_in.here(w_name))
                w = piece(mix_stream, w_name, 8)
                b = halves(mix(name))
                for a in range(2):
                    if name == "v":
                        last = product(b[:, a, 0:P], lambda k: hT[:, k, P * a:P * (a + 1)],
                                       lambda k: w[:, k, 256:384], DT)
                    else:
                        c = (2 * i + a) * P
                        last = product(b[:, a, :], lambda k: w[:, k, c:c + P], lambda k: hT[:, k, :], DT)
                last.then_inc(mix_full.sem, 1)

            pe.wait_ge(mix_drained["act"].sem, MIXFILLS.drain[MIXFILLS.index["v"]][1])
            for h in range(NH):
                b = mix(f"s{h}")
                r = slice(HD * (h % 2), HD * (h % 2) + HD)
                mm(b[:, 0:P], qT[r, h // 2, 0:P], kT[r, h // 4, 0:P], start=True, stop=True)
                mm(b[:, P:3 * P], qT[r, h // 2, P:T], kT[r, h // 4, :], start=True, stop=True) \
                    .then_inc(mix_full.sem, 1)

            pe.wait_ge(*mix_in.here("w_rg"))
            pe.wait_ge(conv_ready.sem, 1)
            w = piece(mix_stream, "w_rg", 8)
            for g in range(2):
                for i in range(2):
                    b = halves(mix(f"rg{2 * g + i}"))
                    for a in range(2):
                        t = 2 * i + a
                        for r in (slice(0, HD), slice(HD, P)):
                            last = mm(b[r, a, :], w[r, 4 * g + t, :], xc[r, t, :], start=True, stop=True)
                    last.then_inc(mix_full.sem, 1)

            pe.wait_ge(probs_ready.sem, 1)
            for h in range(NH):
                b = mix(f"pt{h}")
                for i in range(3):
                    last = nc.tensor.transpose(b[:, P * i:P * (i + 1)], probs[:, h, P * i:P * (i + 1)], ident)
                last.then_inc(mix_full.sem, 1)
                if h % 2:
                    b = mix(f"o{h // 2}")
                    for g in (h - 1, h):
                        pe.wait_ge(mix_drained["act"].sem, MIXFILLS.drain[MIXFILLS.index[f"pt{g}"]][1])
                        r = slice(HD * (g % 2), HD * (g % 2) + HD)
                        kv = slice(HD * (g // 4), HD * (g // 4) + HD)
                        pt = pT[:, g % 2, :]
                        mm(b[r, 0:P], vtok[:, 0, kv], pt[:, 0:P], start=True, stop=True)
                        mm(b[r, P:T], vtok[:, 0, kv], pt[:, P:2 * P], start=True, stop=False)
                        last = mm(b[r, P:T], vtok[:, 1, kv], pt[:, 2 * P:3 * P], start=False, stop=True)
                    last.then_inc(mix_full.sem, 1)

            for j in range(4, 12):
                ada(j)

            pe.wait_ge(sqm_ready.sem, 2)
            for name, o in (("ssa", 0), ("ssl", 4)):
                b = mix(name)
                product(b[:, 0:T], lambda k: const("ones"), lambda k: sqm[:, o + k, :], 4).then_inc(mix_full.sem, 1)
            pe.wait_ge(merged_ready.sem, 2)
            for i in range(4):
                pe.wait_ge(*mix_in.here(f"w_o{i // 2}"))
                w = piece(mix_stream, f"w_o{i // 2}", 8)
                b = halves(mix(f"mo{i}"))
                for a in range(2):
                    c = (2 * (i % 2) + a) * P
                    last = product(b[:, a, :], lambda k: w[:, k, c:c + P], lambda k: merged[:, k, :], DT)
                last.then_inc(mix_full.sem, 1)
            if stop == "mix":
                return

            pe.wait_ge(sq_ready.sem, 2)
            b = mix("ss2")
            product(b[:, 0:T], lambda k: const("ones"), lambda k: sq[:, k, :], DT).then_inc(mix_full.sem, 1)
            pe.wait_ge(h_ready.sem, 16)
            pe.wait_ge(*mix_in.here("w_route"))
            w = piece(mix_stream, "w_route", 8)
            b = mix("rt")
            for t in range(TT):
                last = product(b[:, NE * t:NE * (t + 1)], lambda k: h2T[:, k, P * t:P * (t + 1)],
                               lambda k: w[:, k, :], DT)
            last.then_inc(mix_full.sem, 1)
            pe.wait_ge(chosen_ready.sem, 1)
            b = mix("rank")
            mm(b[:, 0:NE], const("earlier"), chosen[:, 0, :], start=True, stop=True)
            mm(b[:, NE:2 * NE], const("ones"), chosen[:, 0, :], start=True, stop=False)
            mm(b[:, NE:2 * NE], const("earlier"), chosen[:, 1, :], start=False, stop=True)
            mm(b[0:1, 64:96], const("ones", 1), chosen[:, 0, :], start=True, stop=False)
            mm(b[0:1, 64:96], const("ones", 1), chosen[:, 1, :], start=False, stop=True).then_inc(mix_full.sem, 1)
            for i in range(4):
                b = mix(f"ht{i}")
                for k in range(4):
                    last = nc.tensor.transpose(b[:, P * k:P * (k + 1)],
                                               h2T[:, 4 * (i % 2) + k, P * (i // 2):P * (i // 2 + 1)], ident)
                last.then_inc(mix_full.sem, 1)
            pe.wait_ge(gate_ready.sem, 1)
            b = mix("gT")
            for t in range(TT):
                last = nc.tensor.transpose(b[0:NE, P * t:P * (t + 1)], gate[:, t, :], ident)
            last.then_inc(mix_full.sem, 1)

            acc = [psum[4 + d // 2][:, T * (d % 2):T * (d % 2) + T] for d in range(DT)]
            pe.wait_ge(mix_drained["act"].sem, MIXFILLS.count["act"])
            pe.wait_ge(mix_drained["dve"].sem, MIXFILLS.count["dve"])
            for d in range(DT):
                mm(acc[d], b_down[:, P * d:P * (d + 1)], gateT[0:NE, :], start=d % 2 == 0, stop=False,
                   skip_group_check=True)
            pe.wait_ge(slots_ready.sem, 2)

            def expert(e, w):
                wp, js = min(w, P), max(1, w // P)
                xg_w = xgT[:, 0:DT * w].rearrange("p (k w) -> p k w", k=DT)
                hid_w = hid[:, 0:DT * w].rearrange("p (k w) -> p k w", k=DT)
                pe.wait_ge(pick_ready.sem, pick_ready.at(1, e))
                for t in range(TT):
                    for j in range(js):
                        last = nc.tensor.transpose(psum[0][:, T * j + P * t:T * j + P * (t + 1)],
                                                   pickg[:, t, P * j:P * (j + 1)], ident)
                last.then_inc(sg_full.sem, 1)
                per = 512 // w
                for i in range(DT // per):
                    if i == 3:
                        pe.wait_ge(sg_drained.sem, sg_drained.at(1, e))
                    for q in range(per):
                        d = per * i + q
                        last = product(psum[(1 + i) % 4][:, w * q:w * (q + 1)],
                                       lambda t: htok[:, t, P * d:P * (d + 1)], lambda t: pick[:, t, 0:w], TT)
                last.then_inc(xg_full.sem, 1)
                pe.wait_ge(xg_drained.sem, xg_drained.at(1, e))
                pe.wait_ge(sg_drained.sem, sg_drained.at(1, e))
                for s in range(4):
                    pe.wait_ge(exp_in[f"gu{s}"].sem, 2 * exp_in[f"gu{s}"].at(16, e))
                    wt = piece(exp_stream, f"gu{s}", 8, 2)
                    if w == 256 and s >= 2:
                        pe.wait_ge(gu_drained.sem, gu_drained.at(s - 1, e))
                    for f in range(2):
                        for g in range(2):
                            last = product(gu_out(w, s, f)[:, g, :], lambda k: wt[:, k, g, P * f:P * (f + 1)],
                                           lambda k: xg_w[:, k, :], DT)
                    last.then_inc(gu_full.sem, 1)
                for j in range(js):
                    pe.wait_ge(gu_drained.sem, gu_drained.at(2 if w < 256 else 3 + j, e))
                    for k in range(DT):
                        if k % 2 == 0 and j == 0:
                            pe.wait_ge(exp_in[f"dn{k // 2}"].sem, exp_in[f"dn{k // 2}"].at(16, e))
                            pe.wait_ge(hid_ready.sem, hid_ready.at(k // 2 + 1, e))
                        wt = piece(exp_stream, f"dn{k // 2}", 2)
                        for half in range(2):
                            last = mm(psum[2 * j + half][0:wp, :], hid_w[:, k, P * j:P * j + wp],
                                      wt[:, k % 2, 512 * half:512 * (half + 1)], start=k == 0, stop=k == DT - 1)
                            if k == DT - 1 and js == 1:
                                last.then_inc(y_full.sem, 1)
                        if k % 2 and k < DT - 1 and j == js - 1:
                            last.then_inc(dn_used.sem, 1)
                    if js == 2:
                        last.then_inc(y_full.sem, 1)
                for j in range(js):
                    for d in range(DT):
                        if js == 1 and d % 4 == 0:
                            pe.wait_ge(y_drained.sem, y_drained.at(1 + d // 4, e))
                        if js == 2 and d == 0:
                            pe.wait_ge(y_drained.sem, y_drained.at(1 + j, e))
                        last = mm(acc[d], y_sb[0:wp, j, P * d:P * (d + 1)], sgT[0:wp, j, :], start=False, stop=True,
                                  skip_group_check=True)
                last.then_inc(combined.sem, 1)

            with pe.Fori(0, NE) as e:
                n = pe.value_load(counts_i[0:1, bass.ds(e, 1)], min_val=0, max_val=T)
                with pe.If(n > P):
                    expert(e, T)
                with pe.Else():
                    expert(e, 128)

            pe.wait_ge(sq_ready.sem, 3)
            product(psum[0][:, 0:T], lambda k: const("ones"), lambda k: hT[:, k, :], DT).then_inc(fin_full.sem, 1)
            if stop == "moe":
                return

            with pe.Fori(0, NL) as l:
                def lay(name):
                    return opened(LF, lay_drained, name, l)

                def arrived(name):
                    pe.wait_ge(*lay_in.here(name, l))

                def tiles(name, w, cols, x, nk=DT, parts=P):
                    b = halves(lay(name), parts)
                    for a in range(2):
                        c = cols + parts * a
                        last = product(b[:, a, :], lambda k: w[:, k, c:c + parts], x, nk)
                    last.then_inc(lay_full.sem, 1)

                def squares(name, ones, x, groups, parts=P):
                    b = halves(lay(name), parts)
                    for a, (o, nk) in enumerate(groups):
                        last = product(b[:, a, :], lambda k: ones, lambda k: x[0:parts, o + k, :], nk)
                    last.then_inc(lay_full.sem, 1)

                def done(sig, n=1):
                    pe.wait_ge(S[sig].sem, S[sig].at(n, l))

                def drained_act(name):
                    pe.wait_ge(lay_drained["act"].sem, lay_drained["act"].at(LF.drain[LF.index[name]][1], l))

                h = lambda k: L["h"][:, k, :]

                def gates(n):
                    if n % 3 == 0:
                        arrived(f"gate{n // 3}")
                    w = piece(lay_stream, f"gate{n // 3}", 8, 3)
                    b = halves(lay(f"ga{n}"))
                    for a in range(2):
                        last = product(b[:, a, :], lambda k: w[:, k, n % 3, P * a:P * (a + 1)], h, DT)
                    last.then_inc(lay_full.sem, 1)

                done("sq1")
                b = lay("ss1")
                product(b[:, 0:T], lambda k: const("ones"), lambda k: L["sq"][:, k, :], DT).then_inc(lay_full.sem, 1)
                done("h1")
                arrived("w_lat")
                w = piece(lay_stream, "w_lat", 8)
                tiles("cq", w, 0, h)
                b = halves(lay("ckv"))
                product(b[:, 0, :], lambda k: w[:, k, 256:384], h, DT)
                product(b[64:96, 1, :], lambda k: w[:, k, 384:416], h, DT).then_inc(lay_full.sem, 1)
                arrived("w_gq")
                w = piece(lay_stream, "w_gq", 8)
                tiles("gq0", w, 0, h)
                tiles("gq1", w, 256, h)
                arrived("w_gkv")
                w = piece(lay_stream, "w_gkv", 8)
                tiles("gk", w, 0, h)
                b = halves(lay("gv"))
                for a in range(2):
                    last = product(b[:, a, 0:P], lambda k: L["h"][:, k, P * a:P * (a + 1)],
                                   lambda k: w[:, k, 256:384], DT)
                last.then_inc(lay_full.sem, 1)
                arrived("w_pool")
                w = piece(lay_stream, "w_pool", 8)
                tiles("po0", w, 0, h)
                tiles("po1", w, 256, h)
                done("lsq")
                squares("sslat", const("ones"), L["sq"], [(0, 2), (2, 1)])
                done("gsq")
                squares("ssg0", const("pair"), L["sq"], [(3, 1), (4, 1)])
                squares("ssg1", const("pair"), L["sq"], [(5, 1), (6, 1)])
                squares("ssgk", const("pair"), L["p"].rearrange("p a b -> p (a b)").rearrange("p (a b) -> p a b", b=T),
                        [(0, 1), (1, 1)])
                gates(0)
                gates(1)
                done("lat")
                arrived("w_uq")
                w = piece(lay_stream, "w_uq", 2)
                for i in range(4):
                    tiles(f"uq{i}", w, 2 * MQ * i, lambda k: L["cq"][:, k, :], 2, MQ)
                arrived("w_ukv")
                w = piece(lay_stream, "w_ukv", 8)
                for i in range(4):
                    b = halves(lay(f"uk{i}"))
                    for a in range(2):
                        last = mm(b[0:HD, a, :], w[:, 2 * i + a, 0:HD], L["ckv"], start=True, stop=True)
                    last.then_inc(lay_full.sem, 1)
                for t in range(TT):
                    b = lay(f"uv{t}")
                    mm(b[:, :].rearrange("p (a b) -> p a b", a=NH), L["ckv"][:, P * t:P * (t + 1)], w[:, :, HD:P],
                       start=True, stop=True).then_inc(lay_full.sem, 1)
                done("gn")
                for i in range(2):
                    tiles_of(lay(f"swg{i}"), const("swap_g"), L["gq"], 2 * i, P).then_inc(lay_full.sem, 1)
                tiles_of(lay("swgk"), const("swap_g"), L["gk"], 0, P).then_inc(lay_full.sem, 1)
                arrived("pool_w")
                done("mixed")
                w = piece(lay_stream, "pool_w", 4)
                for i in range(2):
                    b = halves(lay(f"pl{i}"))
                    for a in range(2):
                        last = mm(b[:, a, :], w[:, 2 * i + a, :], L["pool"][:, 2 * i + a, PAD:PAD + T],
                                  start=True, stop=True)
                    last.then_inc(lay_full.sem, 1)
                gates(2)
                done("qsq")
                for i in range(4):
                    squares(f"ssq{i}", const("ones")[0:MQ, 0:MQ], L["sq"], [(2 * i, 1), (2 * i + 1, 1)], MQ)
                gates(3)
                gates(4)
                done("ksq")
                for i in range(4):
                    squares(f"ssk{i}", const("ones")[0:MQ, 0:MQ], L["sq"], [(2 * i, 1), (2 * i + 1, 1)], MQ)
                gates(5)
                gates(6)
                done("qn")
                for i in range(4):
                    tiles_of(lay(f"swq{i}"), const("swap_m")[0:MQ, 0:MQ], L["mq"], 2 * i, MQ).then_inc(lay_full.sem, 1)
                done("kn")
                for i in range(4):
                    tiles_of(lay(f"swk{i}"), const("swap_m")[0:MQ, 0:MQ], L["mk"], 2 * i, MQ).then_inc(lay_full.sem, 1)
                gates(7)
                for i in range(2 * NH + 2):
                    if i < 2 * NH:
                        if i == 0:
                            done("rope_g")
                        if i == NH:
                            done("rope_m")
                        name = att[i]
                        n = int(name[1])
                        b = halves(lay(f"s_{name}"))
                        if name[0] == "m":
                            q, k = L["mq"][0:MQ, n, :], L["mk"][0:MQ, n, :]
                        else:
                            r = slice(HD * (n % 2), HD * (n % 2) + HD)
                            q, k = L["gq"][r, n // 2, :], L["gk"][r, n // 4, :]
                        for a in range(2):
                            last = mm(b[:, a, :], q[:, P * a:P * (a + 1)], k, start=True, stop=True)
                        last.then_inc(lay_full.sem, 1)
                    if 1 <= i <= 2 * NH:
                        done("pnorm", i)
                        b = lay(f"t_{att[i - 1]}")
                        pr = L["p"][:, (i - 1) % 2, :].rearrange("p (a b) -> p a b", a=2)
                        for st in range(2):
                            for a in range(2):
                                last = nc.tensor.transpose(b[:, T * st + P * a:T * st + P * (a + 1)],
                                                           pr[:, a, P * st:P * (st + 1)], ident)
                        last.then_inc(lay_full.sem, 1)
                    if i < 4:
                        gates(i + 8)
                    if i >= 3 and i % 2:
                        b = lay(f"o_{att[i - 3]}")
                        for g in (i - 3, i - 2):
                            drained_act(f"t_{att[g]}")
                            n = int(att[g][1])
                            r = slice(HD * (n % 2), HD * (n % 2) + HD)
                            for st in range(2):
                                v = L["mv"][:, st, HD * n:HD * (n + 1)] if att[g][0] == "m" else \
                                    L["gv"][:, st, HD * (n // 4):HD * (n // 4 + 1)]
                                last = mm(b[r, 0:T], v, L["pT"][:, g % 4, T * st:T * (st + 1)],
                                          start=st == 0, stop=st == 1)
                        last.then_inc(lay_full.sem, 1)
                pe.wait_ge(lay_drained["dve"].sem, lay_drained["dve"].at(LF.drain[LF.index["pl1"]][1], l))
                drained_act(f"o_{att[2 * NH - 2]}")
                for b_ in range(3):
                    arrived(f"br{b_}")
                for i in range(4):
                    for br in range(3):
                        tiles(f"br{i}{br}", piece(lay_stream, f"br{br}", 4), 2 * P * i, lambda k: L["o"][:, br, k, :], 4)
                done("merged", 4)
                for i in range(4):
                    if i % 2 == 0:
                        arrived(f"wo{i // 2}")
                    tiles(f"wo{i}", piece(lay_stream, f"wo{i // 2}", 8), 2 * P * (i % 2), lambda k: merged2[:, k, :])
                done("sq2")
                b = lay("ss2")
                product(b[:, 0:T], lambda k: const("ones"), lambda k: L["sq"][:, k, :], DT).then_inc(lay_full.sem, 1)
                done("h2")
                for f in range(FT):
                    if f % 2 == 0:
                        arrived(f"up{f // 2}")
                    w = piece(lay_stream, f"up{f // 2}", 8, 2)
                    b = halves(lay(f"up{f}"))
                    for g in range(2):
                        last = product(b[:, g, :], lambda k: w[:, k, g, P * (f % 2):P * (f % 2 + 1)], h, DT)
                    last.then_inc(lay_full.sem, 1)
                for i in range(4):
                    arrived(f"down{i}")
                    if i == 0:
                        done("ffact", FT)
                    tiles(f"dn{i}", piece(lay_stream, f"down{i}", FT), 0, lambda k: ffact[:, k, :], FT)

        @block.scalar
        def _(act):
            f = nc.scalar.activation
            act.wait_ge(small_in.sem, 5 * 16)

            a = Chain(act, a_chain)

            def full(name):
                act.wait_ge(mix_full.sem, MIXFILLS.full(name))
                return psum[MIXFILLS.bank(name)]

            def out_of(name, dst, src=None, func=ACT.Copy, **kw):
                b = full(name)
                f(dst, b[:, :].rearrange("p (a b) -> p a b", a=2) if src is None else src(b), func, **kw) \
                    .then_inc(mix_drained["act"].sem, 1)

            f(sq[:, :, :], xT[:, :, :], ACT.Square).then_inc(sq_ready.sem, 1)
            act.wait_ge(var_ready.sem, 1)
            f(rstd[:, 0, :], rstd[:, 0, :], ACT.Sqrt).then_inc(std_ready.sem, 1)
            act.wait_ge(lam_exp_in.sem, 1)
            f(small[:, 4:8], small[:, 0:4], ACT.Exp, scale=-1.0).then_inc(lam_exp.sem, 1)
            out_of("q0", qT[:, 0:2, :])
            out_of("q1", qT[:, 2:4, :])
            out_of("kd", kT)
            out_of("v", vtok, lambda b: b[:, :].rearrange("p (a b) -> p a b", a=2)[:, :, 0:P])
            out_of("xr0", xr[:, 0:2, 3:3 + T])
            out_of("xr1", xr[:, 2:4, 3:3 + T])
            act.wait_ge(mix_drained["act"].sem, MIXFILLS.drain[MIXFILLS.index["xr1"]][1])
            for t in range(4):
                ins = f(xc[:, t, :], xr[:, t, 3:3 + T], ACT.Identity, scale=v1("conv_w", 4 * t + 3), bias=v1("conv_b", t))
            ins.then_inc(conv_base.sem, 1)
            out_of("xg0", xg[:, 0:2, :])
            out_of("xg1", xg[:, 2:4, :])
            act.wait_ge(negmax_ready.sem, 1)
            f(stat[:, 3, :, :], stat[:, 3, :, :], ACT.Exp)
            for h in range(NH):
                for blk, (c0, c1) in enumerate(((0, P), (P, 3 * P))):
                    ins = f(probs[:, h, c0:c1], probs[:, h, c0:c1], ACT.Exp, bias=stat[:, 1, blk, h:h + 1],
                            accum_out=stat[:, 2, blk, h:h + 1])
            ins.then_inc(exp_ready.sem, 1)
            for g, (dst, bias) in enumerate(((lru_a, "b_rg_a"), (lru_u, "b_rg_x"))):
                for i in range(2):
                    b = full(f"rg{2 * g + i}")
                    f(dst[:, 2 * i, :], b[:, 0:T], ACT.Sigmoid, bias=v1(bias, 2 * i))
                    f(dst[:, 2 * i + 1, :], b[:, T:2 * T], ACT.Sigmoid, bias=v1(bias, 2 * i + 1)) \
                        .then_inc(mix_drained["act"].sem, 1)
            act.wait_ge(mix_drained["act"].sem, MIXFILLS.drain[MIXFILLS.index["rg3"]][1])
            act.wait_ge(decay_ready.sem, 1)
            for t in range(4):
                ins = f(lru_t[:, t, :], lru_a[:, t, :], ACT.Tanh, scale=decay[:, t:t + 1])
            ins.then_inc(tanh_ready.sem, 1)
            for h in range(NH):
                b = full(f"pt{h}")
                f(pT[:, h % 2, :], b[:, 0:384], ACT.Copy).then_inc(mix_drained["act"].sem, 1)
                if h % 2:
                    out_of(f"o{h // 2}", attnT[:, h // 2, :], lambda b: b[:, 0:T])
            act.wait_ge(gel_poly.sem, 1)
            f(gel, gel, ACT.Tanh, scale=0.7978845608028654).then_inc(gel_tanh.sem, 1)
            act.wait_ge(loga_ready.sem, 1)
            f(lru_t, lru_t, ACT.Sqrt).then_inc(sqrt_ready.sem, 1)
            act.wait_ge(lru_ready.sem, 1)
            act.wait_ge(mix_drained["act"].sem, MIXFILLS.drain[MIXFILLS.index["o3"]][1])
            f(sqm[:, 0:4, :], attnT, ACT.Square).then_inc(sqm_ready.sem, 1)
            f(sqm[:, 4:8, :], lru_a, ACT.Square).then_inc(sqm_ready.sem, 1)
            act.wait_ge(varm_ready.sem, 1)
            f(rstd, rstd, ACT.Sqrt).then_inc(stdm_ready.sem, 1)
            if stop == "mix":
                return
            act.wait_ge(x1_ready.sem, 1)
            f(sq[:, :, :], xT[:, :, :], ACT.Square).then_inc(sq_ready.sem, 1)
            act.wait_ge(var_ready.sem, 2)
            f(rstd[:, 0, :], rstd[:, 0, :], ACT.Sqrt).then_inc(std_ready.sem, 1)
            act.wait_ge(top_ready.sem, 2)
            for t in range(TT):
                f(gexp[:, t, :], top8[:, t, 0:TOPK], ACT.Exp, bias=ntop[:, t, :], accum_out=gsum[:, t, 0:1]) \
                    .then_inc(gate_exp.sem, 1)
            for i in range(4):
                out_of(f"ht{i}", htok[:, i // 2, 512 * (i % 2):512 * (i % 2 + 1)], lambda b: b[:, :])
            b = full("gT")
            f(gateT[0:NE, :], b[0:NE, 0:T], ACT.Copy).then_inc(mix_drained["act"].sem, 1)

            act.wait_ge(slots_ready.sem, 2)

            def expert(e, w):
                wp, js, per = min(w, P), max(1, w // P), 512 // w
                act.wait_ge(xg_full.sem, xg_full.at(1, e))
                for i in range(DT // per):
                    ins = f(xgT[:, 512 * i:512 * (i + 1)], psum[(1 + i) % 4][:, :], ACT.Copy)
                ins.then_inc(xg_drained.sem, 1)
                for s in range(4):
                    act.wait_ge(pre_ready.sem, pre_ready.at(s + 1, e))
                    o = 512 * (s % 2)
                    f(act_s[:, o:o + 2 * w], act_g[:, o:o + 2 * w], ACT.Sigmoid, scale=ALPHA).then_inc(sig_ready.sem, 1)
                for j in range(js):
                    if js == 2:
                        act.wait_ge(y_full.sem, y_full.at(j + 1, e))
                    for half in range(2):
                        if js == 1:
                            act.wait_ge(y_full.sem, y_full.at(half + 1, e))
                        ins = f(y_sb[0:wp, j, 512 * half:512 * (half + 1)], psum[2 * j + half][0:wp, :], ACT.Copy)
                        if js == 1:
                            ins.then_inc(y_drained.sem, 1)
                    if js == 2:
                        ins.then_inc(y_drained.sem, 1)

            with act.Fori(0, NE) as e:
                n = act.value_load(counts_i[0:1, bass.ds(e, 1)], min_val=0, max_val=T)
                with act.If(n > P):
                    expert(e, T)
                with act.Else():
                    expert(e, 128)

            act.wait_ge(x2_ready.sem, 8)
            f(hT, xT[:, :, :], ACT.Square).then_inc(sq_ready.sem, 1)
            act.wait_ge(var_ready.sem, 3)
            f(rstd[:, 0, :], rstd[:, 0, :], ACT.Sqrt).then_inc(std_ready.sem, 1)
            if stop == "moe":
                return
            act.wait_ge(xin_ready.sem, 8)

            with act.Fori(0, NL) as l:
                a = Chain(act, l_achain, l)

                def full(name):
                    act.wait_ge(lay_full.sem, lay_full.at(LF.full(name), l))
                    return psum[LF.bank(name)]

                def own(name):
                    act.wait_ge(lay_drained["act"].sem, lay_drained["act"].at(LF.drain[LF.index[name]][1], l))

                def out_of(name, dst, src=None, func=ACT.Copy, **kw):
                    b = full(name)
                    f(dst, b[:, :].rearrange("p (a b) -> p a b", a=2) if src is None else src(b), func, **kw) \
                        .then_inc(lay_drained["act"].sem, 1)

                def ready(sig, n=1):
                    act.wait_ge(S[sig].sem, S[sig].at(n, l))

                def two(b):
                    return b.rearrange("p (a b) -> p a b", a=2)

                def gates(n):
                    o = 8 * (n % 3) + 2 * (n // 3)
                    out_of(f"ga{n}", L["gates"][:, o:o + 2, :], func=ACT.Tanh, scale=0.5)

                ready("vecs")
                f(L["sq"], xT[:, :, :], ACT.Square).then_inc(S["sq1"].sem, 1)
                ready("var1")
                f(L["rs"][:, 0, :], L["rs"][:, 0, :], ACT.Sqrt).then_inc(S["std1"].sem, 1)
                out_of("cq", L["cq"])
                b = full("ckv")
                f(L["ckv"], b[:, 0:T], ACT.Copy)
                f(L["krope"][64:96, :], b[64:96, T:2 * T], ACT.Copy).then_inc(lay_drained["act"].sem, 1)
                out_of("gq0", L["gq"][:, 0:2, :])
                out_of("gq1", L["gq"][:, 2:4, :])
                out_of("gk", L["gk"])
                out_of("gv", L["gv"], lambda b: two(b)[:, :, 0:P])
                out_of("po0", L["pool"][:, 0:2, PAD:PAD + T])
                out_of("po1", L["pool"][:, 2:4, PAD:PAD + T])
                ready("lvar")
                f(L["rs"][:, 0:2, :], L["rs"][:, 0:2, :], ACT.Sqrt).then_inc(S["lstd"].sem, 1)
                ready("gvar")
                f(L["rs"][:, 2:8, :], L["rs"][:, 2:8, :], ACT.Sqrt).then_inc(S["gstd"].sem, 1)
                gates(0)
                gates(1)
                for i in range(4):
                    out_of(f"uq{i}", L["mq"][0:MQ, 2 * i:2 * i + 2, :], lambda b: two(b)[0:MQ])
                for i in range(4):
                    out_of(f"uk{i}", L["mk"][0:HD, 2 * i:2 * i + 2, :], lambda b: two(b)[0:HD])
                own("ckv")
                f(L["mk"][64:96, :, :], L["krope"][64:96, :].unsqueeze(1).to_broadcast([32, NH, T]), ACT.Copy) \
                    .then_inc(S["krope"].sem, 1)
                own("uq3")
                f(L["sq"][0:MQ], L["mq"][0:MQ], ACT.Square).then_inc(S["qsq"].sem, 1)
                for t in range(TT):
                    out_of(f"uv{t}", L["mv"][:, t, :], lambda b: b)
                gates(2)
                ready("qvar")
                f(L["rs"][0:MQ], L["rs"][0:MQ], ACT.Sqrt).then_inc(S["qstd"].sem, 1)
                full("ssq3")
                ready("krope")
                own("uk3")
                f(L["sq"][0:MQ], L["mk"][0:MQ], ACT.Square).then_inc(S["ksq"].sem, 1)
                gates(3)
                gates(4)
                ready("kvar")
                f(L["rs"][0:MQ], L["rs"][0:MQ], ACT.Sqrt).then_inc(S["kstd"].sem, 1)
                gates(5)
                gates(6)
                gates(7)
                for i in range(2 * NH + 2):
                    if i < 2 * NH:
                        b = two(full(f"s_{att[i]}"))
                        ready("nmax", i + 1)
                        scale = (MQ if att[i][0] == "m" else HD) ** -0.5
                        st = L["stat"][:, i % 2, :]
                        pr = two(L["p"][:, i % 2, :])
                        f(pr[:, 0, :], b[:, 0, :], ACT.Exp, scale=scale, bias=st[:, 2:3], accum_out=st[:, 4:5])
                        f(pr[:, 1, :], b[:, 1, :], ACT.Exp, scale=scale, bias=st[:, 3:4], accum_out=st[:, 5:6]) \
                            .then_inc(lay_drained["act"].sem, 1)
                    if 1 <= i <= 2 * NH:
                        out_of(f"t_{att[i - 1]}", L["pT"][:, (i - 1) % 4, :], lambda b: b)
                    if i < 4:
                        gates(i + 8)
                    if i >= 3 and i % 2:
                        n = int(att[i - 3][1])
                        out_of(f"o_{att[i - 3]}", L["o"][:, 0 if att[i - 3][0] == "m" else 1, n // 2, :],
                               lambda b: b[:, 0:T])
                ready("x3")
                f(L["sq"], xT[:, :, :], ACT.Square).then_inc(S["sq2"].sem, 1)
                ready("var2")
                f(L["rs"][:, 0, :], L["rs"][:, 0, :], ACT.Sqrt).then_inc(S["std2"].sem, 1)
                for ft in range(FT + 1):
                    if ft < FT:
                        b = two(full(f"up{ft}"))
                        if ft >= 4:
                            ready("ffact", ft - 3)
                        for g in range(2):
                            c = g * FT + ft
                            ins = f(conv_t[:, 2 * (ft % 4) + g, :], b[:, g, :], ACT.Identity,
                                    scale=v2("conv_w", 2 * FT + c), bias=v2("conv_b", c))
                        ins.then_inc(S["vals"].sem, 1)
                    if ft >= 1:
                        ready("conv", ft)
                        f(silu_t[:, (ft - 1) % 4, :], conv_t[:, 2 * ((ft - 1) % 4), :], ACT.Silu).then_inc(S["silu"].sem, 1)

        @block.vector
        def _(dve):
            v = nc.vector
            dve.wait_ge(small_in.sem, 5 * 16)
            d = Chain(dve, d_chain)

            def full(name):
                dve.wait_ge(mix_full.sem, MIXFILLS.full(name))
                return psum[MIXFILLS.bank(name)]

            def taken(ins):
                ins.then_inc(mix_drained["dve"].sem, 1)

            def own(name):
                dve.wait_ge(mix_drained["dve"].sem, MIXFILLS.drain[MIXFILLS.index[name]][1])

            def variance(name, dst, n, ready):
                taken(v.tensor_scalar(dst, full(name)[:, 0:T], 1.0 / n, EPS, ALU.mult, ALU.add))
                own(name)
                v.reciprocal(dst, dst).then_inc(ready.sem, 1)

            d.step(v.tensor_scalar(small[:, 0:4], v1("lam"), -1.0, None, ALU.mult))
            v.tensor_tensor(small[:, 0:4], small[:, 0:4], v1("lam"), ALU.max).then_inc(lam_exp_in.sem, 1)
            variance("ss1", rstd[:, 0, :], D, var_ready)
            e4, s4, z4, p4 = small[:, 4:8], small[:, 8:12], small[:, 12:16], small[:, 16:20]
            dve.wait_ge(lam_exp.sem, 1)
            d.step(v.tensor_scalar(s4, e4, 2.0, None, ALU.add))
            d.step(v.reciprocal(s4, s4))
            d.step(v.tensor_tensor(s4, s4, e4, ALU.mult))
            d.step(v.tensor_tensor(z4, s4, s4, ALU.mult))
            d.step(v.tensor_scalar(p4, z4, 1.0 / 17, 1.0 / 15, ALU.mult, ALU.add))
            for k in range(13, 0, -2):
                d.step(v.tensor_tensor(p4, p4, z4, ALU.mult))
                d.step(v.tensor_scalar(p4, p4, 1.0 / k, None, ALU.add))
            d.step(v.tensor_tensor(p4, p4, s4, ALU.mult))
            d.step(v.tensor_scalar(z4, v1("lam"), -1.0, 0.0, ALU.mult, ALU.max))
            d.step(v.scalar_tensor_tensor(out=p4, in0=p4, scalar=2.0, in1=z4, op0=ALU.mult, op1=ALU.add))
            v.tensor_scalar(decay, p4, 4.0, None, ALU.mult).then_inc(decay_ready.sem, 1)

            def ada(j):
                b = full(f"ada{j}")
                taken(v.tensor_tensor(modT[:, 4 * j:4 * j + 4], b[:, 0:4], v1("b_ada")[:, 4 * j:4 * j + 4], ALU.add))

            def modulated(scale, shift, dst, r, ready):
                for k in range(DT):
                    d.mark(v.scalar_tensor_tensor(out=dst[:, k, :], in0=xT[:, k, :], scalar=scale[:, k:k + 1], in1=r,
                                                  op0=ALU.mult, op1=ALU.mult))
                d.settle()
                for k in range(DT):
                    v.tensor_scalar(dst[:, k, :], dst[:, k, :], modT[:, shift + k:shift + k + 1], None, ALU.add) \
                        .then_inc(ready.sem, 1)

            for j in range(4):
                ada(j)
            own("ada3")
            d.step(v.scalar_tensor_tensor(out=scale1, in0=modT[:, 8:16], scalar=1.0, in1=v1("g_mix"),
                                          op0=ALU.add, op1=ALU.mult))
            dve.wait_ge(std_ready.sem, 1)
            modulated(scale1, 0, hT, rstd[:, 0, :], h_ready)

            for h in range(NH):
                b = full(f"s{h}")
                taken(v.scalar_tensor_tensor(out=probs[:, h, :], in0=b[:, 0:384], scalar=HD ** -0.5, in1=const("band"),
                                             op0=ALU.mult, op1=ALU.add))
            own(f"s{NH - 1}")
            d.mark(v.tensor_reduce(stat[:, 0, 0, :], probs[:, :, 0:P], AX.X, ALU.max))
            d.step(v.tensor_reduce(stat[:, 0, 1, :], probs[:, :, P:3 * P], AX.X, ALU.max))
            sinks = v1("sinks").unsqueeze(1).to_broadcast([P, 2, NH])
            d.step(v.tensor_tensor(stat[:, 0, :, :], stat[:, 0, :, :], sinks, ALU.max))
            d.mark(v.tensor_scalar(stat[:, 1, :, :], stat[:, 0, :, :], -1.0, None, ALU.mult))
            v.tensor_tensor(stat[:, 3, :, :], sinks, stat[:, 0, :, :], ALU.subtract).then_inc(negmax_ready.sem, 1)
            dve.wait_ge(conv_base.sem, 1)
            dve.wait_ge(zeroed.sem, 1)
            for j in range(3):
                for t in range(4):
                    ins = v.scalar_tensor_tensor(out=xc[:, t, :], in0=xr[:, t, j:j + T], scalar=v1("conv_w", 4 * t + j),
                                                 in1=xc[:, t, :], op0=ALU.mult, op1=ALU.add)
                    if j == 2 and t == 3:
                        ins.then_inc(conv_ready.sem, 1)
                    else:
                        d.mark(ins)
                if j < 2:
                    d.settle()
            dve.wait_ge(exp_ready.sem, 1)
            d.step(v.tensor_tensor(stat[:, 4, :, :], stat[:, 2, :, :], stat[:, 3, :, :], ALU.add))
            d.step(v.reciprocal(stat[:, 5, :, :], stat[:, 4, :, :]))
            d.mark(v.tensor_tensor(probs[:, :, 0:P], probs[:, :, 0:P],
                                   stat[:, 5, 0, :].unsqueeze(2).to_broadcast([P, NH, P]), ALU.mult))
            v.tensor_tensor(probs[:, :, P:3 * P], probs[:, :, P:3 * P],
                            stat[:, 5, 1, :].unsqueeze(2).to_broadcast([P, NH, T]), ALU.mult).then_inc(probs_ready.sem, 1)
            full("xg1")
            dve.wait_ge(mix_drained["act"].sem, MIXFILLS.drain[MIXFILLS.index["xg1"]][1])
            d.step(v.tensor_tensor(gel, xg, xg, ALU.mult))
            d.step(v.tensor_scalar(gel, gel, 0.044715, 1.0, ALU.mult, ALU.add))
            v.tensor_tensor(gel, gel, xg, ALU.mult).then_inc(gel_poly.sem, 1)
            dve.wait_ge(tanh_ready.sem, 1)
            d.step(v.tensor_scalar(lru_d, lru_t, 1.0, None, ALU.add))
            d.mark(v.reciprocal(lru_d, lru_d))
            d.step(v.tensor_scalar(lru_a, lru_t, -1.0, 1.0, ALU.mult, ALU.add))
            v.tensor_tensor(lru_a, lru_a, lru_d, ALU.mult).then_inc(loga_ready.sem, 1)
            d.step(v.tensor_tensor(lru_u, lru_u, xc, ALU.mult))
            d.step(v.tensor_tensor(lru_u, lru_u, lru_d, ALU.mult))
            dve.wait_ge(sqrt_ready.sem, 1)
            d.step(v.scalar_tensor_tensor(out=lru_u, in0=lru_t, scalar=2.0, in1=lru_u, op0=ALU.mult, op1=ALU.mult))
            dve.wait_ge(loga_ready.sem, 1)
            for t in range(4):
                d.mark(v.tensor_tensor_scan(lru_h[:, t, :], lru_a[:, t, :], lru_u[:, t, :], 0.0, ALU.mult, ALU.add))
            dve.wait_ge(gel_tanh.sem, 1)
            d.step(v.scalar_tensor_tensor(out=gel, in0=gel, scalar=1.0, in1=xg, op0=ALU.add, op1=ALU.mult))
            v.scalar_tensor_tensor(out=lru_a, in0=lru_h, scalar=0.5, in1=gel, op0=ALU.mult, op1=ALU.mult) \
                .then_inc(lru_ready.sem, 1)
            for j in range(4, 12):
                ada(j)
            for i, name in enumerate(("ssa", "ssl")):
                taken(v.tensor_scalar(rstd[:, i, :], full(name)[:, 0:T], 1.0 / 512, EPS, ALU.mult, ALU.add))
            own("ssl")
            v.reciprocal(rstd, rstd).then_inc(varm_ready.sem, 1)
            d.step(v.scalar_tensor_tensor(out=scale2, in0=modT[:, 32:40], scalar=1.0, in1=v1("g_ffn"),
                                          op0=ALU.add, op1=ALU.mult))
            dve.wait_ge(stdm_ready.sem, 1)
            dve.wait_ge(lru_ready.sem, 1)
            for half, (src, g) in enumerate(((attnT, "g_attn"), (lru_a, "g_lru"))):
                for t in range(4):
                    ins = v.scalar_tensor_tensor(out=merged[:, 4 * half + t, :], in0=src[:, t, :], scalar=v1(g, t),
                                                 in1=rstd[:, half, :], op0=ALU.mult, op1=ALU.mult)
                ins.then_inc(merged_ready.sem, 1)
            for i in range(4):
                b = full(f"mo{i}")
                for a in range(2):
                    k = 2 * i + a
                    ins = v.scalar_tensor_tensor(out=xT[:, k, :], in0=b[:, T * a:T * (a + 1)],
                                                 scalar=modT[:, 16 + k:17 + k], in1=xT[:, k, :],
                                                 op0=ALU.mult, op1=ALU.add)
                    if a:
                        taken(ins)
                    else:
                        d.mark(ins)
            own("mo3")
            v.tensor_copy(small[:, 20:21], rstd[:, 0, 0:1]).then_inc(x1_ready.sem, 1)
            if stop == "mix":
                return
            variance("ss2", rstd[:, 0, :], D, var_ready)
            dve.wait_ge(std_ready.sem, 2)
            modulated(scale2, 24, h2T, rstd[:, 0, :], h_ready)
            b = full("rt")
            taken(v.tensor_tensor(lg, b[:, 0:2 * NE].rearrange("p (a b) -> p a b", a=2),
                                  v1("b_router").unsqueeze(1).to_broadcast([P, TT, NE]), ALU.add))
            own("rt")
            for t in range(TT):
                d.mark(v.max(top8[:, t, :], lg[:, t, :]))
            d.mark(v.memset(chosen, 0.0))
            d.mark(v.memset(slot, -1.0))
            d.settle()
            for t in range(TT):
                v.tensor_scalar(ntop[:, t, :], top8[:, t, 0:1], -1.0, None, ALU.mult).then_inc(top_ready.sem, 1)
            for t in range(TT):
                d.mark(v.max_index(place[:, t, :].bitcast(U32), top8[:, t, :], lg[:, t, :]))
            d.settle()
            for t in range(TT):
                d.mark(v.tensor_copy(placef[:, t, :], place[:, t, :].bitcast(U32)))
            d.settle()
            for k in range(TOPK):
                for t in range(TT):
                    ins = v.scalar_tensor_tensor(out=chosen[:, t, :], in0=const("experts"), scalar=placef[:, t, k:k + 1],
                                                 in1=chosen[:, t, :], op0=ALU.is_equal, op1=ALU.add)
                    if k == TOPK - 1 and t == TT - 1:
                        ins.then_inc(chosen_ready.sem, 1)
                    else:
                        d.mark(ins)
                if k < TOPK - 1:
                    d.settle()
            dve.wait_ge(gate_exp.sem, 2)
            for t in range(TT):
                d.mark(v.reciprocal(gsum[:, t, 1:2], gsum[:, t, 0:1]))
            d.settle()
            for t in range(TT):
                d.mark(v.tensor_scalar(gexp[:, t, :], gexp[:, t, :], gsum[:, t, 1:2], None, ALU.mult))
            d.settle()
            for k in range(TOPK):
                for t in range(TT):
                    d.mark(v.tensor_scalar(onehot[:, t, :] if k else gate[:, t, :], const("experts"),
                                           placef[:, t, k:k + 1], gexp[:, t, k:k + 1], ALU.is_equal, ALU.mult))
                d.settle()
                if k:
                    ins = v.tensor_tensor(gate, gate, onehot, ALU.add)
                    if k == TOPK - 1:
                        ins.then_inc(gate_ready.sem, 1)
                    else:
                        d.step(ins)
            b = full("rank")
            d.step(v.scalar_tensor_tensor(out=slot[:, :, 0:NE], in0=b[:, 0:2 * NE].rearrange("p (a b) -> p a b", a=2),
                                          scalar=1.0, in1=chosen, op0=ALU.add, op1=ALU.mult))
            taken(v.tensor_copy(counts_i[0:1, 0:NE], b[0:1, 64:96]))
            v.tensor_scalar(slot[:, :, 0:NE], slot[:, :, 0:NE], -1.0, None, ALU.add).then_inc(slots_ready.sem, 1)
            own("rank")
            dve.wait_ge(slots_ready.sem, 1)
            dve.wait_ge(gate_ready.sem, 1)
            v.tensor_copy(small_done, gsum[:, 0, 0:1]).then_inc(slots_ready.sem, 1)

            def select(e):
                for t in range(TT):
                    v.tensor_scalar(pick[:, t, :], const("slots"), slot[:, t, bass.ds(e, 1)], None, ALU.is_equal)
                for t in range(TT):
                    ins = v.tensor_scalar(pickg[:, t, :], const("slots"), slot[:, t, bass.ds(e, 1)],
                                          gate_of[:, t, bass.ds(e, 1)], ALU.is_equal, ALU.mult)
                return ins

            select(0).then_inc(pick_ready.sem, 1)

            def expert(e, w):
                c = Chain(dve, e_chain, e)
                js = max(1, w // P)
                wp = min(w, P)
                dve.wait_ge(sg_full.sem, sg_full.at(1, e))
                v.tensor_copy(sgT[0:wp, 0:js, :], psum[0][0:wp, 0:T * js].rearrange("p (a b) -> p a b", a=js)) \
                    .then_inc(sg_drained.sem, 1)

                def part(buf, s):
                    return buf[:, 512 * (s % 2):512 * (s % 2) + 2 * w].rearrange("p (a b) -> p a b", a=2)

                def finish(s):
                    dve.wait_ge(sig_ready.sem, sig_ready.at(s + 1, e))
                    c.step(v.tensor_tensor(part(act_s, s), part(act_s, s), part(act_g, s), ALU.mult))
                    v.tensor_tensor(hid[:, 2 * w * s:2 * w * (s + 1)].rearrange("p (a b) -> p a b", a=2), part(act_s, s),
                                    part(act_u, s), ALU.mult).then_inc(hid_ready.sem, 1)

                for s in range(4):
                    dve.wait_ge(gu_full.sem, gu_full.at(s + 1, e))
                    for g, buf in ((0, act_g), (1, act_u)):
                        for i in range(2):
                            ins = v.tensor_scalar(part(buf, s)[:, i, :], gu_out(w, s, i)[:, g, :],
                                                  v1("b_gu")[:, bass.ds(16 * e + (8 * g + 2 * s + i), 1)], LIMIT,
                                                  ALU.add, ALU.min)
                            if i:
                                ins.then_inc((gu_drained if g else pre_ready).sem, 1)
                    if s:
                        finish(s - 1)
                    dve.wait_ge(gu_drained.sem, gu_drained.at(s + 1, e))
                    c.step(v.tensor_scalar(part(act_u, s), part(act_u, s), -LIMIT, 1.0, ALU.max, ALU.add))
                finish(3)
                assert c.n == LCH["expert"], ("expert", c.n)

            with dve.Fori(0, NE) as e:
                n = dve.value_load(counts_i[0:1, bass.ds(e, 1)], min_val=0, max_val=T)
                with dve.If(n > P):
                    expert(e, T)
                with dve.Else():
                    expert(e, 128)
                dve.wait_ge(xg_full.sem, xg_full.at(1, e))
                select(e + 1).then_inc(pick_ready.sem, 1)

            dve.wait_ge(combined.sem, combined.at(1, NE - 1))
            for k in range(DT):
                v.scalar_tensor_tensor(out=xT[:, k, :], in0=psum[4 + k // 2][:, T * (k % 2):T * (k % 2) + T],
                                       scalar=modT[:, 40 + k:41 + k], in1=xT[:, k, :], op0=ALU.mult, op1=ALU.add) \
                    .then_inc(x2_ready.sem, 1)
            dve.wait_ge(fin_full.sem, 1)
            c = Chain(dve, fin_chain)
            c.step(v.tensor_scalar(rstd[:, 0, :], psum[0][:, 0:T], 1.0 / D, EPS, ALU.mult, ALU.add))
            v.reciprocal(rstd[:, 0, :], rstd[:, 0, :]).then_inc(var_ready.sem, 1)
            dve.wait_ge(std_ready.sem, 3)
            for k in range(DT):
                v.scalar_tensor_tensor(out=xT[:, k, :], in0=xT[:, k, :], scalar=v1("g_final", k), in1=rstd[:, 0, :],
                                       op0=ALU.mult, op1=ALU.mult).then_inc(xin_ready.sem, 1)
            if stop == "moe":
                return
            dve.wait_ge(xin_ready.sem, 8)

            with dve.Fori(0, NL) as l:
                c = Chain(dve, l_dchain, l)

                def full(name):
                    dve.wait_ge(lay_full.sem, lay_full.at(LF.full(name), l))
                    return psum[LF.bank(name)]

                def taken(ins):
                    ins.then_inc(lay_drained["dve"].sem, 1)

                def own(name):
                    dve.wait_ge(lay_drained["dve"].sem, lay_drained["dve"].at(LF.drain[LF.index[name]][1], l))

                def out_act(name):
                    dve.wait_ge(lay_drained["act"].sem, lay_drained["act"].at(LF.drain[LF.index[name]][1], l))

                def ready(sig, n=1):
                    dve.wait_ge(S[sig].sem, S[sig].at(n, l))

                def two(b):
                    return b.rearrange("p (a b) -> p a b", a=2)

                def mean(dst, src, n):
                    return v.tensor_scalar(dst, src, 1.0 / n, EPS, ALU.mult, ALU.add)

                def scaled(dst, g, r, **kw):
                    return v.scalar_tensor_tensor(out=dst, in0=dst, scalar=g, in1=r, op0=ALU.mult, op1=ALU.mult)

                v.tensor_copy(vec2[:, :], vec2_all[:, bass.ds(l, 1), :].rearrange("p a b -> p (a b)")) \
                    .then_inc(S["vecs"].sem, 1)
                ready("vecs")
                taken(mean(L["rs"][:, 0, :], full("ss1")[:, 0:T], D))
                own("ss1")
                v.reciprocal(L["rs"][:, 0, :], L["rs"][:, 0, :]).then_inc(S["var1"].sem, 1)
                ready("std1")
                for k in range(DT):
                    ins = v.scalar_tensor_tensor(out=L["h"][:, k, :], in0=xT[:, k, :], scalar=v2("attn_norm", k),
                                                 in1=L["rs"][:, 0, :], op0=ALU.mult, op1=ALU.mult)
                ins.then_inc(S["h1"].sem, 1)
                out_act("ckv")
                c.mark(v.tensor_tensor(L["sq"][:, 0:2, :], L["cq"], L["cq"], ALU.mult))
                v.tensor_tensor(L["sq"][:, 2, :], L["ckv"], L["ckv"], ALU.mult).then_inc(S["lsq"].sem, 1)
                out_act("gk")
                c.mark(v.tensor_tensor(L["sq"][:, 3:7, :], L["gq"], L["gq"], ALU.mult))
                gkk = L["gk"].rearrange("p a b -> p (a b)")
                v.tensor_tensor(L["p"][:, 0, :], gkk, gkk, ALU.mult).then_inc(S["gsq"].sem, 1)
                b = two(full("sslat"))
                c.mark(mean(L["rs"][:, 0, :], b[:, 0, :], 256))
                taken(mean(L["rs"][:, 1, :], b[:, 1, :], 128))
                own("sslat")
                v.reciprocal(L["rs"][:, 0:2, :], L["rs"][:, 0:2, :]).then_inc(S["lvar"].sem, 1)
                for i, name in enumerate(("ssg0", "ssg1", "ssgk")):
                    taken(mean(L["rs"][:, 2 + 2 * i:4 + 2 * i, :], two(full(name)), HD))
                own("ssgk")
                v.reciprocal(L["rs"][:, 2:8, :], L["rs"][:, 2:8, :]).then_inc(S["gvar"].sem, 1)
                ready("lstd")
                for k in range(2):
                    c.mark(scaled(L["cq"][:, k, :], v2("q_norm", k), L["rs"][:, 0, :]))
                scaled(L["ckv"], v2("kv_norm", 0), L["rs"][:, 1, :]).then_inc(S["lat"].sem, 1)
                ready("gstd")
                c.mark(scaled(L["gq"], v2("gq_head", 0), L["rs"][:, 2:6, :]))
                scaled(L["gk"], v2("gk_head", 0), L["rs"][:, 6:8, :]).then_inc(S["gn"].sem, 1)
                cos, sin = const("cos_g"), const("sin_g")
                for i, name in enumerate(("swg0", "swg1", "swgk")):
                    taken(v.tensor_tensor(L["rs"][:, 2 * i:2 * i + 2, :], two(full(name)),
                                          sin.unsqueeze(1).to_broadcast([P, 2, T]), ALU.mult))
                c.mark(v.tensor_tensor(L["gq"], L["gq"], cos.unsqueeze(1).to_broadcast([P, 4, T]), ALU.mult))
                c.step(v.tensor_tensor(L["gk"], L["gk"], cos.unsqueeze(1).to_broadcast([P, 2, T]), ALU.mult))
                own("swgk")
                c.mark(v.tensor_tensor(L["gq"], L["gq"], L["rs"][:, 0:4, :], ALU.add))
                v.tensor_tensor(L["gk"], L["gk"], L["rs"][:, 4:6, :], ALU.add).then_inc(S["rope_g"].sem, 1)
                for i in range(2):
                    b = full(f"pl{i}")
                    for a in range(2):
                        k = 2 * i + a
                        ins = v.tensor_scalar(L["o"][:, 2, k, :], b[:, T * a:T * (a + 1)], v2("pool_scale", k), None,
                                              ALU.mult)
                        if a:
                            taken(ins)
                        else:
                            c.mark(ins)
                own("pl1")
                ready("rope_g")
                for q, var, std, norm, buf, gain in (("q", "qvar", "qstd", "qn", "mq", "q_head"),
                                                     ("k", "kvar", "kstd", "kn", "mk", "k_head")):
                    for i in range(4):
                        taken(mean(L["rs"][0:MQ, 2 * i:2 * i + 2, :], two(full(f"ss{q}{i}"))[0:MQ], MQ))
                    own(f"ss{q}3")
                    v.reciprocal(L["rs"][0:MQ], L["rs"][0:MQ]).then_inc(S[var].sem, 1)
                    ready(std)
                    scaled(L[buf][0:MQ], v2(gain, 0)[0:MQ], L["rs"][0:MQ]).then_inc(S[norm].sem, 1)
                    ready(norm)
                cos, sin = const("cos_m")[0:MQ], const("sin_m")[0:MQ]
                for q, buf, tmp in (("q", "mq", "sq"), ("k", "mk", "rs")):
                    for i in range(4):
                        taken(v.tensor_tensor(L[tmp][0:MQ, 2 * i:2 * i + 2, :], two(full(f"sw{q}{i}"))[0:MQ],
                                              sin.unsqueeze(1).to_broadcast([MQ, 2, T]), ALU.mult))
                    c.step(v.tensor_tensor(L[buf][0:MQ], L[buf][0:MQ], cos.unsqueeze(1).to_broadcast([MQ, NH, T]),
                                           ALU.mult))
                    own(f"sw{q}3")
                    ins = v.tensor_tensor(L[buf][0:MQ], L[buf][0:MQ], L[tmp][0:MQ], ALU.add)
                    if q == "q":
                        c.mark(ins)
                    else:
                        ins.then_inc(S["rope_m"].sem, 1)
                for i in range(2 * NH + 1):
                    if i < 2 * NH:
                        b = full(f"s_{att[i]}")
                        scale = (MQ if att[i][0] == "m" else HD) ** -0.5
                        st = L["stat"][:, i % 2, :]
                        c.step(v.tensor_reduce(st[:, 0:2], two(b), AX.X, ALU.max))
                        v.tensor_scalar(st[:, 2:4], st[:, 0:2], -scale, None, ALU.mult).then_inc(S["nmax"].sem, 1)
                    if i >= 1:
                        out_act(f"s_{att[i - 1]}")
                        st = L["stat"][:, (i - 1) % 2, :]
                        c.step(v.reciprocal(st[:, 6:8], st[:, 4:6]))
                        pr = two(L["p"][:, (i - 1) % 2, :])
                        v.tensor_tensor(pr, pr, st[:, 6:8].unsqueeze(2).to_broadcast([P, 2, T]), ALU.mult) \
                            .then_inc(S["pnorm"].sem, 1)
                out_act("ga11")
                for i in range(4):
                    o = 4 * (i % 2)
                    acc, tmp = L["sq"][:, o:o + 2, :], L["sq"][:, o + 2:o + 4, :]
                    for br in range(3):
                        taken(v.scalar_tensor_tensor(out=tmp if br else acc, in0=L["gates"][:, 8 * br + 2 * i:8 * br + 2 * i + 2, :],
                                                     scalar=1.0, in1=two(full(f"br{i}{br}")), op0=ALU.add, op1=ALU.mult))
                        own(f"br{i}{br}")
                        if br == 1:
                            c.step(v.tensor_tensor(acc, acc, tmp, ALU.add))
                        if br == 2:
                            v.tensor_tensor(merged2[:, 2 * i:2 * i + 2, :], acc, tmp, ALU.add).then_inc(S["merged"].sem, 1)
                for i in range(4):
                    taken(v.scalar_tensor_tensor(out=xT[:, 2 * i:2 * i + 2, :], in0=two(full(f"wo{i}")), scalar=0.5,
                                                 in1=xT[:, 2 * i:2 * i + 2, :], op0=ALU.mult, op1=ALU.add))
                own("wo3")
                c.mark(v.tensor_copy(L["stat"][:, 0, 0:1], L["stat"][:, 0, 1:2]))
                v.tensor_copy(L["stat"][:, 1, 0:1], L["stat"][:, 1, 1:2]).then_inc(S["x3"].sem, 1)
                taken(mean(L["rs"][:, 0, :], full("ss2")[:, 0:T], D))
                own("ss2")
                v.reciprocal(L["rs"][:, 0, :], L["rs"][:, 0, :]).then_inc(S["var2"].sem, 1)
                ready("std2")
                for k in range(DT):
                    ins = v.scalar_tensor_tensor(out=L["h"][:, k, :], in0=xT[:, k, :], scalar=v2("ffn_norm", k),
                                                 in1=L["rs"][:, 0, :], op0=ALU.mult, op1=ALU.mult)
                ins.then_inc(S["h2"].sem, 1)
                for ft in range(FT + 1):
                    if ft < FT:
                        b = two(full(f"up{ft}"))
                        ready("vals", ft + 1)
                        for tap in (0, 2):
                            for g in range(2):
                                dst = conv_t[:, 2 * (ft % 4) + g, :]
                                to, src = (slice(1, T), slice(0, T - 1)) if tap == 0 else (slice(0, T - 1), slice(1, T))
                                ins = v.scalar_tensor_tensor(out=dst[:, to], in0=b[:, g, src],
                                                             scalar=v2("conv_w", 2 * FT * tap + g * FT + ft),
                                                             in1=dst[:, to], op0=ALU.mult, op1=ALU.add)
                                if tap == 2 and g == 1:
                                    taken(ins)
                                else:
                                    c.mark(ins)
                            if tap == 0:
                                c.settle()
                    if ft >= 1:
                        ready("silu", ft)
                        v.tensor_tensor(ffact[:, ft - 1, :], silu_t[:, (ft - 1) % 4, :], conv_t[:, 2 * ((ft - 1) % 4) + 1, :],
                                        ALU.mult).then_inc(S["ffact"].sem, 1)
                    if ft < FT:
                        own(f"up{ft}")
                        v.tensor_copy(L["stat"][:, 0, 0:1], L["stat"][:, 0, 1:2]).then_inc(S["conv"].sem, 1)
                for i in range(4):
                    taken(v.tensor_tensor(xT[:, 2 * i:2 * i + 2, :], two(full(f"dn{i}")), xT[:, 2 * i:2 * i + 2, :],
                                          ALU.add))
                own("dn3")
                v.tensor_copy(L["stat"][:, 0, 0:1], L["stat"][:, 0, 1:2]).then_inc(S["x4"].sem, 1)
                ready("x4")
                assert c.n == LCH["dve"], ("dve", c.n)

        @block.gpsimd
        def _(pool):
            g = nc.gpsimd
            g.memset(xr[:, :, 0:3], 0.0).then_inc(zeroed.sem, 1)
            if stop:
                return
            pool.wait_ge(xin_ready.sem, 8)
            g.memset(L["pool"][:, :, 0:PAD], 0.0)
            g.memset(L["pool"][:, :, PAD + T:], 0.0).then_inc(pads_zero.sem, 1)
            pool.wait_ge(pads_zero.sem, 1)
            with pool.Fori(0, NL) as l:
                c = Chain(pool, l_pchain, l)

                def out_act(name):
                    pool.wait_ge(lay_drained["act"].sem, lay_drained["act"].at(LF.drain[LF.index[name]][1], l))

                out_act("po1")
                n = T + 2 * PAD
                for i, w in enumerate(POOLS):
                    x, src = L["pool"][:, i, :], L["pool"][:, i, :]
                    bufs = [L["sumA"], L["sumB"]]
                    step = 1
                    while step < w:
                        dst = bufs.pop(0)
                        bufs.append(dst)
                        m = n - 2 * step + 1
                        c.step(g.tensor_tensor(dst[:, 0:m], src[:, 0:m], src[:, step:step + m], ALU.add))
                        src, step = dst, 2 * step
                    dst = bufs[0]
                    o = PAD - w // 2
                    c.step(g.tensor_tensor(dst[:, 0:T], src[:, o:o + T], const("mean")[:, T * i:T * (i + 1)], ALU.mult))
                    ins = g.tensor_tensor(x[:, PAD:PAD + T], dst[:, 0:T], x[:, PAD:PAD + T], ALU.subtract)
                    if i == 3:
                        ins.then_inc(S["mixed"].sem, 1)
                    else:
                        c.step(ins)
                assert c.n == LCH["pool"], ("pool", c.n)



def tiled(a):
    a = np.asarray(a)
    return np.moveaxis(a.reshape(-1, P), 1, 0)


def kernel(**inputs):
    import concourse.bacc as bacc
    from concourse.bass_utils import run_bass_kernel_spmd

    x = {k: np.asarray(v) for k, v in inputs.items()}
    table, const_at = constants()
    one = {
        "b_ada": tiled(x["b_ada"][0]), "c": tiled(x["c"][0]), "g_mix": tiled(x["g_mix"][0]),
        "conv_w": x["conv_w"][0].reshape(4, 4, P).transpose(2, 1, 0).reshape(P, 16),
        "conv_b": tiled(x["conv_b"][0]), "b_rg_a": tiled(x["b_rg_a"][0].reshape(-1)),
        "b_rg_x": tiled(x["b_rg_x"][0].reshape(-1)), "lam": tiled(x["lru_lambda"][0]),
        "g_attn": tiled(x["g_attn_out"][0]), "g_lru": tiled(x["g_lru_out"][0]), "g_ffn": tiled(x["g_ffn"][0]),
        "g_final": tiled(x["g_final"]), "sinks": np.broadcast_to(x["sinks"][0], (P, NH)),
        "b_router": np.broadcast_to(x["b_router"][0], (P, NE)), "b_gu": tiled(x["b_gu"][0]),
    }

    def rows(v, reps):
        v = np.concatenate([v] * reps)[:P]
        return np.concatenate([v, v[:P - len(v)]])[:, None]

    layers = []
    for l in range(NL):
        y = {k: v[l] for k, v in x.items() if k.endswith("_2")}
        two = {
            "attn_norm": tiled(y["attn_norm_g_2"]), "q_norm": tiled(y["mla_q_norm_g_2"]),
            "kv_norm": tiled(y["mla_kv_norm_g_2"]), "q_head": rows(y["mla_q_head_g_2"], 1),
            "k_head": rows(y["mla_k_head_g_2"], 1), "gq_head": rows(y["gqa_q_head_g_2"], 2),
            "gk_head": rows(y["gqa_k_head_g_2"], 2), "pool_scale": tiled(y["pool_scale_2"]),
            "ffn_norm": tiled(y["ffn_norm_g_2"]), "conv_w": tiled(y["ffn_conv_w_2"].reshape(-1)),
            "conv_b": tiled(y["ffn_conv_b_2"]),
        }
        layers.append(np.concatenate([two[k] for k in VEC2], 1))
    sent = {
        "xT": np.ascontiguousarray(x["x"][0].T),
        "vec1": np.ascontiguousarray(np.concatenate([one[k] for k in VEC1], 1)),
        "vec2": np.ascontiguousarray(np.stack(layers, 1)),
        "consts": table,
    }
    for name in ("w_ada", "w_in", "w_rg_a", "w_rg_x", "w_out", "w_router", "w_gu", "w_down", "b_down"):
        sent[name] = x[name][0]
    for name in ("w_in_2", "mla_w_uq_2", "mla_w_ukv_2", "pool_w_2", "w_branch_mla_2", "w_branch_gqa_2",
                 "w_branch_pool_2", "w_out_2", "ffn_w_up_2", "ffn_w_down_2"):
        sent[name] = x[name]

    nc = bacc.Bacc("TRN2", target_bir_lowering=False, num_devices=1)
    arrays, dram = {}, {"const_at": const_at}
    for name, a in sent.items():
        arrays[f"in_{name}"] = np.ascontiguousarray(a)
        dram[name] = nc.dram_tensor(f"in_{name}", a.shape, F32, kind="ExternalInput").ap()
    out = nc.dram_tensor("out_xT", (D, T), F32, kind="ExternalOutput").ap()
    build(nc, dram, out, STOP)
    r = run_bass_kernel_spmd(nc, [arrays], core_ids=[0])
    return np.ascontiguousarray(r.results[0]["out_xT"].T)[None]
```

```python
from contextlib import ExitStack

import numpy as np

import concourse.bass as bass
from concourse import mybir

F32 = mybir.dt.float32
F32R = mybir.dt.float32r
I32 = mybir.dt.int32
U32 = mybir.dt.uint32
ALU = mybir.AluOpType
ACT = mybir.ActivationFunctionType
AX = mybir.AxisListType

P = 128
T = 256
TT = T // P
D = 1024
DT = D // P
EPS = 1e-6
HD = 64
NH = 8
NE = 32
TOPK = 4
NL = 2
MQ = 96
FF = 2816
FT = FF // P
POOLS = (2, 4, 8, 16)
PAD = 8
NEG = -1.0e30
FEW = 64
LIMIT, ALPHA = 7.0, 1.702

RING = 24576
LRING = 16384
HEAP = 21600
UNIT = 2048
DN_K = UNIT // T
SPLIT = 2 * DT * T + 4 * UNIT + 2 * FT * T
LCH = {"dve": 116, "pool": 19, "expert": 8}



class Signal:

    def __init__(self, sem, per=0):
        self.sem, self.per = sem, per

    def at(self, count, run=None):
        return count if run is None else run * self.per + count


class Chain:

    def __init__(self, eng, raised, run=None):
        self.eng, self.raised, self.run, self.n = eng, raised, run, 0

    def mark(self, ins):
        self.n += 1
        ins.then_inc(self.raised.sem, 1)

    def settle(self):
        self.eng.wait_ge(self.raised.sem, self.raised.at(self.n, self.run))

    def step(self, ins):
        self.mark(ins)
        self.settle()


class Fills:

    def __init__(self, order, nbanks, first=0):
        self.order, self.nbanks, self.first = order, nbanks, first
        self.index = {name: n for n, (name, _) in enumerate(order)}
        self.count = {"act": 0, "dve": 0}
        self.drain = []
        for _, who in order:
            self.count[who] += 1
            self.drain.append((who, self.count[who]))

    def bank(self, name):
        return self.first + self.index[name] % self.nbanks

    def full(self, name):
        return self.index[name] + 1

    def before(self, name):
        n = self.index[name] - self.nbanks
        return self.drain[n] if n >= 0 else None


class Stream:

    def __init__(self, pieces, words, again=False):
        self.names = [n for n, _ in pieces]
        self.at, self.over = {}, {}
        owners, self.size = [], dict(pieces)
        for run in range(2 if again else 1):
            pos = 0
            for n, (name, w) in enumerate(pieces):
                if pos + w > words:
                    pos = 0
                lo, hi = pos, pos + w
                before = [o for o in owners if o[0] < hi and o[1] > lo]
                rest = [o for o in owners if o not in before]
                for a, b, o in before:
                    rest += [(a, lo, o)] * (a < lo) + [(hi, b, o)] * (b > hi)
                owners = rest + [(lo, hi, run * len(pieces) + n)]
                self.at[name] = lo
                self.over[name] = [o[2] - run * len(pieces) for o in before]
                pos += w

    def here(self, name):
        return [self.names[i] for i in self.over[name] if i >= 0]


class Arrivals:

    def __init__(self, signals, dmas):
        self.where, count = {}, [0] * len(signals)
        for n, (name, k) in enumerate(dmas):
            i = n % len(signals)
            count[i] += 16 * k
            self.where[name] = (signals[i], count[i])
        for sig, c in zip(signals, count):
            sig.per = c

    def sem(self, name):
        return self.where[name][0].sem

    def here(self, name, run=None):
        sig, count = self.where[name]
        return sig.sem, sig.at(count, run)



def constants():
    i = np.arange(P)
    parts = {}
    parts["ident"] = np.eye(P)
    parts["ones"] = np.ones((P, P))
    parts["pair"] = (i[:, None] // HD == i[None, :] // HD).astype(float)
    parts["earlier"] = (i[:, None] < i[None, :]).astype(float)
    cur = np.where(i[None, :] <= i[:, None], 0.0, NEG)
    prev = np.where(i[None, :] > i[:, None], 0.0, NEG)
    parts["band"] = np.concatenate([cur, prev, cur], 1)
    parts["slots"] = np.tile(np.arange(T, dtype=float), (P, 1))
    parts["experts"] = np.tile(np.arange(NE, dtype=float), (P, 1))

    def rope(rot):
        rows = T // 64
        row = np.repeat(np.arange(rows, dtype=np.float32), 64)
        col = np.tile(np.arange(64, dtype=np.float32), rows)
        n = rot // 4
        inv = (np.float32(10000.0) ** (-np.arange(n, dtype=np.float32) / np.float32(n))).astype(np.float32)
        ang = np.concatenate([row[:, None] * inv, col[:, None] * inv], 1).astype(np.float32)
        return np.cos(ang).T, np.sin(ang).T

    def swap(n, base, half):
        m = np.zeros((P, P))
        for r in range(n):
            q = (r - base) % (2 * half) if r >= base else None
            partner = r if q is None else (r + half if q < half else r - half)
            m[partner, r] = 1.0
        return m

    c, s = rope(HD)
    parts["swap_g"] = swap(P, 0, HD // 2)
    parts["cos_g"] = np.concatenate([c, c, c, c], 0)
    parts["sin_g"] = np.concatenate([-s, s, -s, s], 0)
    c, s = rope(32)
    z = np.zeros((32, T))
    parts["swap_m"] = swap(MQ, 64, 16)
    parts["cos_m"] = np.concatenate([z + 1, z + 1, c, c, z], 0)
    parts["sin_m"] = np.concatenate([z, z, -s, s, z], 0)
    t = np.arange(T)
    inv = [1.0 / (np.clip(t + w - w // 2, 0, T) - np.clip(t - w // 2, 0, T)) for w in POOLS]
    parts["mean"] = np.tile(np.concatenate(inv), (P, 1))
    at, off = {}, 0
    for k, v in parts.items():
        at[k] = (off, v.shape[1])
        off += v.shape[1]
    return np.concatenate(list(parts.values()), 1).astype(np.float32), at


VEC1 = {"b_ada": 48, "c": 8, "g_mix": 8, "conv_w": 16, "conv_b": 4, "b_rg_a": 4, "b_rg_x": 4, "lam": 4,
        "g_attn": 4, "g_lru": 4, "g_ffn": 8, "g_final": 8, "sinks": 8, "b_router": 32, "b_gu": NE * 16}
VEC2 = {"attn_norm": 8, "q_norm": 2, "kv_norm": 1, "q_head": 1, "k_head": 1, "gq_head": 1, "gk_head": 1,
        "pool_scale": 4, "ffn_norm": 8, "conv_w": 3 * 2 * FT, "conv_b": 2 * FT}


def columns(table):
    at, off = {}, 0
    for k, n in table.items():
        at[k] = (off, n)
        off += n
    return at, off



def build(nc, dram, out):
    ctx = ExitStack()
    CAT = dram["const_at"]
    V1, V1N = columns(VEC1)
    V2, V2N = columns(VEC2)
    CN = dram["consts"].shape[1]

    def sb(name, shape, dt=F32):
        return ctx.enter_context(nc.sbuf_tensor(name, shape, dt))

    def signal(name, per=0):
        return Signal(ctx.enter_context(nc.semaphore(name)), per)

    with ctx:
        xT = sb("xT", [P, DT, T])
        consts = sb("consts_sb", [P, CN])
        vec1 = sb("vec1", [P, V1N])
        vec2_all = sb("vec2_all", [P, NL, V2N])
        vec2 = sb("vec2", [P, V2N])
        counts_i = sb("counts_i", [1, NE + 1], I32)
        with nc.sbuf_tensor("ring", [P, RING], F32) as ring, nc.sbuf_tensor("heap", [P, HEAP], F32) as heap:
            pass
        sb("layer_ring", [P, LRING])
        h_hi, h_lo = sb("h_hi", [P, DT, T], F32R), sb("h_lo", [P, DT, T], F32R)
        w_hi, w_lo = sb("w_hi", [P, 2, UNIT], F32R), sb("w_lo", [P, 2, UNIT], F32R)
        f_hi, f_lo = sb("f_hi", [P, FT, T], F32R), sb("f_lo", [P, FT, T], F32R)
        psum = [ctx.enter_context(nc.psum_tensor(f"bank{b}", [P, 512], F32))[:, :] for b in range(8)]

        def const(name, n=None):
            o, w = CAT[name]
            return consts[:, o:o + (n or w)]

        def v1(name, i=None):
            o, w = V1[name]
            return vec1[:, o:o + w] if i is None else vec1[:, o + i:o + i + 1]

        def v2(name, i=None):
            o, w = V2[name]
            return vec2[:, o:o + w] if i is None else vec2[:, o + i:o + i + 1]

        class Carve:

            def __init__(self, spare=False):
                self.areas = [[heap, 0, HEAP]] + ([[ring, LRING, RING]] if spare else [])

            def __call__(self, *shape):
                n = int(np.prod(shape))
                for a in self.areas:
                    if a[1] + n <= a[2]:
                        ap = a[0][:, a[1]:a[1] + n]
                        a[1] += n
                        break
                else:
                    raise ValueError(f"no room for {shape}")
                if len(shape) == 2:
                    return ap.rearrange("p (a b) -> p a b", a=shape[0])
                if len(shape) == 3:
                    return ap.rearrange("p (a b c) -> p a b c", a=shape[0], b=shape[1])
                return ap

        mixer = [(f"ada{j}", 8 * 512) for j in range(4)] + [("w_q", 8 * 512), ("w_kv", 8 * 384), ("w_xr", 8 * 512),
                 ("w_xg", 8 * 512)] + [(f"ada{j}", 8 * 512) for j in range(4, 12)] \
            + [("w_o0", 8 * 512), ("w_o1", 8 * 512), ("w_route", 8 * NE)]
        mix_stream = Stream(mixer, RING)
        MIX_LAST = {**{f"ada{j}": f"ad{j // 4}" for j in range(12)}, "w_q": "q1", "w_kv": "v", "w_xr": "xr1", "w_xg": "xg1",
                    "w_o0": "mo1", "w_o1": "mo3", "w_route": "rt"}
        EXPERT = [(f"gu{j}", 8 * 2 * 256) for j in range(4)] + [(f"dn{j}", 2 * D) for j in range(4)]
        exp_stream = Stream(EXPERT, RING)
        layer = [("w_lat", 8 * 416), ("w_gq", 8 * 512), ("w_gkv", 8 * 384), ("w_pool", 8 * 512), ("w_uq", 2 * 768),
                 ("w_ukv", 1024), ("pool_w", 4 * P)] + [(f"gate{j}", 8 * 3 * 256) for j in range(4)] \
            + [(f"br{b}", 4 * D) for b in range(3)] + [(f"wo{j}", 8 * 512) for j in range(2)] \
            + [(f"up{j}", 8 * 2 * 256) for j in range(FT // 2)] + [(f"down{j}", FT * 256) for j in range(4)]
        lay_stream = Stream(layer, LRING, again=True)
        LAY_LAST = {"w_lat": "ckv", "w_gq": "gq1", "w_gkv": "gv", "w_pool": "po1", "w_uq": "uq3", "w_ukv": "uv1",
                    "pool_w": "pl1", **{f"gate{j}": f"ga{3 * j + 2}" for j in range(4)},
                    **{f"br{b}": f"br3{b}" for b in range(3)}, **{f"wo{j}": f"wo{2 * j + 1}" for j in range(2)},
                    **{f"up{j}": f"up{2 * j + 1}" for j in range(FT // 2)}, **{f"down{j}": f"dn{j}" for j in range(4)}}

        def piece(stream, name, a, b=None):
            o = stream.at[name]
            ap = ring[:, o:o + stream.size[name]]
            return ap.rearrange("p (k n) -> p k n", k=a) if b is None else \
                ap.rearrange("p (k g n) -> p k g n", k=a, g=b)

        small_in = signal("small_in")
        mix_in = Arrivals([signal(f"mix_in{i}") for i in range(8)],
                          [(n, {"w_kv": 5}.get(n, 1)) for n, _ in mixer])
        exp_in = {n: signal(f"in_{n}", 16) for n, _ in EXPERT}
        lay_in = Arrivals([signal(f"lay_in{i}") for i in range(11)],
                          [(n, {"w_gkv": 5}.get(n, 3 if n[:4] == "gate" else 2 if n[:2] == "up" else 1))
                           for n, _ in layer])
        out_stored = signal("out_stored")

        take = Carve()
        hT = take(DT, T)
        sq = take(DT, T)
        rstd = take(2, T)
        modT = take(48)
        scale1, scale2 = take(8), take(8)
        qT = take(4, T)
        kT = take(2, T)
        vtok = take(TT, P)
        xr = take(4, 3 + T)
        xg = take(4, T)
        xc = take(4, T)
        lru_a, lru_u = take(4, T), take(4, T)
        lru_t = take(4, T)
        decay = take(4)
        small_done = take(1)
        mod_rows = take(512)
        w_rg = take(2 * 4, 64)
        small = take(64)
        probs = take(NH, 384)
        pT = take(2, 384)
        stat = take(8, 2, NH)
        attnT = take(4, T)
        merged = sq
        gel, lru_h = hT[:, 0:4, :], hT[:, 4:8, :]
        sqm = hT
        lru_d = xr[:, :, 3:3 + T]
        b_down = heap[0:NE, 19800:19800 + D]
        assert take.areas[0][1] <= 19800, take.areas

        MIXFILLS = Fills([("ss1", "dve"), ("ad0", "act"), ("at0", "dve"), ("q0", "act"), ("q1", "act"), ("kd", "act"), ("v", "act"),
                          ("xr0", "act"), ("xr1", "act"), ("xg0", "act"), ("xg1", "act")]
                         + [(f"s{h}", "dve") for h in range(NH)]
                         + [("ad1", "act"), ("at1", "dve")] + [(f"rg{i}", "act") for i in range(4)]
                         + [x for h in range(NH) for x in
                            ([(f"pt{h}", "act")] + ([(f"o{h // 2}", "act")] if h % 2 else []))]
                         + [("ad2", "act"), ("at2", "dve"), ("ssa", "dve"), ("ssl", "dve")]
                         + [(f"mo{i}", "dve") for i in range(4)]
                         + [("ss2", "dve"), ("rt", "dve"), ("rank", "dve"), ("ht0", "act"), ("ht1", "act"),
                            ("ht2", "act"), ("ht3", "act"), ("gT", "act")], 8)
        mix_full = signal("mix_full")
        mix_drained = {"act": signal("mix_drained_act"), "dve": signal("mix_drained_dve")}
        d_chain = signal("mixer_dve_chain")
        zeroed = signal("zeroed")
        sq_ready, var_ready, std_ready = signal("sq_ready"), signal("var_ready"), signal("std_ready")
        h_ready = signal("h_ready")
        negmax_ready, exp_ready = signal("negmax_ready"), signal("exp_ready")
        probs_ready = signal("probs_ready")
        conv_base, conv_ready = signal("conv_base"), signal("conv_ready")
        decay_ready = signal("decay_ready")
        loga_ready, tanh_ready, sqrt_ready = signal("loga_ready"), signal("tanh_ready"), signal("sqrt_ready")
        gel_poly, gel_tanh, lru_ready = signal("gel_poly"), signal("gel_tanh"), signal("lru_ready")
        lam_exp_in, lam_exp = signal("lam_exp_in"), signal("lam_exp")
        sqm_ready, varm_ready, stdm_ready, merged_ready = (signal("sqm_ready"), signal("varm_ready"),
                                                           signal("stdm_ready"), signal("merged_ready"))
        x1_ready = signal("x1_ready")
        top_ready, gate_exp = signal("top_ready"), signal("gate_exp")
        chosen_ready, gate_ready, slots_ready = signal("chosen_ready"), signal("gate_ready"), signal("slots_ready")

        h2T = hT
        htok = sq.rearrange("p a b -> p (a b)").rearrange("p (a b) -> p a b", a=TT)
        take_e = Carve()
        take_e.areas[0][1] = 2 * DT * T + 2 * T + 64
        xgT = take_e(TT, DT, P)
        hid = take_e(DT * T)
        act_g, act_u, act_s = take_e(1024), take_e(1024), take_e(1024)
        y_sb = take_e(2, D)
        sgT = take_e(2, T)
        pick, pickg = take_e(TT, T), take_e(TT, FEW + T)
        pre_tok = take_e(2, 2, P)
        gateT = take_e(T)
        expert_end = take_e.areas[0][1]
        router_at = HEAP - TT * 320
        assert expert_end <= router_at, (expert_end, router_at)
        router = heap[:, router_at:HEAP].rearrange("p (a b) -> p a b", a=TT)
        lg, top8, place, gexp, gsum = (router[:, :, 0:32], router[:, :, 32:40], router[:, :, 40:48],
                                       router[:, :, 48:52], router[:, :, 52:54])
        ntop, chosen, gate, slot = (router[:, :, 54:55], router[:, :, 64:96], router[:, :, 96:128],
                                    router[:, :, 128:161])
        gate_of = router[:, :, 96:129]
        onehot, placef = router[:, :, 192:224], router[:, :, 56:64]

        sg_full, sg_drained = signal("sg_full", 1), signal("sg_drained", 1)
        xg_full, xg_drained = signal("xg_full", 1), signal("xg_drained", 1)
        gu_full, gu_drained = signal("gu_full", 4), signal("gu_drained", 4)
        gu_taken = signal("gu_taken", 4)
        turned_full = signal("turned_full", 4)
        y_full, y_drained = signal("y_full", 2), signal("y_drained", 2)
        dn_used = signal("dn_used", 3)
        pick_ready = signal("pick_ready", 1)
        pre_ready, sig_ready = signal("pre_ready", 4), signal("sig_ready", 4)
        hid_ready = signal("hid_ready", 4)
        combined = signal("combined", 1)
        e_chain = signal("expert_dve_chain", LCH["expert"])
        fin_chain = signal("final_dve_chain")
        x2_ready = signal("x2_ready")
        fin_full = signal("fin_full")
        xin_ready = signal("xin_ready")

        take = Carve(spare=True)
        L = {}
        tail = Carve()
        tail.areas[0][1] = HEAP - 3 * DT * T - 64
        assert tail.areas[0][1] >= SPLIT - (RING - LRING)
        take.areas[0][2] = tail.areas[0][1]
        L["sq"], L["rs"], L["mk"] = tail(NH, T), tail(NH, T), tail(NH, T)
        L["stat"] = tail(3, 8)
        L["h"] = take(DT, T)
        L["cq"], L["ckv"], L["krope"] = take(2, T), take(T), take(T)
        L["gq"], L["gk"], L["gv"] = take(4, T), take(2, T), take(TT, P)
        L["pool"] = take(4, T + 2 * PAD)
        L["sumA"], L["sumB"] = take(T + 2 * PAD), take(T + 2 * PAD)
        L["mq"], L["mv"] = take(NH, T), take(TT, 512)
        L["gates"] = take(24, T)
        L["o"] = take(3, 4, T)
        L["p"], L["pT"] = take(3, 512), take(4, 512)
        merged2 = L["mq"]
        h_full = L["mk"]
        ff_t = L["rs"][:, 4:8, :]
        conv_t = L["mk"]
        silu_t = L["sq"]

        heads = [f"m{h}" for h in range(NH)] + [f"g{h}" for h in range(NH)]
        order = [("ss1", "dve"), ("cq", "act"), ("ckv", "act"), ("gq0", "act"), ("gq1", "act"), ("gk", "act"),
                 ("gv", "act"), ("po0", "act"), ("po1", "act"), ("sslat", "dve"), ("ssg0", "dve"), ("ssg1", "dve"),
                 ("ssgk", "dve"), ("ga0", "act"), ("ga1", "act")]
        order += [(f"uq{i}", "act") for i in range(4)] + [(f"uk{i}", "act") for i in range(4)]
        order += [("uv0", "act"), ("uv1", "act")] + [("swg0", "dve"), ("swg1", "dve"), ("swgk", "dve")]
        order += [("pl0", "dve"), ("pl1", "dve"), ("ga2", "act")] + [(f"ssq{i}", "dve") for i in range(4)] + [("ga3", "act"), ("ga4", "act")]
        order += [(f"ssk{i}", "dve") for i in range(4)] + [("ga5", "act"), ("ga6", "act")]
        order += [(f"swq{i}", "dve") for i in range(4)] + [(f"swk{i}", "dve") for i in range(4)] + [("ga7", "act")]
        att = heads[NH:] + heads[:NH]
        for i in range(2 * NH + 3):
            if i < 2 * NH:
                order.append((f"s_{att[i]}", "act"))
            if 2 <= i < 2 * NH + 2:
                order.append((f"t_{att[i - 2]}", "act"))
            if i < 4:
                order.append((f"ga{i + 8}", "act"))
            if i >= 4 and i % 2 == 0:
                order.append((f"o_{att[i - 4]}", "act"))
        order += [(f"br{i}{b}", "dve") for i in range(4) for b in range(3)]
        order += [(f"wo{i}", "dve") for i in range(4)] + [("ss2", "dve")]
        order += [(f"up{f}", "dve") for f in range(FT)] + [(f"dn{i}", "dve") for i in range(4)]
        LF = Fills(order, 8)
        lay_full = signal("lay_full", len(order))
        lay_drained = {"act": signal("lay_drained_act", LF.count["act"]),
                       "dve": signal("lay_drained_dve", LF.count["dve"])}
        l_dchain = signal("layer_dve_chain", LCH["dve"])
        l_pchain = signal("layer_pool_chain", LCH["pool"])
        S = {name: signal(f"l_{name}", per) for name, per in {
            "vecs": 1, "sq1": 1, "var1": 1, "std1": 1, "h1": 1, "lsq": 1, "lvar": 1, "lstd": 1, "lat": 1,
            "gsq": 1, "gvar": 1, "gstd": 1, "gn": 1, "rope_g": 1, "qsq": 1, "qvar": 1, "qstd": 1, "qn": 1,
            "ksq": 1, "kvar": 1, "kstd": 1, "kn": 1, "rope_m": 1, "krope": 1, "mixed": 1,
            "nmax": 2 * NH, "pexp": 2 * NH, "pnorm": 2 * NH, "merged": 4, "sq2": 4, "var2": 1, "std2": 1,
            "h2": 2, "vals": FT, "conv": FT, "silu": FT, "ffact": FT, "x4": 1,
            "hfull": 2, "hhi": 2, "whi": FT + 12, "wlo": FT + 12, "wused": 8, "fhi": FT, "flo": FT}.items()}

        def unit(n):
            if n < FT:
                src = piece(lay_stream, f"up{n // 2}", 8, 2)[:, :, :, P * (n % 2):P * (n % 2 + 1)]
                name, src = f"up{n // 2}", src.rearrange("p k g n -> p (k g) n")
            else:
                i, c = divmod(n - FT, 3)
                name = f"down{i}"
                src = piece(lay_stream, name, FT)[:, DN_K * c:min(DN_K * (c + 1), FT), :]
            shape = src.shape
            hi, lo = (x[:, n % 2, 0:shape[1] * shape[2]].rearrange("p (a b) -> p a b", a=shape[1]) for x in (w_hi, w_lo))
            before = n - 2
            if before < 0:
                free = (lay_full, LF.full("wo3"))
            elif before < FT:
                free = (lay_full, LF.full(f"up{before}"))
            else:
                i, c = divmod(before - FT, 3)
                free = (lay_full, LF.full(f"dn{i}")) if c == 2 else (S["wused"], 2 * i + c + 1)
            return name, src, hi, lo, free

        def gu_out(w, s, f):
            if w == FEW:
                return psum[2 + s % 2][:, 0:4 * w].rearrange("p (g f w) -> p g f w", g=2, f=2)[:, :, f, :]
            if w == T:
                return psum[2 * (s % 2) + f].rearrange("p (g w) -> p g w", g=2)
            return psum[s][:, 2 * w * f:2 * w * (f + 1)].rearrange("p (g w) -> p g w", g=2)

        def tiles_of(bank, w, x, first, parts):
            for a in range(2):
                last = nc.tensor.matmul(bank[0:parts, T * a:T * (a + 1)], w, x[0:parts, first + a, :],
                                        start=True, stop=True)
            return last

        block = ctx.enter_context(nc.Block())

        @block.sync
        def _(sp):
            sp.dma_start(xT[:, :, :], dram["xT"].rearrange("(k p) t -> p k t", p=P)).then_inc(small_in.sem, 16)
            sp.dma_start(vec1[:, :], dram["vec1"]).then_inc(small_in.sem, 16)
            sp.dma_start(consts[:, :], dram["consts"]).then_inc(small_in.sem, 16)
            sp.dma_start(vec2_all[:, :, :], dram["vec2"]).then_inc(small_in.sem, 16)
            sp.dma_start(b_down, dram["b_down"]).then_inc(small_in.sem, 16)
            for g, w in enumerate(("w_rg_a", "w_rg_x")):
                sp.dma_start(w_rg[:, 4 * g:4 * g + 4, :],
                             dram[w].rearrange("(t b) i j -> (b i) t j", b=2)).then_inc(small_in.sem, 16)

            w_in = dram["w_in"].rearrange("(k p) n -> p k n", p=P)
            w_ada = dram["w_ada"].rearrange("(k p) n -> p k n", p=P)
            w_out = dram["w_out"].rearrange("(k p) n -> p k n", p=P)
            for name, _ in mixer:
                if mix_stream.here(name):
                    sp.wait_ge(mix_full.sem, max(MIXFILLS.full(MIX_LAST[m]) for m in mix_stream.here(name)))
                here = mix_in.sem(name)
                if name.startswith("ada"):
                    j = int(name[3:])
                    sp.dma_start(piece(mix_stream, name, 8), w_ada[:, :, 512 * j:512 * (j + 1)]).then_inc(here, 16)
                elif name == "w_q":
                    sp.dma_start(piece(mix_stream, name, 8), w_in[:, :, 0:512]).then_inc(here, 16)
                elif name == "w_kv":
                    dst = piece(mix_stream, name, 8)
                    for kv in range(2):
                        for twice in range(2):
                            c = 128 * kv + 64 * twice
                            sp.dma_start(dst[:, :, c:c + 64], w_in[:, :, 512 + 64 * kv:576 + 64 * kv]).then_inc(here, 16)
                    sp.dma_start(dst[:, :, 256:384], w_in[:, :, 640:768]).then_inc(here, 16)
                elif name in ("w_xr", "w_xg"):
                    c = 768 if name == "w_xr" else 1280
                    sp.dma_start(piece(mix_stream, name, 8), w_in[:, :, c:c + 512]).then_inc(here, 16)
                elif name in ("w_o0", "w_o1"):
                    c = 512 * int(name[3])
                    sp.dma_start(piece(mix_stream, name, 8), w_out[:, :, c:c + 512]).then_inc(here, 16)
                elif name == "w_route":
                    sp.dma_start(piece(mix_stream, name, 8),
                                 dram["w_router"].rearrange("(k p) n -> p k n", p=P)).then_inc(here, 16)

            def load_expert(e, free):
                gu = dram["w_gu"][e].rearrange("(k p) (g n) -> p k g n", p=P, g=2)
                dn = dram["w_down"][e].rearrange("(k p) n -> p k n", p=P)
                for n, (name, _) in enumerate(EXPERT):
                    sp.wait_ge(*free(name))
                    j = int(name[2])
                    if name.startswith("gu"):
                        dst = piece(exp_stream, name, 8, 2)
                        for g in range(2):
                            sp.dma_start(dst[:, :, g, :], gu[:, :, g, 256 * j:256 * (j + 1)]) \
                              .then_inc(exp_in[name].sem, 16)
                    else:
                        sp.dma_start(piece(exp_stream, name, 2), dn[:, 2 * j:2 * j + 2, :]).then_inc(exp_in[name].sem, 16)

            def after_mixer(name):
                lo = exp_stream.at[name]
                return mix_full.sem, max(MIXFILLS.full(MIX_LAST[m]) for m, w in mixer
                                         if mix_stream.at[m] < lo + exp_stream.size[name] and mix_stream.at[m] + w > lo)

            def after_expert(e):
                def free(name):
                    j = int(name[2])
                    if name.startswith("gu"):
                        return gu_full.sem, gu_full.at(j + 1, e)
                    return (dn_used.sem, dn_used.at(j + 1, e)) if j < 3 else (y_full.sem, y_full.at(2, e))
                return free

            load_expert(0, after_mixer)
            with sp.Fori(0, NE - 1) as e:
                load_expert(e + 1, after_expert(e))

            lay_names = [n for n, _ in layer]

            def load_layer(l, names, before):
                w_in2 = dram["w_in_2"][l].rearrange("(k p) n -> p k n", p=P)
                w_out2 = dram["w_out_2"][l].rearrange("(k p) n -> p k n", p=P)
                w_up = dram["ffn_w_up_2"][l].rearrange("(k p) (g n) -> p k g n", p=P, g=2)
                w_down = dram["ffn_w_down_2"][l].rearrange("(k p) n -> p k n", p=P)
                for name in names:
                    w = lay_stream.size[name]
                    if lay_stream.here(name):
                        sp.wait_ge(lay_full.sem, lay_full.at(max(LF.full(LAY_LAST[m]) for m in lay_stream.here(name)), l))
                    elif before is None:
                        j = (lay_stream.at[name] + w - 1) // exp_stream.size["gu0"]
                        sp.wait_ge(gu_full.sem, gu_full.at(j + 1, NE - 1))
                    else:
                        sp.wait_ge(lay_full.sem, lay_full.at(max(LF.full(LAY_LAST[lay_names[i]])
                                                                 for i in lay_stream.over[name]), before))
                    here = lay_in.sem(name)
                    if name == "w_lat":
                        sp.dma_start(piece(lay_stream, name, 8), w_in2[:, :, 0:416]).then_inc(here, 16)
                    elif name == "w_gq":
                        sp.dma_start(piece(lay_stream, name, 8), w_in2[:, :, 416:928]).then_inc(here, 16)
                    elif name == "w_gkv":
                        dst = piece(lay_stream, name, 8)
                        for kv in range(2):
                            for twice in range(2):
                                c = 128 * kv + 64 * twice
                                sp.dma_start(dst[:, :, c:c + 64], w_in2[:, :, 928 + 64 * kv:992 + 64 * kv]) \
                                  .then_inc(here, 16)
                        sp.dma_start(dst[:, :, 256:384], w_in2[:, :, 1056:1184]).then_inc(here, 16)
                    elif name == "w_pool":
                        sp.dma_start(piece(lay_stream, name, 8), w_in2[:, :, 1184:1696]).then_inc(here, 16)
                    elif name == "w_uq":
                        sp.dma_start(piece(lay_stream, name, 2), dram["mla_w_uq_2"][l].rearrange("(k p) n -> p k n", p=P)) \
                          .then_inc(here, 16)
                    elif name == "w_ukv":
                        o = lay_stream.at[name]
                        sp.dma_start(ring[:, o:o + 1024], dram["mla_w_ukv_2"][l]).then_inc(here, 16)
                    elif name == "pool_w":
                        sp.dma_start(piece(lay_stream, name, 4), dram["pool_w_2"][l].rearrange("g c d -> c g d")) \
                          .then_inc(here, 16)
                    elif name.startswith("gate"):
                        j = int(name[4])
                        dst = piece(lay_stream, name, 8, 3)
                        for b in range(3):
                            c = 1696 + b * D + 256 * j
                            sp.dma_start(dst[:, :, b, :], w_in2[:, :, c:c + 256]).then_inc(here, 16)
                    elif name.startswith("br"):
                        w_br = dram[("w_branch_mla_2", "w_branch_gqa_2", "w_branch_pool_2")[int(name[2])]][l]
                        sp.dma_start(piece(lay_stream, name, 4), w_br.rearrange("(k p) n -> p k n", p=P)) \
                          .then_inc(here, 16)
                    elif name.startswith("wo"):
                        j = int(name[2])
                        sp.dma_start(piece(lay_stream, name, 8), w_out2[:, :, 512 * j:512 * (j + 1)]).then_inc(here, 16)
                    elif name.startswith("up"):
                        j = int(name[2:])
                        dst = piece(lay_stream, name, 8, 2)
                        for g in range(2):
                            sp.dma_start(dst[:, :, g, :], w_up[:, :, g, 256 * j:256 * (j + 1)]).then_inc(here, 16)
                    elif name.startswith("down"):
                        j = int(name[4:])
                        sp.dma_start(piece(lay_stream, name, FT), w_down[:, :, 256 * j:256 * (j + 1)]).then_inc(here, 16)

            early = [n for n in lay_names if not lay_stream.here(n)]
            late = [n for n in lay_names if lay_stream.here(n)]
            assert lay_names[:len(early)] == early
            load_layer(0, early, None)
            with sp.Fori(0, NL - 1) as l:
                load_layer(l, late, None)
                load_layer(l + 1, early, l)
            load_layer(NL - 1, late, None)
            sp.wait_ge(S["x4"].sem, NL * S["x4"].per)
            sp.dma_start(out.rearrange("(k p) t -> p k t", p=P), xT[:, :, :]).then_inc(out_stored.sem, 16)
            sp.wait_ge(out_stored.sem, 16)

        @block.tensor
        def _(pe):
            mm = nc.tensor.matmul

            def product(outp, w, x, nk):
                for k in range(nk):
                    last = mm(outp, w(k), x(k), start=k == 0, stop=k == nk - 1)
                return last

            def opened(fills, drained, name, run=None):
                b = fills.before(name)
                if b:
                    pe.wait_ge(drained[b[0]].sem, drained[b[0]].at(b[1], run))
                return psum[fills.bank(name)]

            def halves(bank, parts=P):
                return bank[0:parts, :].rearrange("p (a b) -> p a b", a=2)

            ident = const("ident")
            pe.wait_ge(small_in.sem, 7 * 16)

            def mix(name):
                return opened(MIXFILLS, mix_drained, name)

            pe.wait_ge(sq_ready.sem, 1)
            b = mix("ss1")
            product(b[:, 0:T], lambda k: const("ones"), lambda k: sq[:, k, :], DT).then_inc(mix_full.sem, 1)

            def modulation(r):
                b = mix(f"ad{r}")
                steps = [(g, k) for g in range(4) for k in range(DT)] if r == 0 else \
                    [(g, k) for k in range(DT) for g in range(4)]
                for g, k in steps:
                    if k == 0:
                        pe.wait_ge(*mix_in.here(f"ada{4 * r + g}"))
                    last = mm(b[32 * g:32 * g + 32, :], v1("c", k).to_broadcast([P, 32]),
                              piece(mix_stream, f"ada{4 * r + g}", 8)[:, k, :], start=k == 0, stop=k == DT - 1)
                last.then_inc(mix_full.sem, 1)
                pe.wait_ge(mix_drained["act"].sem, MIXFILLS.drain[MIXFILLS.index[f"ad{r}"]][1])
                b = mix(f"at{r}")
                for i in range(4):
                    last = nc.tensor.transpose(b[:, P * i:P * (i + 1)], mod_rows[:, P * i:P * (i + 1)], ident)
                last.then_inc(mix_full.sem, 1)

            modulation(0)

            pe.wait_ge(h_ready.sem, 8)
            for name, w_name, i in (("q0", "w_q", 0), ("q1", "w_q", 1), ("kd", "w_kv", 0), ("v", "w_kv", 1),
                                    ("xr0", "w_xr", 0), ("xr1", "w_xr", 1), ("xg0", "w_xg", 0), ("xg1", "w_xg", 1)):
                pe.wait_ge(*mix_in.here(w_name))
                w = piece(mix_stream, w_name, 8)
                b = halves(mix(name))
                for a in range(2):
                    if name == "v":
                        last = product(b[:, a, 0:P], lambda k: hT[:, k, P * a:P * (a + 1)],
                                       lambda k: w[:, k, 256:384], DT)
                    else:
                        c = (2 * i + a) * P
                        last = product(b[:, a, :], lambda k: w[:, k, c:c + P], lambda k: hT[:, k, :], DT)
                last.then_inc(mix_full.sem, 1)

            pe.wait_ge(mix_drained["act"].sem, MIXFILLS.drain[MIXFILLS.index["v"]][1])
            for h in range(NH):
                b = mix(f"s{h}")
                r = slice(HD * (h % 2), HD * (h % 2) + HD)
                mm(b[:, 0:P], qT[r, h // 2, 0:P], kT[r, h // 4, 0:P], start=True, stop=True)
                mm(b[:, P:3 * P], qT[r, h // 2, P:T], kT[r, h // 4, :], start=True, stop=True) \
                    .then_inc(mix_full.sem, 1)

            modulation(1)

            pe.wait_ge(conv_ready.sem, 1)
            w = w_rg
            for g in range(2):
                for i in range(2):
                    b = halves(mix(f"rg{2 * g + i}"))
                    for a in range(2):
                        t = 2 * i + a
                        for r in (slice(0, HD), slice(HD, P)):
                            last = mm(b[r, a, :], w[r, 4 * g + t, :], xc[r, t, :], start=True, stop=True)
                    last.then_inc(mix_full.sem, 1)

            pe.wait_ge(probs_ready.sem, 1)
            for h in range(NH):
                b = mix(f"pt{h}")
                for i in range(3):
                    last = nc.tensor.transpose(b[:, P * i:P * (i + 1)], probs[:, h, P * i:P * (i + 1)], ident)
                last.then_inc(mix_full.sem, 1)
                if h % 2:
                    b = mix(f"o{h // 2}")
                    for g in (h - 1, h):
                        pe.wait_ge(mix_drained["act"].sem, MIXFILLS.drain[MIXFILLS.index[f"pt{g}"]][1])
                        r = slice(HD * (g % 2), HD * (g % 2) + HD)
                        kv = slice(HD * (g // 4), HD * (g // 4) + HD)
                        pt = pT[:, g % 2, :]
                        mm(b[r, 0:P], vtok[:, 0, kv], pt[:, 0:P], start=True, stop=True)
                        mm(b[r, P:T], vtok[:, 0, kv], pt[:, P:2 * P], start=True, stop=False)
                        last = mm(b[r, P:T], vtok[:, 1, kv], pt[:, 2 * P:3 * P], start=False, stop=True)
                    last.then_inc(mix_full.sem, 1)

            modulation(2)

            pe.wait_ge(sqm_ready.sem, 2)
            for name, o in (("ssa", 0), ("ssl", 4)):
                b = mix(name)
                product(b[:, 0:T], lambda k: const("ones"), lambda k: sqm[:, o + k, :], 4).then_inc(mix_full.sem, 1)
            pe.wait_ge(merged_ready.sem, 2)
            for i in range(4):
                pe.wait_ge(*mix_in.here(f"w_o{i // 2}"))
                w = piece(mix_stream, f"w_o{i // 2}", 8)
                b = halves(mix(f"mo{i}"))
                for a in range(2):
                    c = (2 * (i % 2) + a) * P
                    last = product(b[:, a, :], lambda k: w[:, k, c:c + P], lambda k: merged[:, k, :], DT)
                last.then_inc(mix_full.sem, 1)

            pe.wait_ge(sq_ready.sem, 2)
            b = mix("ss2")
            product(b[:, 0:T], lambda k: const("ones"), lambda k: sq[:, k, :], DT).then_inc(mix_full.sem, 1)
            pe.wait_ge(h_ready.sem, 16)
            pe.wait_ge(*mix_in.here("w_route"))
            w = piece(mix_stream, "w_route", 8)
            b = mix("rt")
            for t in range(TT):
                last = product(b[:, NE * t:NE * (t + 1)], lambda k: h2T[:, k, P * t:P * (t + 1)],
                               lambda k: w[:, k, :], DT)
            last.then_inc(mix_full.sem, 1)
            pe.wait_ge(chosen_ready.sem, 1)
            b = mix("rank")
            mm(b[:, 0:NE], const("earlier"), chosen[:, 0, :], start=True, stop=True)
            mm(b[:, NE:2 * NE], const("ones"), chosen[:, 0, :], start=True, stop=False)
            mm(b[:, NE:2 * NE], const("earlier"), chosen[:, 1, :], start=False, stop=True)
            mm(b[0:1, 64:96], const("ones", 1), chosen[:, 0, :], start=True, stop=False)
            mm(b[0:1, 64:96], const("ones", 1), chosen[:, 1, :], start=False, stop=True).then_inc(mix_full.sem, 1)
            for i in range(4):
                b = mix(f"ht{i}")
                for k in range(4):
                    last = nc.tensor.transpose(b[:, P * k:P * (k + 1)],
                                               h2T[:, 4 * (i % 2) + k, P * (i // 2):P * (i // 2 + 1)], ident)
                last.then_inc(mix_full.sem, 1)
            pe.wait_ge(gate_ready.sem, 1)
            b = mix("gT")
            for t in range(TT):
                last = nc.tensor.transpose(b[0:NE, P * t:P * (t + 1)], gate[:, t, :], ident)
            last.then_inc(mix_full.sem, 1)

            acc = [psum[4 + d // 2][:, T * (d % 2):T * (d % 2) + T] for d in range(DT)]
            pe.wait_ge(mix_drained["act"].sem, MIXFILLS.count["act"])
            pe.wait_ge(mix_drained["dve"].sem, MIXFILLS.count["dve"])
            for d in range(DT):
                mm(acc[d], b_down[:, P * d:P * (d + 1)], gateT[0:NE, :], start=d % 2 == 0, stop=False,
                   skip_group_check=True)
            pe.wait_ge(slots_ready.sem, 2)

            def gather(tile):
                for d in range(DT):
                    last = product(psum[2 + d // 4][:, P * (d % 4):P * (d % 4 + 1)],
                                   lambda t: htok[:, t, P * d:P * (d + 1)], lambda t: pick[:, t, P * tile:P * (tile + 1)], TT)
                return last

            def gather_next(e):
                pe.wait_ge(pick_ready.sem, pick_ready.at(2, e))
                gather(0).then_inc(xg_full.sem, 1)

            def expert(e, w):
                js = w // P
                hid_w = hid[:, 0:DT * w].rearrange("p (k w) -> p k w", k=DT)
                pe.wait_ge(xg_drained.sem, xg_drained.at(1, e))
                if w == T:
                    gather(1)
                for t in range(TT):
                    for j in range(js):
                        last = nc.tensor.transpose(psum[0][:, T * j + P * t:T * j + P * (t + 1)],
                                                   pickg[:, t, FEW + P * j:FEW + P * (j + 1)], ident)
                last.then_inc(sg_full.sem, 1)
                pe.wait_ge(sg_drained.sem, sg_drained.at(1, e))

                def xg_w(k):
                    return xgT[:, :, k, :] if js == 2 else xgT[:, 0, k, :]

                for s in range(4):
                    pe.wait_ge(exp_in[f"gu{s}"].sem, 2 * exp_in[f"gu{s}"].at(16, e))
                    wt = piece(exp_stream, f"gu{s}", 8, 2)
                    if w == T and s >= 2:
                        pe.wait_ge(gu_drained.sem, gu_drained.at(s - 1, e))
                    for f in range(2):
                        for g in range(2):
                            last = product(gu_out(w, s, f)[:, g, :], lambda k: wt[:, k, g, P * f:P * (f + 1)],
                                           xg_w, DT)
                            if f == 1 and g == 0:
                                last.then_inc(turned_full.sem, 1)
                    last.then_inc(gu_full.sem, 1)
                for j in range(js):
                    pe.wait_ge(gu_drained.sem, gu_drained.at(2 if w < T else 3 + j, e))
                    for k in range(DT):
                        if k % 2 == 0 and j == 0:
                            pe.wait_ge(exp_in[f"dn{k // 2}"].sem, exp_in[f"dn{k // 2}"].at(16, e))
                            pe.wait_ge(hid_ready.sem, hid_ready.at(k // 2 + 1, e))
                        wt = piece(exp_stream, f"dn{k // 2}", 2)
                        for half in range(2):
                            last = mm(psum[2 * j + half], hid_w[:, k, P * j:P * (j + 1)],
                                      wt[:, k % 2, 512 * half:512 * (half + 1)], start=k == 0, stop=k == DT - 1)
                            if k == DT - 1 and js == 1:
                                last.then_inc(y_full.sem, 1)
                        if k % 2 and k < DT - 1 and j == js - 1:
                            last.then_inc(dn_used.sem, 1)
                    if js == 2:
                        last.then_inc(y_full.sem, 1)
                if js == 2:
                    pe.wait_ge(y_drained.sem, y_drained.at(2, e))
                gather_next(e)
                for j in range(js):
                    for d in range(DT):
                        if js == 1 and d % 4 == 0:
                            pe.wait_ge(y_drained.sem, y_drained.at(1 + d // 4, e))
                        if js == 2 and d == 0:
                            pe.wait_ge(y_drained.sem, y_drained.at(1 + j, e))
                        last = mm(acc[d], y_sb[:, j, P * d:P * (d + 1)], sgT[:, j, :], start=False, stop=True,
                                  skip_group_check=True)
                last.then_inc(combined.sem, 1)

            def expert_few(e):
                both = (slice(0, FEW), slice(FEW, P))

                def gate_up(s):
                    pe.wait_ge(exp_in[f"gu{s}"].sem, 2 * exp_in[f"gu{s}"].at(16, e))
                    wt = piece(exp_stream, f"gu{s}", 8, 2)
                    for k in range(DT):
                        for f in range(2):
                            last = mm(psum[s % 2][both[f], 0:2 * P], xgT[:, 0, k, 0:FEW], wt[:, k, :, P * f:P * (f + 1)],
                                      start=k == 0, stop=k == DT - 1)
                    last.then_inc(gu_full.sem, 1)

                def turn(s):
                    pe.wait_ge(gu_taken.sem, gu_taken.at(s + 1, e))
                    if s >= 2:
                        pe.wait_ge(gu_drained.sem, gu_drained.at(s - 1, e))
                    for g in range(2):
                        last = nc.tensor.transpose(psum[2 + s % 2][:, P * g:P * (g + 1)], pre_tok[:, s % 2, g, :], ident)
                    last.then_inc(turned_full.sem, 1)

                pe.wait_ge(xg_drained.sem, xg_drained.at(1, e))
                gate_up(0)
                for s in range(1, 4):
                    gate_up(s)
                    turn(s - 1)
                for f in range(2):
                    for t in range(TT):
                        last = nc.tensor.transpose(psum[0][:, T * f + P * t:T * f + P * (t + 1)],
                                                   pickg[:, t, FEW * (1 - f):FEW * (1 - f) + P], ident)
                last.then_inc(sg_full.sem, 1)
                turn(3)
                for k in range(DT):
                    if k % 2 == 0:
                        pe.wait_ge(exp_in[f"dn{k // 2}"].sem, exp_in[f"dn{k // 2}"].at(16, e))
                        pe.wait_ge(hid_ready.sem, hid_ready.at(k // 2 + 1, e))
                    wt = piece(exp_stream, f"dn{k // 2}", 2)[:, k % 2, :].rearrange("p (c f n) -> p c f n", f=2, n=P)
                    for f in range(2):
                        last = mm(psum[1][both[f], :], hid[:, FEW * k:FEW * (k + 1)], wt[:, :, f, :],
                                  start=k == 0, stop=k == DT - 1)
                        if k == DT - 1:
                            last.then_inc(y_full.sem, 1)
                    if k % 2 and k < DT - 1:
                        last.then_inc(dn_used.sem, 1)
                gather_next(e)
                pe.wait_ge(sg_drained.sem, sg_drained.at(1, e))
                for c in range(DT // 2):
                    if c % 2 == 0:
                        pe.wait_ge(y_drained.sem, y_drained.at(1 + c // 2, e))
                    last = mm(psum[4 + c], y_sb[:, 0, P * c:P * (c + 1)], sgT.rearrange("p a b -> p (a b)"), start=False,
                              stop=True, skip_group_check=True)
                last.then_inc(combined.sem, 1)

            pe.wait_ge(pick_ready.sem, 1)
            gather(0).then_inc(xg_full.sem, 1)
            with pe.Fori(0, NE) as e:
                n = pe.value_load(counts_i[0:1, bass.ds(e, 1)], min_val=0, max_val=T)
                with pe.If(n > P):
                    expert(e, T)
                with pe.Else():
                    with pe.If(n > FEW):
                        expert(e, P)
                    with pe.Else():
                        expert_few(e)
            pe.wait_ge(xg_drained.sem, xg_drained.at(1, NE))

            pe.wait_ge(sq_ready.sem, 3)
            product(psum[0][:, 0:T], lambda k: const("ones"), lambda k: hT[:, k, :], DT).then_inc(fin_full.sem, 1)

            with pe.Fori(0, NL) as l:
                def lay(name):
                    return opened(LF, lay_drained, name, l)

                def arrived(name):
                    pe.wait_ge(*lay_in.here(name, l))

                def tiles(name, w, cols, x, nk=DT, parts=P):
                    b = halves(lay(name), parts)
                    for a in range(2):
                        c = cols + parts * a
                        last = product(b[:, a, :], lambda k: w[:, k, c:c + parts], x, nk)
                    last.then_inc(lay_full.sem, 1)

                def squares(name, ones, x, groups, parts=P):
                    b = halves(lay(name), parts)
                    for a, (o, nk) in enumerate(groups):
                        last = product(b[:, a, :], lambda k: ones, lambda k: x[0:parts, o + k, :], nk)
                    last.then_inc(lay_full.sem, 1)

                def done(sig, n=1):
                    pe.wait_ge(S[sig].sem, S[sig].at(n, l))

                def drained_act(name):
                    pe.wait_ge(lay_drained["act"].sem, lay_drained["act"].at(LF.drain[LF.index[name]][1], l))

                h = lambda k: L["h"][:, k, :]

                def gates(n):
                    if n % 3 == 0:
                        arrived(f"gate{n // 3}")
                    w = piece(lay_stream, f"gate{n // 3}", 8, 3)
                    b = halves(lay(f"ga{n}"))
                    for a in range(2):
                        last = product(b[:, a, :], lambda k: w[:, k, n % 3, P * a:P * (a + 1)], h, DT)
                    last.then_inc(lay_full.sem, 1)

                done("sq1")
                b = lay("ss1")
                product(b[:, 0:T], lambda k: const("ones"), lambda k: L["sq"][:, k, :], DT).then_inc(lay_full.sem, 1)
                done("h1")
                arrived("w_lat")
                w = piece(lay_stream, "w_lat", 8)
                tiles("cq", w, 0, h)
                b = halves(lay("ckv"))
                product(b[:, 0, :], lambda k: w[:, k, 256:384], h, DT)
                product(b[64:96, 1, :], lambda k: w[:, k, 384:416], h, DT).then_inc(lay_full.sem, 1)
                arrived("w_gq")
                w = piece(lay_stream, "w_gq", 8)
                tiles("gq0", w, 0, h)
                tiles("gq1", w, 256, h)
                arrived("w_gkv")
                w = piece(lay_stream, "w_gkv", 8)
                tiles("gk", w, 0, h)
                b = halves(lay("gv"))
                for a in range(2):
                    last = product(b[:, a, 0:P], lambda k: L["h"][:, k, P * a:P * (a + 1)],
                                   lambda k: w[:, k, 256:384], DT)
                last.then_inc(lay_full.sem, 1)
                arrived("w_pool")
                w = piece(lay_stream, "w_pool", 8)
                tiles("po0", w, 0, h)
                tiles("po1", w, 256, h)
                done("lsq")
                squares("sslat", const("ones"), L["sq"], [(0, 2), (2, 1)])
                done("gsq")
                squares("ssg0", const("pair"), L["sq"], [(3, 1), (4, 1)])
                squares("ssg1", const("pair"), L["sq"], [(5, 1), (6, 1)])
                squares("ssgk", const("pair"), L["p"].rearrange("p a b -> p (a b)").rearrange("p (a b) -> p a b", b=T),
                        [(0, 1), (1, 1)])
                gates(0)
                gates(1)
                done("lat")
                arrived("w_uq")
                w = piece(lay_stream, "w_uq", 2)
                for i in range(4):
                    tiles(f"uq{i}", w, 2 * MQ * i, lambda k: L["cq"][:, k, :], 2, MQ)
                arrived("w_ukv")
                w = piece(lay_stream, "w_ukv", 8)
                for i in range(4):
                    b = halves(lay(f"uk{i}"))
                    for a in range(2):
                        last = mm(b[0:HD, a, :], w[:, 2 * i + a, 0:HD], L["ckv"], start=True, stop=True)
                    last.then_inc(lay_full.sem, 1)
                for t in range(TT):
                    b = lay(f"uv{t}")
                    mm(b[:, :].rearrange("p (a b) -> p a b", a=NH), L["ckv"][:, P * t:P * (t + 1)], w[:, :, HD:P],
                       start=True, stop=True).then_inc(lay_full.sem, 1)
                done("gn")
                for i in range(2):
                    tiles_of(lay(f"swg{i}"), const("swap_g"), L["gq"], 2 * i, P).then_inc(lay_full.sem, 1)
                tiles_of(lay("swgk"), const("swap_g"), L["gk"], 0, P).then_inc(lay_full.sem, 1)
                arrived("pool_w")
                done("mixed")
                w = piece(lay_stream, "pool_w", 4)
                for i in range(2):
                    b = halves(lay(f"pl{i}"))
                    for a in range(2):
                        last = mm(b[:, a, :], w[:, 2 * i + a, :], L["pool"][:, 2 * i + a, PAD:PAD + T],
                                  start=True, stop=True)
                    last.then_inc(lay_full.sem, 1)
                gates(2)
                done("qsq")
                for i in range(4):
                    squares(f"ssq{i}", const("ones")[0:MQ, 0:MQ], L["sq"], [(2 * i, 1), (2 * i + 1, 1)], MQ)
                gates(3)
                gates(4)
                done("ksq")
                for i in range(4):
                    squares(f"ssk{i}", const("ones")[0:MQ, 0:MQ], L["sq"], [(2 * i, 1), (2 * i + 1, 1)], MQ)
                gates(5)
                gates(6)
                done("qn")
                for i in range(4):
                    tiles_of(lay(f"swq{i}"), const("swap_m")[0:MQ, 0:MQ], L["mq"], 2 * i, MQ).then_inc(lay_full.sem, 1)
                done("kn")
                for i in range(4):
                    tiles_of(lay(f"swk{i}"), const("swap_m")[0:MQ, 0:MQ], L["mk"], 2 * i, MQ).then_inc(lay_full.sem, 1)
                gates(7)
                for i in range(2 * NH + 3):
                    if i < 2 * NH:
                        if i == 0:
                            done("rope_g")
                        if i == NH:
                            done("rope_m")
                        name = att[i]
                        n = int(name[1])
                        b = halves(lay(f"s_{name}"))
                        if name[0] == "m":
                            q, k = L["mq"][0:MQ, n, :], L["mk"][0:MQ, n, :]
                        else:
                            r = slice(HD * (n % 2), HD * (n % 2) + HD)
                            q, k = L["gq"][r, n // 2, :], L["gk"][r, n // 4, :]
                        for a in range(2):
                            last = mm(b[:, a, :], q[:, P * a:P * (a + 1)], k, start=True, stop=True)
                        last.then_inc(lay_full.sem, 1)
                    if 2 <= i < 2 * NH + 2:
                        done("pnorm", i - 1)
                        b = lay(f"t_{att[i - 2]}")
                        pr = L["p"][:, (i - 2) % 3, :].rearrange("p (a b) -> p a b", a=2)
                        for st in range(2):
                            for a in range(2):
                                last = nc.tensor.transpose(b[:, T * st + P * a:T * st + P * (a + 1)],
                                                           pr[:, a, P * st:P * (st + 1)], ident)
                        last.then_inc(lay_full.sem, 1)
                    if i < 4:
                        gates(i + 8)
                    if i >= 4 and i % 2 == 0:
                        b = lay(f"o_{att[i - 4]}")
                        for g in (i - 4, i - 3):
                            drained_act(f"t_{att[g]}")
                            n = int(att[g][1])
                            r = slice(HD * (n % 2), HD * (n % 2) + HD)
                            for st in range(2):
                                v = L["mv"][:, st, HD * n:HD * (n + 1)] if att[g][0] == "m" else \
                                    L["gv"][:, st, HD * (n // 4):HD * (n // 4 + 1)]
                                last = mm(b[r, 0:T], v, L["pT"][:, g % 4, T * st:T * (st + 1)],
                                          start=st == 0, stop=st == 1)
                        last.then_inc(lay_full.sem, 1)
                pe.wait_ge(lay_drained["dve"].sem, lay_drained["dve"].at(LF.drain[LF.index["pl1"]][1], l))
                drained_act(f"o_{att[2 * NH - 2]}")
                for b_ in range(3):
                    arrived(f"br{b_}")
                for i in range(4):
                    for br in range(3):
                        tiles(f"br{i}{br}", piece(lay_stream, f"br{br}", 4), 2 * P * i, lambda k: L["o"][:, br, k, :], 4)
                done("merged", 4)
                for i in range(4):
                    if i % 2 == 0:
                        arrived(f"wo{i // 2}")
                    tiles(f"wo{i}", piece(lay_stream, f"wo{i // 2}", 8), 2 * P * (i % 2), lambda k: merged2[:, k, :])
                b = lay("ss2")
                for k in range(DT):
                    if k % 2 == 0:
                        done("sq2", k // 2 + 1)
                    last = mm(b[:, 0:T], const("ones"), L["sq"][:, k, :], start=k == 0, stop=k == DT - 1)
                last.then_inc(lay_full.sem, 1)
                for f in range(FT):
                    done("wlo", f + 1)
                    _, _, hi, lo, _ = unit(f)
                    b = halves(lay(f"up{f}"))
                    for g in range(2):
                        for k in range(DT):
                            if f == 0 and g == 0 and k % 4 == 0:
                                done("h2", k // 4 + 1)
                            wh, wl = hi[:, 2 * k + g, :], lo[:, 2 * k + g, :]
                            mm(b[:, g, :], wh, h_hi[:, k, :], start=k == 0, stop=False)
                            mm(b[:, g, :], wh, h_lo[:, k, :], start=False, stop=False)
                            last = mm(b[:, g, :], wl, h_hi[:, k, :], start=False, stop=k == DT - 1)
                    last.then_inc(lay_full.sem, 1)
                for i in range(4):
                    b = halves(lay(f"dn{i}"))
                    for c in range(3):
                        if i == 0:
                            done("flo", min(DN_K * (c + 1), FT))
                        done("wlo", FT + 3 * i + c + 1)
                        _, _, hi, lo, _ = unit(FT + 3 * i + c)
                        for q in range(hi.shape[1]):
                            k = DN_K * c + q
                            for a in range(2):
                                wh, wl = hi[:, q, P * a:P * (a + 1)], lo[:, q, P * a:P * (a + 1)]
                                mm(b[:, a, :], wh, f_hi[:, k, :], start=k == 0 and a == 0, stop=False, skip_group_check=True)
                                mm(b[:, a, :], wh, f_lo[:, k, :], start=False, stop=False, skip_group_check=True)
                                last = mm(b[:, a, :], wl, f_hi[:, k, :], start=False, stop=k == FT - 1,
                                          skip_group_check=True)
                        last.then_inc(S["wused"].sem if c < 2 else lay_full.sem, 1)

        @block.scalar
        def _(act):
            f = nc.scalar.activation
            act.wait_ge(small_in.sem, 7 * 16)


            def full(name):
                act.wait_ge(mix_full.sem, MIXFILLS.full(name))
                return psum[MIXFILLS.bank(name)]

            def out_of(name, dst, src=None, func=ACT.Copy, **kw):
                b = full(name)
                f(dst, b[:, :].rearrange("p (a b) -> p a b", a=2) if src is None else src(b), func, **kw) \
                    .then_inc(mix_drained["act"].sem, 1)

            f(sq[:, :, :], xT[:, :, :], ACT.Square).then_inc(sq_ready.sem, 1)
            act.wait_ge(var_ready.sem, 1)
            f(rstd[:, 0, :], rstd[:, 0, :], ACT.Sqrt).then_inc(std_ready.sem, 1)
            act.wait_ge(lam_exp_in.sem, 1)
            f(small[:, 4:8], small[:, 0:4], ACT.Exp, scale=-1.0).then_inc(lam_exp.sem, 1)
            out_of("ad0", mod_rows, lambda b: b)
            out_of("q0", qT[:, 0:2, :])
            out_of("q1", qT[:, 2:4, :])
            out_of("kd", kT)
            out_of("v", vtok, lambda b: b[:, :].rearrange("p (a b) -> p a b", a=2)[:, :, 0:P])
            out_of("xr0", xr[:, 0:2, 3:3 + T])
            out_of("xr1", xr[:, 2:4, 3:3 + T])
            act.wait_ge(mix_drained["act"].sem, MIXFILLS.drain[MIXFILLS.index["xr1"]][1])
            for t in range(4):
                ins = f(xc[:, t, :], xr[:, t, 3:3 + T], ACT.Identity, scale=v1("conv_w", 4 * t + 3), bias=v1("conv_b", t))
            ins.then_inc(conv_base.sem, 1)
            out_of("xg0", xg[:, 0:2, :])
            out_of("xg1", xg[:, 2:4, :])
            act.wait_ge(negmax_ready.sem, 1)
            f(stat[:, 3, :, :], stat[:, 3, :, :], ACT.Exp)
            for h in range(NH):
                for blk, (c0, c1) in enumerate(((0, P), (P, 3 * P))):
                    ins = f(probs[:, h, c0:c1], probs[:, h, c0:c1], ACT.Exp, bias=stat[:, 1, blk, h:h + 1],
                            accum_out=stat[:, 2, blk, h:h + 1])
            ins.then_inc(exp_ready.sem, 1)
            out_of("ad1", mod_rows, lambda b: b)
            for g, (dst, bias) in enumerate(((lru_a, "b_rg_a"), (lru_u, "b_rg_x"))):
                for i in range(2):
                    b = full(f"rg{2 * g + i}")
                    f(dst[:, 2 * i, :], b[:, 0:T], ACT.Sigmoid, bias=v1(bias, 2 * i))
                    f(dst[:, 2 * i + 1, :], b[:, T:2 * T], ACT.Sigmoid, bias=v1(bias, 2 * i + 1)) \
                        .then_inc(mix_drained["act"].sem, 1)
            act.wait_ge(mix_drained["act"].sem, MIXFILLS.drain[MIXFILLS.index["rg3"]][1])
            act.wait_ge(decay_ready.sem, 1)
            for t in range(4):
                ins = f(lru_t[:, t, :], lru_a[:, t, :], ACT.Tanh, scale=decay[:, t:t + 1])
            ins.then_inc(tanh_ready.sem, 1)
            for h in range(NH):
                b = full(f"pt{h}")
                f(pT[:, h % 2, :], b[:, 0:384], ACT.Copy).then_inc(mix_drained["act"].sem, 1)
                if h % 2:
                    out_of(f"o{h // 2}", attnT[:, h // 2, :], lambda b: b[:, 0:T])
            act.wait_ge(gel_poly.sem, 1)
            f(gel, gel, ACT.Tanh, scale=0.7978845608028654).then_inc(gel_tanh.sem, 1)
            act.wait_ge(loga_ready.sem, 1)
            f(lru_t, lru_t, ACT.Sqrt).then_inc(sqrt_ready.sem, 1)
            out_of("ad2", mod_rows, lambda b: b)
            act.wait_ge(lru_ready.sem, 1)
            act.wait_ge(mix_drained["act"].sem, MIXFILLS.drain[MIXFILLS.index["o3"]][1])
            f(sqm[:, 0:4, :], attnT, ACT.Square).then_inc(sqm_ready.sem, 1)
            f(sqm[:, 4:8, :], lru_a, ACT.Square).then_inc(sqm_ready.sem, 1)
            act.wait_ge(varm_ready.sem, 1)
            f(rstd, rstd, ACT.Sqrt).then_inc(stdm_ready.sem, 1)
            act.wait_ge(x1_ready.sem, 1)
            f(sq[:, :, :], xT[:, :, :], ACT.Square).then_inc(sq_ready.sem, 1)
            act.wait_ge(var_ready.sem, 2)
            f(rstd[:, 0, :], rstd[:, 0, :], ACT.Sqrt).then_inc(std_ready.sem, 1)
            act.wait_ge(top_ready.sem, 2)
            for t in range(TT):
                f(gexp[:, t, :], top8[:, t, 0:TOPK], ACT.Exp, bias=ntop[:, t, :], accum_out=gsum[:, t, 0:1]) \
                    .then_inc(gate_exp.sem, 1)
            for i in range(4):
                out_of(f"ht{i}", htok[:, i // 2, 512 * (i % 2):512 * (i % 2 + 1)], lambda b: b[:, :])
            b = full("gT")
            f(gateT[0:NE, :], b[0:NE, 0:T], ACT.Copy).then_inc(mix_drained["act"].sem, 1)

            act.wait_ge(slots_ready.sem, 2)

            def gathered(e):
                act.wait_ge(xg_full.sem, xg_full.at(1, e))
                for i in range(2):
                    ins = f(xgT[:, 0, 4 * i:4 * i + 4, :], psum[2 + i].rearrange("p (a b) -> p a b", a=4), ACT.Copy)
                ins.then_inc(xg_drained.sem, 1)

            def expert(e, w):
                js = w // P
                for s in range(4):
                    act.wait_ge(pre_ready.sem, pre_ready.at(s + 1, e))
                    o = 512 * (s % 2)
                    f(act_s[:, o:o + w], act_g[:, o:o + w], ACT.Sigmoid, scale=ALPHA).then_inc(gu_taken.sem, 1)
                    f(act_s[:, o + w:o + 2 * w], act_g[:, o + w:o + 2 * w], ACT.Sigmoid, scale=ALPHA) \
                        .then_inc(sig_ready.sem, 1)
                for j in range(js):
                    if js == 2:
                        act.wait_ge(y_full.sem, y_full.at(j + 1, e))
                    for half in range(2):
                        if js == 1:
                            act.wait_ge(y_full.sem, y_full.at(half + 1, e))
                        ins = f(y_sb[:, j, 512 * half:512 * (half + 1)], psum[2 * j + half], ACT.Copy)
                        if js == 1:
                            ins.then_inc(y_drained.sem, 1)
                    if js == 2:
                        ins.then_inc(y_drained.sem, 1)

            def expert_few(e):
                def gates(s):
                    act.wait_ge(pre_ready.sem, pre_ready.at(s + 1, e))
                    o = 512 * (s % 2)
                    f(act_s[:, o:o + 2 * FEW], act_g[:, o:o + 2 * FEW], ACT.Sigmoid, scale=ALPHA).then_inc(sig_ready.sem, 1)

                for s in range(4):
                    act.wait_ge(gu_full.sem, gu_full.at(s + 1, e))
                    if s >= 2:
                        act.wait_ge(turned_full.sem, turned_full.at(s - 1, e))
                    f(pre_tok[:, s % 2, :, :], psum[s % 2][:, 0:2 * P].rearrange("p (a b) -> p a b", a=2), ACT.Copy) \
                        .then_inc(gu_taken.sem, 1)
                    if s:
                        gates(s - 1)
                gates(3)
                act.wait_ge(y_full.sem, y_full.at(2, e))
                for half in range(2):
                    f(y_sb[:, 0, T * half:T * (half + 1)], psum[1][:, T * half:T * (half + 1)], ACT.Copy) \
                        .then_inc(y_drained.sem, 1)

            gathered(0)
            with act.Fori(0, NE) as e:
                n = act.value_load(counts_i[0:1, bass.ds(e, 1)], min_val=0, max_val=T)
                with act.If(n > P):
                    expert(e, T)
                with act.Else():
                    with act.If(n > FEW):
                        expert(e, P)
                    with act.Else():
                        expert_few(e)
                gathered(e + 1)

            act.wait_ge(x2_ready.sem, 8)
            f(hT, xT[:, :, :], ACT.Square).then_inc(sq_ready.sem, 1)
            act.wait_ge(var_ready.sem, 3)
            f(rstd[:, 0, :], rstd[:, 0, :], ACT.Sqrt).then_inc(std_ready.sem, 1)
            act.wait_ge(xin_ready.sem, 8)

            with act.Fori(0, NL) as l:

                def full(name):
                    act.wait_ge(lay_full.sem, lay_full.at(LF.full(name), l))
                    return psum[LF.bank(name)]

                def own(name):
                    act.wait_ge(lay_drained["act"].sem, lay_drained["act"].at(LF.drain[LF.index[name]][1], l))

                def out_of(name, dst, src=None, func=ACT.Copy, **kw):
                    b = full(name)
                    f(dst, b[:, :].rearrange("p (a b) -> p a b", a=2) if src is None else src(b), func, **kw) \
                        .then_inc(lay_drained["act"].sem, 1)

                def ready(sig, n=1):
                    act.wait_ge(S[sig].sem, S[sig].at(n, l))

                def two(b):
                    return b.rearrange("p (a b) -> p a b", a=2)

                def gates(n):
                    o = 8 * (n % 3) + 2 * (n // 3)
                    out_of(f"ga{n}", L["gates"][:, o:o + 2, :], func=ACT.Tanh, scale=0.5)

                ready("vecs")
                f(L["sq"], xT[:, :, :], ACT.Square).then_inc(S["sq1"].sem, 1)
                ready("var1")
                f(L["rs"][:, 0, :], L["rs"][:, 0, :], ACT.Sqrt).then_inc(S["std1"].sem, 1)
                out_of("cq", L["cq"])
                b = full("ckv")
                f(L["ckv"], b[:, 0:T], ACT.Copy)
                f(L["krope"][64:96, :], b[64:96, T:2 * T], ACT.Copy).then_inc(lay_drained["act"].sem, 1)
                out_of("gq0", L["gq"][:, 0:2, :])
                out_of("gq1", L["gq"][:, 2:4, :])
                out_of("gk", L["gk"])
                out_of("gv", L["gv"], lambda b: two(b)[:, :, 0:P])
                out_of("po0", L["pool"][:, 0:2, PAD:PAD + T])
                out_of("po1", L["pool"][:, 2:4, PAD:PAD + T])
                ready("lvar")
                f(L["rs"][:, 0:2, :], L["rs"][:, 0:2, :], ACT.Sqrt).then_inc(S["lstd"].sem, 1)
                ready("gvar")
                f(L["rs"][:, 2:8, :], L["rs"][:, 2:8, :], ACT.Sqrt).then_inc(S["gstd"].sem, 1)
                gates(0)
                gates(1)
                for i in range(4):
                    out_of(f"uq{i}", L["mq"][0:MQ, 2 * i:2 * i + 2, :], lambda b: two(b)[0:MQ])
                for i in range(4):
                    out_of(f"uk{i}", L["mk"][0:HD, 2 * i:2 * i + 2, :], lambda b: two(b)[0:HD])
                own("ckv")
                f(L["mk"][64:96, :, :], L["krope"][64:96, :].unsqueeze(1).to_broadcast([32, NH, T]), ACT.Copy) \
                    .then_inc(S["krope"].sem, 1)
                own("uq3")
                f(L["sq"][0:MQ], L["mq"][0:MQ], ACT.Square).then_inc(S["qsq"].sem, 1)
                for t in range(TT):
                    out_of(f"uv{t}", L["mv"][:, t, :], lambda b: b)
                gates(2)
                ready("qvar")
                f(L["rs"][0:MQ], L["rs"][0:MQ], ACT.Sqrt).then_inc(S["qstd"].sem, 1)
                full("ssq3")
                ready("krope")
                own("uk3")
                f(L["sq"][0:MQ], L["mk"][0:MQ], ACT.Square).then_inc(S["ksq"].sem, 1)
                gates(3)
                gates(4)
                ready("kvar")
                f(L["rs"][0:MQ], L["rs"][0:MQ], ACT.Sqrt).then_inc(S["kstd"].sem, 1)
                gates(5)
                gates(6)
                gates(7)
                for i in range(2 * NH + 3):
                    if i < 2 * NH:
                        b = two(full(f"s_{att[i]}"))
                        ready("nmax", i + 1)
                        scale = (MQ if att[i][0] == "m" else HD) ** -0.5
                        st = L["stat"][:, i % 3, :]
                        pr = two(L["p"][:, i % 3, :])
                        f(pr[:, 0, :], b[:, 0, :], ACT.Exp, scale=scale, bias=st[:, 2:3], accum_out=st[:, 4:5])
                        f(pr[:, 1, :], b[:, 1, :], ACT.Exp, scale=scale, bias=st[:, 3:4], accum_out=st[:, 5:6]) \
                            .then_inc(lay_drained["act"].sem, 1)
                    if 2 <= i < 2 * NH + 2:
                        out_of(f"t_{att[i - 2]}", L["pT"][:, (i - 2) % 4, :], lambda b: b)
                    if i < 4:
                        gates(i + 8)
                    if i >= 4 and i % 2 == 0:
                        n = int(att[i - 4][1])
                        out_of(f"o_{att[i - 4]}", L["o"][:, 0 if att[i - 4][0] == "m" else 1, n // 2, :],
                               lambda b: b[:, 0:T])
                for i in range(4):
                    act.wait_ge(lay_drained["dve"].sem, lay_drained["dve"].at(LF.drain[LF.index[f"wo{i}"]][1], l))
                    f(L["sq"][:, 2 * i:2 * i + 2, :], xT[:, 2 * i:2 * i + 2, :], ACT.Square).then_inc(S["sq2"].sem, 1)

                def leading(n):
                    name, src, hi, _, free = unit(n)
                    act.wait_ge(*lay_in.here(name, l))
                    act.wait_ge(free[0].sem, free[0].at(free[1], l))
                    f(hi, src, ACT.Copy).then_inc(S["whi"].sem, 1)

                leading(0)
                ready("var2")
                f(L["rs"][:, 0, :], L["rs"][:, 0, :], ACT.Sqrt).then_inc(S["std2"].sem, 1)

                for i in range(2):
                    ready("hfull", i + 1)
                    f(h_hi[:, 4 * i:4 * i + 4, :], h_full[:, 4 * i:4 * i + 4, :], ACT.Copy).then_inc(S["hhi"].sem, 1)
                leading(1)
                for ft in range(FT + 2):
                    if ft < FT:
                        leading(ft + 2)
                        b = two(full(f"up{ft}"))
                        if ft >= 4:
                            ready("ffact", ft - 3)
                        for g in range(2):
                            c = g * FT + ft
                            ins = f(conv_t[:, 2 * (ft % 4) + g, :], b[:, g, :], ACT.Identity,
                                    scale=v2("conv_w", 2 * FT + c), bias=v2("conv_b", c))
                        ins.then_inc(S["vals"].sem, 1)
                    if 1 <= ft <= FT:
                        ready("conv", ft)
                        f(silu_t[:, (ft - 1) % 4, :], conv_t[:, 2 * ((ft - 1) % 4), :], ACT.Silu).then_inc(S["silu"].sem, 1)
                    if ft >= 2:
                        ready("ffact", ft - 1)
                        f(f_hi[:, ft - 2, :], ff_t[:, (ft - 2) % 4, :], ACT.Copy).then_inc(S["fhi"].sem, 1)
                for n in range(FT + 2, FT + 12):
                    leading(n)

        @block.vector
        def _(dve):
            v = nc.vector
            dve.wait_ge(small_in.sem, 7 * 16)
            d = Chain(dve, d_chain)

            def full(name):
                dve.wait_ge(mix_full.sem, MIXFILLS.full(name))
                return psum[MIXFILLS.bank(name)]

            def taken(ins):
                ins.then_inc(mix_drained["dve"].sem, 1)

            def own(name):
                dve.wait_ge(mix_drained["dve"].sem, MIXFILLS.drain[MIXFILLS.index[name]][1])

            def variance(name, dst, n, ready):
                taken(v.tensor_scalar(dst, full(name)[:, 0:T], 1.0 / n, EPS, ALU.mult, ALU.add))
                own(name)
                v.reciprocal(dst, dst).then_inc(ready.sem, 1)

            d.step(v.tensor_scalar(small[:, 0:4], v1("lam"), -1.0, None, ALU.mult))
            v.tensor_tensor(small[:, 0:4], small[:, 0:4], v1("lam"), ALU.max).then_inc(lam_exp_in.sem, 1)
            variance("ss1", rstd[:, 0, :], D, var_ready)
            e4, s4, z4, p4 = small[:, 4:8], small[:, 8:12], small[:, 12:16], small[:, 16:20]
            dve.wait_ge(lam_exp.sem, 1)
            d.step(v.tensor_scalar(s4, e4, 2.0, None, ALU.add))
            d.step(v.reciprocal(s4, s4))
            d.step(v.tensor_tensor(s4, s4, e4, ALU.mult))
            d.step(v.tensor_tensor(z4, s4, s4, ALU.mult))
            d.step(v.tensor_scalar(p4, z4, 1.0 / 17, 1.0 / 15, ALU.mult, ALU.add))
            for k in range(13, 0, -2):
                d.step(v.tensor_tensor(p4, p4, z4, ALU.mult))
                d.step(v.tensor_scalar(p4, p4, 1.0 / k, None, ALU.add))
            d.step(v.tensor_tensor(p4, p4, s4, ALU.mult))
            d.step(v.tensor_scalar(z4, v1("lam"), -1.0, 0.0, ALU.mult, ALU.max))
            d.step(v.scalar_tensor_tensor(out=p4, in0=p4, scalar=2.0, in1=z4, op0=ALU.mult, op1=ALU.add))
            v.tensor_scalar(decay, p4, 4.0, None, ALU.mult).then_inc(decay_ready.sem, 1)

            def modulation(r):
                b = full(f"at{r}").rearrange("p (b g n) -> p g b n", b=4, g=4)[:, :, :, 0]
                taken(v.tensor_tensor(modT[:, 16 * r:16 * r + 16].rearrange("p (g b) -> p g b", g=4), b,
                                      v1("b_ada")[:, 16 * r:16 * r + 16].rearrange("p (g b) -> p g b", g=4), ALU.add))

            def modulated(scale, shift, dst, r, ready):
                for k in range(DT):
                    d.mark(v.scalar_tensor_tensor(out=dst[:, k, :], in0=xT[:, k, :], scalar=scale[:, k:k + 1], in1=r,
                                                  op0=ALU.mult, op1=ALU.mult))
                d.settle()
                for k in range(DT):
                    v.tensor_scalar(dst[:, k, :], dst[:, k, :], modT[:, shift + k:shift + k + 1], None, ALU.add) \
                        .then_inc(ready.sem, 1)

            modulation(0)
            own("at0")
            d.step(v.scalar_tensor_tensor(out=scale1, in0=modT[:, 8:16], scalar=1.0, in1=v1("g_mix"),
                                          op0=ALU.add, op1=ALU.mult))
            dve.wait_ge(std_ready.sem, 1)
            modulated(scale1, 0, hT, rstd[:, 0, :], h_ready)

            for h in range(NH):
                b = full(f"s{h}")
                taken(v.scalar_tensor_tensor(out=probs[:, h, :], in0=b[:, 0:384], scalar=HD ** -0.5, in1=const("band"),
                                             op0=ALU.mult, op1=ALU.add))
            own(f"s{NH - 1}")
            d.mark(v.tensor_reduce(stat[:, 0, 0, :], probs[:, :, 0:P], AX.X, ALU.max))
            d.step(v.tensor_reduce(stat[:, 0, 1, :], probs[:, :, P:3 * P], AX.X, ALU.max))
            sinks = v1("sinks").unsqueeze(1).to_broadcast([P, 2, NH])
            d.step(v.tensor_tensor(stat[:, 0, :, :], stat[:, 0, :, :], sinks, ALU.max))
            d.mark(v.tensor_scalar(stat[:, 1, :, :], stat[:, 0, :, :], -1.0, None, ALU.mult))
            v.tensor_tensor(stat[:, 3, :, :], sinks, stat[:, 0, :, :], ALU.subtract).then_inc(negmax_ready.sem, 1)
            dve.wait_ge(conv_base.sem, 1)
            dve.wait_ge(zeroed.sem, 1)
            for j in range(3):
                for t in range(4):
                    ins = v.scalar_tensor_tensor(out=xc[:, t, :], in0=xr[:, t, j:j + T], scalar=v1("conv_w", 4 * t + j),
                                                 in1=xc[:, t, :], op0=ALU.mult, op1=ALU.add)
                    if j == 2 and t == 3:
                        ins.then_inc(conv_ready.sem, 1)
                    else:
                        d.mark(ins)
                if j < 2:
                    d.settle()
            dve.wait_ge(exp_ready.sem, 1)
            d.step(v.tensor_tensor(stat[:, 4, :, :], stat[:, 2, :, :], stat[:, 3, :, :], ALU.add))
            d.step(v.reciprocal(stat[:, 5, :, :], stat[:, 4, :, :]))
            d.mark(v.tensor_tensor(probs[:, :, 0:P], probs[:, :, 0:P],
                                   stat[:, 5, 0, :].unsqueeze(2).to_broadcast([P, NH, P]), ALU.mult))
            v.tensor_tensor(probs[:, :, P:3 * P], probs[:, :, P:3 * P],
                            stat[:, 5, 1, :].unsqueeze(2).to_broadcast([P, NH, T]), ALU.mult).then_inc(probs_ready.sem, 1)
            full("xg1")
            dve.wait_ge(mix_drained["act"].sem, MIXFILLS.drain[MIXFILLS.index["xg1"]][1])
            d.step(v.tensor_tensor(gel, xg, xg, ALU.mult))
            d.step(v.tensor_scalar(gel, gel, 0.044715, 1.0, ALU.mult, ALU.add))
            v.tensor_tensor(gel, gel, xg, ALU.mult).then_inc(gel_poly.sem, 1)
            modulation(1)
            dve.wait_ge(tanh_ready.sem, 1)
            d.step(v.tensor_scalar(lru_d, lru_t, 1.0, None, ALU.add))
            d.mark(v.reciprocal(lru_d, lru_d))
            d.step(v.tensor_scalar(lru_a, lru_t, -1.0, 1.0, ALU.mult, ALU.add))
            v.tensor_tensor(lru_a, lru_a, lru_d, ALU.mult).then_inc(loga_ready.sem, 1)
            d.step(v.tensor_tensor(lru_u, lru_u, xc, ALU.mult))
            d.step(v.tensor_tensor(lru_u, lru_u, lru_d, ALU.mult))
            dve.wait_ge(sqrt_ready.sem, 1)
            d.step(v.scalar_tensor_tensor(out=lru_u, in0=lru_t, scalar=2.0, in1=lru_u, op0=ALU.mult, op1=ALU.mult))
            dve.wait_ge(loga_ready.sem, 1)
            for t in range(4):
                d.mark(v.tensor_tensor_scan(lru_h[:, t, :], lru_a[:, t, :], lru_u[:, t, :], 0.0, ALU.mult, ALU.add))
            dve.wait_ge(gel_tanh.sem, 1)
            d.step(v.scalar_tensor_tensor(out=gel, in0=gel, scalar=1.0, in1=xg, op0=ALU.add, op1=ALU.mult))
            v.scalar_tensor_tensor(out=lru_a, in0=lru_h, scalar=0.5, in1=gel, op0=ALU.mult, op1=ALU.mult) \
                .then_inc(lru_ready.sem, 1)
            modulation(2)
            for i, name in enumerate(("ssa", "ssl")):
                taken(v.tensor_scalar(rstd[:, i, :], full(name)[:, 0:T], 1.0 / 512, EPS, ALU.mult, ALU.add))
            own("ssl")
            v.reciprocal(rstd, rstd).then_inc(varm_ready.sem, 1)
            d.step(v.scalar_tensor_tensor(out=scale2, in0=modT[:, 32:40], scalar=1.0, in1=v1("g_ffn"),
                                          op0=ALU.add, op1=ALU.mult))
            dve.wait_ge(stdm_ready.sem, 1)
            dve.wait_ge(lru_ready.sem, 1)
            for half, (src, g) in enumerate(((attnT, "g_attn"), (lru_a, "g_lru"))):
                for t in range(4):
                    ins = v.scalar_tensor_tensor(out=merged[:, 4 * half + t, :], in0=src[:, t, :], scalar=v1(g, t),
                                                 in1=rstd[:, half, :], op0=ALU.mult, op1=ALU.mult)
                ins.then_inc(merged_ready.sem, 1)
            for i in range(4):
                b = full(f"mo{i}")
                for a in range(2):
                    k = 2 * i + a
                    ins = v.scalar_tensor_tensor(out=xT[:, k, :], in0=b[:, T * a:T * (a + 1)],
                                                 scalar=modT[:, 16 + k:17 + k], in1=xT[:, k, :],
                                                 op0=ALU.mult, op1=ALU.add)
                    if a:
                        taken(ins)
                    else:
                        d.mark(ins)
            own("mo3")
            v.tensor_copy(small[:, 20:21], rstd[:, 0, 0:1]).then_inc(x1_ready.sem, 1)
            variance("ss2", rstd[:, 0, :], D, var_ready)
            dve.wait_ge(std_ready.sem, 2)
            modulated(scale2, 24, h2T, rstd[:, 0, :], h_ready)
            b = full("rt")
            taken(v.tensor_tensor(lg, b[:, 0:2 * NE].rearrange("p (a b) -> p a b", a=2),
                                  v1("b_router").unsqueeze(1).to_broadcast([P, TT, NE]), ALU.add))
            own("rt")
            for t in range(TT):
                d.mark(v.max(top8[:, t, :], lg[:, t, :]))
            d.mark(v.memset(chosen, 0.0))
            d.mark(v.memset(slot, -1.0))
            d.settle()
            for t in range(TT):
                v.tensor_scalar(ntop[:, t, :], top8[:, t, 0:1], -1.0, None, ALU.mult).then_inc(top_ready.sem, 1)
            for t in range(TT):
                d.mark(v.max_index(place[:, t, :].bitcast(U32), top8[:, t, :], lg[:, t, :]))
            d.settle()
            for t in range(TT):
                d.mark(v.tensor_copy(placef[:, t, :], place[:, t, :].bitcast(U32)))
            d.settle()
            for k in range(TOPK):
                for t in range(TT):
                    ins = v.scalar_tensor_tensor(out=chosen[:, t, :], in0=const("experts"), scalar=placef[:, t, k:k + 1],
                                                 in1=chosen[:, t, :], op0=ALU.is_equal, op1=ALU.add)
                    if k == TOPK - 1 and t == TT - 1:
                        ins.then_inc(chosen_ready.sem, 1)
                    else:
                        d.mark(ins)
                if k < TOPK - 1:
                    d.settle()
            dve.wait_ge(gate_exp.sem, 2)
            for t in range(TT):
                d.mark(v.reciprocal(gsum[:, t, 1:2], gsum[:, t, 0:1]))
            d.settle()
            for t in range(TT):
                d.mark(v.tensor_scalar(gexp[:, t, :], gexp[:, t, :], gsum[:, t, 1:2], None, ALU.mult))
            d.settle()
            for k in range(TOPK):
                for t in range(TT):
                    d.mark(v.tensor_scalar(onehot[:, t, :] if k else gate[:, t, :], const("experts"),
                                           placef[:, t, k:k + 1], gexp[:, t, k:k + 1], ALU.is_equal, ALU.mult))
                d.settle()
                if k:
                    ins = v.tensor_tensor(gate, gate, onehot, ALU.add)
                    if k == TOPK - 1:
                        ins.then_inc(gate_ready.sem, 1)
                    else:
                        d.step(ins)
            b = full("rank")
            d.step(v.scalar_tensor_tensor(out=slot[:, :, 0:NE], in0=b[:, 0:2 * NE].rearrange("p (a b) -> p a b", a=2),
                                          scalar=1.0, in1=chosen, op0=ALU.add, op1=ALU.mult))
            taken(v.tensor_copy(counts_i[0:1, 0:NE], b[0:1, 64:96]))
            v.tensor_scalar(slot[:, :, 0:NE], slot[:, :, 0:NE], -1.0, None, ALU.add).then_inc(slots_ready.sem, 1)
            own("rank")
            dve.wait_ge(slots_ready.sem, 1)
            dve.wait_ge(gate_ready.sem, 1)
            v.tensor_copy(small_done, gsum[:, 0, 0:1]).then_inc(slots_ready.sem, 1)

            def select(e):
                for t in range(TT):
                    v.tensor_scalar(pick[:, t, :], const("slots"), slot[:, t, bass.ds(e, 1)], None, ALU.is_equal)
                for t in range(TT):
                    ins = v.tensor_scalar(pickg[:, t, FEW:FEW + T], const("slots"), slot[:, t, bass.ds(e, 1)],
                                          gate_of[:, t, bass.ds(e, 1)], ALU.is_equal, ALU.mult)
                return ins

            v.memset(pickg[:, :, 0:FEW], 0.0)
            select(0).then_inc(pick_ready.sem, 1)

            def expert(e, w):
                c = Chain(dve, e_chain, e)
                full = turned_full if w == FEW else gu_full

                def combining(js):
                    dve.wait_ge(sg_full.sem, sg_full.at(1, e))
                    ins = v.tensor_copy(sgT[:, 0:js, :], psum[0][:, 0:T * js].rearrange("p (a b) -> p a b", a=js))
                    if w == T:
                        for i in range(2):
                            ins = v.tensor_copy(xgT[:, 1, 4 * i:4 * i + 4, :], psum[2 + i].rearrange("p (a b) -> p a b", a=4))
                    ins.then_inc(sg_drained.sem, 1)

                if w > FEW:
                    combining(w // P)

                def part(buf, s):
                    return buf[:, 512 * (s % 2):512 * (s % 2) + 2 * w].rearrange("p (a b) -> p a b", a=2)

                def finish(s):
                    dve.wait_ge(sig_ready.sem, sig_ready.at(s + 1, e))
                    c.step(v.tensor_tensor(part(act_s, s), part(act_s, s), part(act_g, s), ALU.mult))
                    v.tensor_tensor(hid[:, 2 * w * s:2 * w * (s + 1)].rearrange("p (a b) -> p a b", a=2), part(act_s, s),
                                    part(act_u, s), ALU.mult).then_inc(hid_ready.sem, 1)

                for s in range(4):
                    dve.wait_ge(full.sem, full.at(s + 1, e))
                    for g, buf in ((0, act_g), (1, act_u)):
                        for i in range(2):
                            ins = v.tensor_scalar(part(buf, s)[:, i, :], gu_out(w, s, i)[:, g, :],
                                                  v1("b_gu")[:, bass.ds(16 * e + (8 * g + 2 * s + i), 1)], LIMIT,
                                                  ALU.add, ALU.min)
                            if i:
                                ins.then_inc((gu_drained if g else pre_ready).sem, 1)
                    if s:
                        finish(s - 1)
                    dve.wait_ge(gu_drained.sem, gu_drained.at(s + 1, e))
                    c.step(v.tensor_scalar(part(act_u, s), part(act_u, s), -LIMIT, 1.0, ALU.max, ALU.add))
                finish(3)
                if w == FEW:
                    combining(2)
                assert c.n == LCH["expert"], ("expert", c.n)

            with dve.Fori(0, NE) as e:
                n = dve.value_load(counts_i[0:1, bass.ds(e, 1)], min_val=0, max_val=T)
                with dve.If(n > P):
                    expert(e, T)
                with dve.Else():
                    with dve.If(n > FEW):
                        expert(e, P)
                    with dve.Else():
                        expert(e, FEW)
                dve.wait_ge(sg_full.sem, sg_full.at(1, e))
                select(e + 1).then_inc(pick_ready.sem, 1)

            dve.wait_ge(combined.sem, combined.at(1, NE - 1))
            for k in range(DT):
                v.scalar_tensor_tensor(out=xT[:, k, :], in0=psum[4 + k // 2][:, T * (k % 2):T * (k % 2) + T],
                                       scalar=modT[:, 40 + k:41 + k], in1=xT[:, k, :], op0=ALU.mult, op1=ALU.add) \
                    .then_inc(x2_ready.sem, 1)
            dve.wait_ge(fin_full.sem, 1)
            c = Chain(dve, fin_chain)
            c.step(v.tensor_scalar(rstd[:, 0, :], psum[0][:, 0:T], 1.0 / D, EPS, ALU.mult, ALU.add))
            v.reciprocal(rstd[:, 0, :], rstd[:, 0, :]).then_inc(var_ready.sem, 1)
            dve.wait_ge(std_ready.sem, 3)
            for k in range(DT):
                v.scalar_tensor_tensor(out=xT[:, k, :], in0=xT[:, k, :], scalar=v1("g_final", k), in1=rstd[:, 0, :],
                                       op0=ALU.mult, op1=ALU.mult).then_inc(xin_ready.sem, 1)
            dve.wait_ge(xin_ready.sem, 8)

            with dve.Fori(0, NL) as l:
                c = Chain(dve, l_dchain, l)

                def full(name):
                    dve.wait_ge(lay_full.sem, lay_full.at(LF.full(name), l))
                    return psum[LF.bank(name)]

                def taken(ins):
                    ins.then_inc(lay_drained["dve"].sem, 1)

                def own(name):
                    dve.wait_ge(lay_drained["dve"].sem, lay_drained["dve"].at(LF.drain[LF.index[name]][1], l))

                def out_act(name):
                    dve.wait_ge(lay_drained["act"].sem, lay_drained["act"].at(LF.drain[LF.index[name]][1], l))

                def ready(sig, n=1):
                    dve.wait_ge(S[sig].sem, S[sig].at(n, l))

                def two(b):
                    return b.rearrange("p (a b) -> p a b", a=2)

                def mean(dst, src, n):
                    return v.tensor_scalar(dst, src, 1.0 / n, EPS, ALU.mult, ALU.add)

                def scaled(dst, g, r, **kw):
                    return v.scalar_tensor_tensor(out=dst, in0=dst, scalar=g, in1=r, op0=ALU.mult, op1=ALU.mult)

                v.tensor_copy(vec2[:, :], vec2_all[:, bass.ds(l, 1), :].rearrange("p a b -> p (a b)")) \
                    .then_inc(S["vecs"].sem, 1)
                ready("vecs")
                taken(mean(L["rs"][:, 0, :], full("ss1")[:, 0:T], D))
                own("ss1")
                v.reciprocal(L["rs"][:, 0, :], L["rs"][:, 0, :]).then_inc(S["var1"].sem, 1)
                ready("std1")
                for k in range(DT):
                    ins = v.scalar_tensor_tensor(out=L["h"][:, k, :], in0=xT[:, k, :], scalar=v2("attn_norm", k),
                                                 in1=L["rs"][:, 0, :], op0=ALU.mult, op1=ALU.mult)
                ins.then_inc(S["h1"].sem, 1)
                out_act("ckv")
                c.mark(v.tensor_tensor(L["sq"][:, 0:2, :], L["cq"], L["cq"], ALU.mult))
                v.tensor_tensor(L["sq"][:, 2, :], L["ckv"], L["ckv"], ALU.mult).then_inc(S["lsq"].sem, 1)
                out_act("gk")
                c.mark(v.tensor_tensor(L["sq"][:, 3:7, :], L["gq"], L["gq"], ALU.mult))
                gkk = L["gk"].rearrange("p a b -> p (a b)")
                v.tensor_tensor(L["p"][:, 0, :], gkk, gkk, ALU.mult).then_inc(S["gsq"].sem, 1)
                b = two(full("sslat"))
                c.mark(mean(L["rs"][:, 0, :], b[:, 0, :], 256))
                taken(mean(L["rs"][:, 1, :], b[:, 1, :], 128))
                own("sslat")
                v.reciprocal(L["rs"][:, 0:2, :], L["rs"][:, 0:2, :]).then_inc(S["lvar"].sem, 1)
                for i, name in enumerate(("ssg0", "ssg1", "ssgk")):
                    taken(mean(L["rs"][:, 2 + 2 * i:4 + 2 * i, :], two(full(name)), HD))
                own("ssgk")
                v.reciprocal(L["rs"][:, 2:8, :], L["rs"][:, 2:8, :]).then_inc(S["gvar"].sem, 1)
                ready("lstd")
                for k in range(2):
                    c.mark(scaled(L["cq"][:, k, :], v2("q_norm", k), L["rs"][:, 0, :]))
                scaled(L["ckv"], v2("kv_norm", 0), L["rs"][:, 1, :]).then_inc(S["lat"].sem, 1)
                ready("gstd")
                c.mark(scaled(L["gq"], v2("gq_head", 0), L["rs"][:, 2:6, :]))
                scaled(L["gk"], v2("gk_head", 0), L["rs"][:, 6:8, :]).then_inc(S["gn"].sem, 1)
                cos, sin = const("cos_g"), const("sin_g")
                for i, name in enumerate(("swg0", "swg1", "swgk")):
                    taken(v.tensor_tensor(L["rs"][:, 2 * i:2 * i + 2, :], two(full(name)),
                                          sin.unsqueeze(1).to_broadcast([P, 2, T]), ALU.mult))
                c.mark(v.tensor_tensor(L["gq"], L["gq"], cos.unsqueeze(1).to_broadcast([P, 4, T]), ALU.mult))
                c.step(v.tensor_tensor(L["gk"], L["gk"], cos.unsqueeze(1).to_broadcast([P, 2, T]), ALU.mult))
                own("swgk")
                c.mark(v.tensor_tensor(L["gq"], L["gq"], L["rs"][:, 0:4, :], ALU.add))
                v.tensor_tensor(L["gk"], L["gk"], L["rs"][:, 4:6, :], ALU.add).then_inc(S["rope_g"].sem, 1)
                for i in range(2):
                    b = full(f"pl{i}")
                    for a in range(2):
                        k = 2 * i + a
                        ins = v.tensor_scalar(L["o"][:, 2, k, :], b[:, T * a:T * (a + 1)], v2("pool_scale", k), None,
                                              ALU.mult)
                        if a:
                            taken(ins)
                        else:
                            c.mark(ins)
                own("pl1")
                ready("rope_g")
                for q, var, std, norm, buf, gain in (("q", "qvar", "qstd", "qn", "mq", "q_head"),
                                                     ("k", "kvar", "kstd", "kn", "mk", "k_head")):
                    for i in range(4):
                        taken(mean(L["rs"][0:MQ, 2 * i:2 * i + 2, :], two(full(f"ss{q}{i}"))[0:MQ], MQ))
                    own(f"ss{q}3")
                    v.reciprocal(L["rs"][0:MQ], L["rs"][0:MQ]).then_inc(S[var].sem, 1)
                    ready(std)
                    scaled(L[buf][0:MQ], v2(gain, 0)[0:MQ], L["rs"][0:MQ]).then_inc(S[norm].sem, 1)
                    ready(norm)
                cos, sin = const("cos_m")[0:MQ], const("sin_m")[0:MQ]
                for q, buf, tmp in (("q", "mq", "sq"), ("k", "mk", "rs")):
                    for i in range(4):
                        taken(v.tensor_tensor(L[tmp][0:MQ, 2 * i:2 * i + 2, :], two(full(f"sw{q}{i}"))[0:MQ],
                                              sin.unsqueeze(1).to_broadcast([MQ, 2, T]), ALU.mult))
                    c.step(v.tensor_tensor(L[buf][0:MQ], L[buf][0:MQ], cos.unsqueeze(1).to_broadcast([MQ, NH, T]),
                                           ALU.mult))
                    own(f"sw{q}3")
                    ins = v.tensor_tensor(L[buf][0:MQ], L[buf][0:MQ], L[tmp][0:MQ], ALU.add)
                    if q == "q":
                        c.mark(ins)
                    else:
                        ins.then_inc(S["rope_m"].sem, 1)
                for i in range(2 * NH + 1):
                    if i < 2 * NH:
                        b = full(f"s_{att[i]}")
                        scale = (MQ if att[i][0] == "m" else HD) ** -0.5
                        st = L["stat"][:, i % 3, :]
                        c.step(v.tensor_reduce(st[:, 0:2], two(b), AX.X, ALU.max))
                        v.tensor_scalar(st[:, 2:4], st[:, 0:2], -scale, None, ALU.mult).then_inc(S["nmax"].sem, 1)
                    if i >= 1:
                        out_act(f"s_{att[i - 1]}")
                        st = L["stat"][:, (i - 1) % 3, :]
                        c.step(v.reciprocal(st[:, 6:8], st[:, 4:6]))
                        pr = two(L["p"][:, (i - 1) % 3, :])
                        v.tensor_tensor(pr, pr, st[:, 6:8].unsqueeze(2).to_broadcast([P, 2, T]), ALU.mult) \
                            .then_inc(S["pnorm"].sem, 1)
                out_act("ga11")
                for i in range(4):
                    o = 4 * (i % 2)
                    acc, tmp = L["sq"][:, o:o + 2, :], L["sq"][:, o + 2:o + 4, :]
                    for br in range(3):
                        taken(v.scalar_tensor_tensor(out=tmp if br else acc, in0=L["gates"][:, 8 * br + 2 * i:8 * br + 2 * i + 2, :],
                                                     scalar=1.0, in1=two(full(f"br{i}{br}")), op0=ALU.add, op1=ALU.mult))
                        own(f"br{i}{br}")
                        if br == 1:
                            c.step(v.tensor_tensor(acc, acc, tmp, ALU.add))
                        if br == 2:
                            v.tensor_tensor(merged2[:, 2 * i:2 * i + 2, :], acc, tmp, ALU.add).then_inc(S["merged"].sem, 1)
                for i in range(4):
                    taken(v.scalar_tensor_tensor(out=xT[:, 2 * i:2 * i + 2, :], in0=two(full(f"wo{i}")), scalar=0.5,
                                                 in1=xT[:, 2 * i:2 * i + 2, :], op0=ALU.mult, op1=ALU.add))
                own("wo3")
                def rest(n):
                    _, src, hi, lo, _ = unit(n)
                    ready("whi", n + 1)
                    v.tensor_tensor(lo, src, hi.bitcast(F32), ALU.subtract).then_inc(S["wlo"].sem, 1)

                rest(0)
                taken(mean(L["rs"][:, 0, :], full("ss2")[:, 0:T], D))
                own("ss2")
                v.reciprocal(L["rs"][:, 0, :], L["rs"][:, 0, :]).then_inc(S["var2"].sem, 1)
                ready("std2")
                for k in range(DT):
                    ins = v.scalar_tensor_tensor(out=h_full[:, k, :], in0=xT[:, k, :], scalar=v2("ffn_norm", k),
                                                 in1=L["rs"][:, 0, :], op0=ALU.mult, op1=ALU.mult)
                    if k % 4 == 3:
                        ins.then_inc(S["hfull"].sem, 1)

                for i in range(2):
                    ready("hhi", i + 1)
                    v.tensor_tensor(h_lo[:, 4 * i:4 * i + 4, :], h_full[:, 4 * i:4 * i + 4, :],
                                    h_hi[:, 4 * i:4 * i + 4, :].bitcast(F32), ALU.subtract).then_inc(S["h2"].sem, 1)
                rest(1)
                for ft in range(FT + 2):
                    if ft < FT:
                        rest(ft + 2)
                        b = two(full(f"up{ft}"))
                        ready("vals", ft + 1)
                        for tap in (0, 2):
                            for g in range(2):
                                dst = conv_t[:, 2 * (ft % 4) + g, :]
                                to, src = (slice(1, T), slice(0, T - 1)) if tap == 0 else (slice(0, T - 1), slice(1, T))
                                ins = v.scalar_tensor_tensor(out=dst[:, to], in0=b[:, g, src],
                                                             scalar=v2("conv_w", 2 * FT * tap + g * FT + ft),
                                                             in1=dst[:, to], op0=ALU.mult, op1=ALU.add)
                                if tap == 2 and g == 1:
                                    taken(ins)
                                else:
                                    c.mark(ins)
                            if tap == 0:
                                c.settle()
                    if 1 <= ft <= FT:
                        ready("silu", ft)
                        if ft > 4:
                            ready("flo", ft - 4)
                        v.tensor_tensor(ff_t[:, (ft - 1) % 4, :], silu_t[:, (ft - 1) % 4, :],
                                        conv_t[:, 2 * ((ft - 1) % 4) + 1, :], ALU.mult).then_inc(S["ffact"].sem, 1)
                    if ft < FT:
                        own(f"up{ft}")
                        v.tensor_copy(L["stat"][:, 0, 0:1], L["stat"][:, 0, 1:2]).then_inc(S["conv"].sem, 1)
                    if ft >= 2:
                        ready("fhi", ft - 1)
                        v.tensor_tensor(f_lo[:, ft - 2, :], ff_t[:, (ft - 2) % 4, :], f_hi[:, ft - 2, :].bitcast(F32),
                                        ALU.subtract).then_inc(S["flo"].sem, 1)

                def added(i):
                    taken(v.tensor_tensor(xT[:, 2 * i:2 * i + 2, :], two(full(f"dn{i}")), xT[:, 2 * i:2 * i + 2, :],
                                          ALU.add))

                for n in range(2, 12):
                    rest(FT + n)
                    if n > 2 and n % 3 == 2:
                        added(n // 3 - 1)
                added(3)
                own("dn3")
                v.tensor_copy(L["stat"][:, 0, 0:1], L["stat"][:, 0, 1:2]).then_inc(S["x4"].sem, 1)
                ready("x4")
                assert c.n == LCH["dve"], ("dve", c.n)

        @block.gpsimd
        def _(pool):
            g = nc.gpsimd
            g.memset(xr[:, :, 0:3], 0.0).then_inc(zeroed.sem, 1)
            with pool.Fori(0, NL) as l:
                c = Chain(pool, l_pchain, l)

                def out_act(name):
                    pool.wait_ge(lay_drained["act"].sem, lay_drained["act"].at(LF.drain[LF.index[name]][1], l))

                pool.wait_ge(S["vecs"].sem, S["vecs"].at(1, l))
                ones = const("ones", PAD).unsqueeze(1).to_broadcast([P, 4, PAD])
                for pad in (L["pool"][:, :, 0:PAD], L["pool"][:, :, PAD + T:]):
                    c.mark(g.tensor_tensor(pad, ones, ones, ALU.subtract))
                out_act("po1")
                c.settle()
                n = T + 2 * PAD
                for i, w in enumerate(POOLS):
                    x, src = L["pool"][:, i, :], L["pool"][:, i, :]
                    bufs = [L["sumA"], L["sumB"]]
                    step = 1
                    while step < w:
                        dst = bufs.pop(0)
                        bufs.append(dst)
                        m = n - 2 * step + 1
                        c.step(g.tensor_tensor(dst[:, 0:m], src[:, 0:m], src[:, step:step + m], ALU.add))
                        src, step = dst, 2 * step
                    dst = bufs[0]
                    o = PAD - w // 2
                    c.step(g.tensor_tensor(dst[:, 0:T], src[:, o:o + T], const("mean")[:, T * i:T * (i + 1)], ALU.mult))
                    ins = g.tensor_tensor(x[:, PAD:PAD + T], dst[:, 0:T], x[:, PAD:PAD + T], ALU.subtract)
                    if i == 3:
                        ins.then_inc(S["mixed"].sem, 1)
                    else:
                        c.step(ins)
                assert c.n == LCH["pool"], ("pool", c.n)



def tiled(a):
    a = np.asarray(a)
    return np.moveaxis(a.reshape(-1, P), 1, 0)


def kernel(**inputs):
    import concourse.bacc as bacc
    from concourse.bass_utils import run_bass_kernel_spmd

    x = {k: np.asarray(v) for k, v in inputs.items()}
    table, const_at = constants()
    one = {
        "b_ada": tiled(x["b_ada"][0]), "c": tiled(x["c"][0]), "g_mix": tiled(x["g_mix"][0]),
        "conv_w": x["conv_w"][0].reshape(4, 4, P).transpose(2, 1, 0).reshape(P, 16),
        "conv_b": tiled(x["conv_b"][0]), "b_rg_a": tiled(x["b_rg_a"][0].reshape(-1)),
        "b_rg_x": tiled(x["b_rg_x"][0].reshape(-1)), "lam": tiled(x["lru_lambda"][0]),
        "g_attn": tiled(x["g_attn_out"][0]), "g_lru": tiled(x["g_lru_out"][0]), "g_ffn": tiled(x["g_ffn"][0]),
        "g_final": tiled(x["g_final"]), "sinks": np.broadcast_to(x["sinks"][0], (P, NH)),
        "b_router": np.broadcast_to(x["b_router"][0], (P, NE)), "b_gu": tiled(x["b_gu"][0]),
    }

    def rows(v, reps):
        v = np.concatenate([v] * reps)[:P]
        return np.concatenate([v, v[:P - len(v)]])[:, None]

    layers = []
    for l in range(NL):
        y = {k: v[l] for k, v in x.items() if k.endswith("_2")}
        two = {
            "attn_norm": tiled(y["attn_norm_g_2"]), "q_norm": tiled(y["mla_q_norm_g_2"]),
            "kv_norm": tiled(y["mla_kv_norm_g_2"]), "q_head": rows(y["mla_q_head_g_2"], 1),
            "k_head": rows(y["mla_k_head_g_2"], 1), "gq_head": rows(y["gqa_q_head_g_2"], 2),
            "gk_head": rows(y["gqa_k_head_g_2"], 2), "pool_scale": tiled(y["pool_scale_2"]),
            "ffn_norm": tiled(y["ffn_norm_g_2"]), "conv_w": tiled(y["ffn_conv_w_2"].reshape(-1)),
            "conv_b": tiled(y["ffn_conv_b_2"]),
        }
        layers.append(np.concatenate([two[k] for k in VEC2], 1))
    sent = {
        "xT": np.ascontiguousarray(x["x"][0].T),
        "vec1": np.ascontiguousarray(np.concatenate([one[k] for k in VEC1], 1)),
        "vec2": np.ascontiguousarray(np.stack(layers, 1)),
        "consts": table,
    }
    for name in ("w_ada", "w_in", "w_rg_a", "w_rg_x", "w_out", "w_router", "w_gu", "w_down", "b_down"):
        sent[name] = x[name][0]
    for name in ("w_in_2", "mla_w_uq_2", "mla_w_ukv_2", "pool_w_2", "w_branch_mla_2", "w_branch_gqa_2",
                 "w_branch_pool_2", "w_out_2", "ffn_w_up_2", "ffn_w_down_2"):
        sent[name] = x[name]

    nc = bacc.Bacc("TRN2", target_bir_lowering=False, num_devices=1)
    arrays, dram = {}, {"const_at": const_at}
    for name, a in sent.items():
        arrays[f"in_{name}"] = np.ascontiguousarray(a)
        dram[name] = nc.dram_tensor(f"in_{name}", a.shape, F32, kind="ExternalInput").ap()
    out = nc.dram_tensor("out_xT", (D, T), F32, kind="ExternalOutput").ap()
    build(nc, dram, out)
    r = run_bass_kernel_spmd(nc, [arrays], core_ids=[0])
    return np.ascontiguousarray(r.results[0]["out_xT"].T)[None]
```
